# Optimizing a Trainium2 kernel written in Bass

```python
import math
import jax, jax.numpy as jnp
from jax import lax
import numpy as np

D_MODEL = 1024
BATCH = 1
SEQ = 256
DEPTH = 2

RET_HEADS = 4
RET_DK = 256
RET_DV = 512
RET_CHUNK = 128
ROPE_BASE = 10000.0
GN_EPS = 1e-5
NSA_HEADS = 16
NSA_KV_GROUPS = 2
NSA_HD = 64
CMP_LEN = 32
CMP_STRIDE = 16
CMP_HIDDEN = 256
SEL_BLOCK = 64
SEL_TOPK = 8
WINDOW = 512
NSA_Q_BLOCK = 64
FORCED_SCORE = 1e4
REL_BUCKETS = 32
REL_MAX_DIST = 128
FFN_HIDDEN = -(-8 * D_MODEL // (3 * 256)) * 256
EPS = 1e-6
NEG_INF = -1e30
SPLIT_SIZES = (RET_HEADS * RET_DK, RET_HEADS * RET_DK, RET_HEADS * RET_DV, RET_HEADS * RET_DV,
               NSA_HEADS * NSA_HD, 6 * NSA_KV_GROUPS * NSA_HD, 3 * NSA_HEADS, D_MODEL, D_MODEL)
C_IN = sum(SPLIT_SIZES)


def rms_norm(x, g):
    xf = x.astype(jnp.float32)
    y = xf * lax.rsqrt(jnp.mean(xf * xf, -1, keepdims=True) + EPS)
    return (y * g.astype(jnp.float32)).astype(x.dtype)

def masked_softmax(logits, mask):
    z = jnp.where(mask, logits.astype(jnp.float32), NEG_INF)
    z = z - jnp.max(z, -1, keepdims=True)
    e = jnp.exp(z) * mask
    return e / jnp.maximum(jnp.sum(e, -1, keepdims=True), 1e-30)

def t5_bucket(dist):
    dist = jnp.maximum(dist, 0)
    max_exact = REL_BUCKETS // 2
    large = max_exact + (jnp.log(jnp.maximum(dist, 1).astype(jnp.float32) / max_exact)
                         / math.log(REL_MAX_DIST / max_exact) * (REL_BUCKETS - max_exact)).astype(jnp.int32)
    large = jnp.minimum(large, REL_BUCKETS - 1)
    return jnp.where(dist < max_exact, dist, large)

def rotary(x, pos):
    half = x.shape[-1] // 2
    freqs = ROPE_BASE ** (-jnp.arange(half, dtype=jnp.float32) / half)
    ang = pos.astype(jnp.float32)[:, None] * freqs
    cos = jnp.cos(ang)[None, :, None, :]
    sin = jnp.sin(ang)[None, :, None, :]
    x1, x2 = x[..., :half], x[..., half:]
    return jnp.concatenate([x1 * cos - x2 * sin, x1 * sin + x2 * cos], -1)

def retention(q, k, v):
    B, T, H, dk = q.shape
    dv = v.shape[-1]
    nc = T // RET_CHUNK
    lg = jnp.log(1.0 - 2.0 ** (-5.0 - jnp.arange(H, dtype=jnp.float32)))
    n = jnp.arange(RET_CHUNK, dtype=jnp.float32)
    diff = n[:, None] - n[None, :]
    dmask = jnp.where(diff >= 0, jnp.exp(jnp.maximum(diff, 0.0)[None] * lg[:, None, None]), 0.0)
    xi = jnp.exp((n + 1.0)[None] * lg[:, None])
    zeta = jnp.exp((RET_CHUNK - 1.0 - n)[None] * lg[:, None])
    g_chunk = jnp.exp(RET_CHUNK * lg)

    def to_chunks(t):
        return t.reshape(B, nc, RET_CHUNK, H, t.shape[-1]).transpose(1, 0, 3, 2, 4)

    def step(R, qkv):
        qc, kc, vc = qkv
        s = jnp.einsum('bhnd,bhmd->bhnm', qc, kc) * dmask
        o = (jnp.einsum('bhnm,bhme->bhne', s, vc)
             + jnp.einsum('bhnd,bhde->bhne', qc, R) * xi[:, :, None])
        R = g_chunk[:, None, None] * R + jnp.einsum('bhmd,bhme->bhde', kc * zeta[:, :, None], vc)
        return R, o

    R0 = jnp.zeros((B, H, dk, dv), jnp.float32)
    _, o = lax.scan(step, R0, (to_chunks(q), to_chunks(k), to_chunks(v)))
    return o.transpose(1, 0, 3, 2, 4).reshape(B, T, H, dv)

def compress(kv, pos_emb, w1, w2):
    T = kv.shape[2]
    n_cmp = (T - CMP_LEN) // CMP_STRIDE + 1
    idx = jnp.arange(n_cmp)[:, None] * CMP_STRIDE + jnp.arange(CMP_LEN)[None]
    blocks = kv[:, :, idx, :] + pos_emb
    flat = blocks.reshape(blocks.shape[0], blocks.shape[1], n_cmp, CMP_LEN * NSA_HD)
    return jax.nn.gelu(flat @ w1) @ w2

def nsa(q, k_c, v_c, k_s, v_s, k_w, v_w, gates, pos_k, pos_v, w1_k, w2_k, w1_v, w2_v, rel_bias):
    B, T, H, hd = q.shape
    G = NSA_KV_GROUPS
    HG = H // G
    QB = NSA_Q_BLOCK
    scale = hd ** -0.5
    grp = lambda t: t.transpose(0, 2, 1, 3)
    kc = compress(grp(k_c), pos_k, w1_k, w2_k)
    vc = compress(grp(v_c), pos_v, w1_v, w2_v)
    n_cmp = kc.shape[2]
    cmp_end = jnp.arange(n_cmp) * CMP_STRIDE + CMP_LEN - 1
    n_sel = T // SEL_BLOCK
    sel_k = min(SEL_TOPK, n_sel)
    sel_start = jnp.arange(n_sel) * SEL_BLOCK
    overlap = ((cmp_end[:, None] - CMP_LEN + 1 < sel_start[None] + SEL_BLOCK)
               & (cmp_end[:, None] >= sel_start[None])).astype(jnp.float32)
    ks_blocks = grp(k_s).reshape(B, G, n_sel, SEL_BLOCK, hd)
    vs_blocks = grp(v_s).reshape(B, G, n_sel, SEL_BLOCK, hd)
    kw_pad = jnp.pad(grp(k_w), ((0, 0), (0, 0), (WINDOW, 0), (0, 0)))
    vw_pad = jnp.pad(grp(v_w), ((0, 0), (0, 0), (WINDOW, 0), (0, 0)))
    table = rel_bias.reshape(REL_BUCKETS, G, HG).astype(jnp.float32)
    nq = T // QB
    qb = q.reshape(B, nq, QB, G, HG, hd).transpose(1, 0, 3, 4, 2, 5)
    gb = gates.reshape(B, nq, QB, G, HG, 3).transpose(1, 0, 3, 4, 2, 5)
    starts = jnp.arange(nq, dtype=jnp.int32) * QB
    bidx = jnp.arange(B)[:, None, None, None]
    gidx = jnp.arange(G)[None, :, None, None]
    jj = jnp.arange(n_sel)

    def head_bias(dist):
        return jnp.moveaxis(table[t5_bucket(dist)], (-2, -1), (0, 1))

    def sel_bias(dist):
        b = jax.vmap(lambda tb, bk: tb[bk], in_axes=(1, 1), out_axes=1)(table, t5_bucket(dist))
        return jnp.moveaxis(b, -1, 2)

    def block(args):
        qx, gx, s = args
        pos = s + jnp.arange(QB, dtype=jnp.int32)
        dc = pos[:, None] - cmp_end[None]
        lc = jnp.einsum('bghqd,bgnd->bghqn', qx, kc) * scale + head_bias(dc)
        pc = masked_softmax(lc, dc >= 0)
        oc = jnp.einsum('bghqn,bgnd->bghqd', pc.astype(vc.dtype), vc)
        imp = jnp.einsum('bghqn,nj->bgqj', pc, overlap)
        cur = pos // SEL_BLOCK
        forced = (jj[None] == 0) | (jj[None] == cur[:, None]) | (jj[None] == cur[:, None] - 1)
        imp = jnp.where(forced, FORCED_SCORE, imp)
        imp = jnp.where(sel_start[None] <= pos[:, None], imp, NEG_INF)
        _, sel = lax.top_k(imp, sel_k)
        ksel = ks_blocks[bidx, gidx, sel]
        vsel = vs_blocks[bidx, gidx, sel]
        kpos = sel[..., None] * SEL_BLOCK + jnp.arange(SEL_BLOCK)
        ds = pos[:, None, None] - kpos
        ls = jnp.einsum('bghqd,bgqkld->bghqkl', qx, ksel) * scale + sel_bias(ds)
        bsz, g_, hg_, qn, kk, bs = ls.shape
        ps = masked_softmax(ls.reshape(bsz, g_, hg_, qn, kk * bs),
                            (ds >= 0)[:, :, None].reshape(bsz, g_, 1, qn, kk * bs))
        os_ = jnp.einsum('bghqm,bgqmd->bghqd', ps.astype(vsel.dtype),
                         vsel.reshape(bsz, g_, qn, kk * bs, hd))
        kw = lax.dynamic_slice_in_dim(kw_pad, s, WINDOW + QB, axis=2)
        vw = lax.dynamic_slice_in_dim(vw_pad, s, WINDOW + QB, axis=2)
        wpos = s - WINDOW + jnp.arange(WINDOW + QB, dtype=jnp.int32)
        dw = pos[:, None] - wpos[None]
        lw = jnp.einsum('bghqd,bgld->bghql', qx, kw) * scale + head_bias(dw)
        pw = masked_softmax(lw, (dw >= 0) & (dw < WINDOW) & (wpos[None] >= 0))
        ow = jnp.einsum('bghql,bgld->bghqd', pw.astype(vw.dtype), vw)
        return gx[..., 0:1] * oc + gx[..., 1:2] * os_ + gx[..., 2:3] * ow

    out = lax.map(block, (qb, gb, starts))
    return out.transpose(1, 0, 4, 2, 3, 5).reshape(B, T, H * hd)

def first_inputs(seed: int = 0) -> dict:
    key = jax.random.key(seed)
    ks = jax.random.split(key, 20)
    nrm = lambda k, shape, fan: jax.random.normal(k, shape, jnp.float32) * (fan ** -0.5)
    gain = lambda k, shape: 1.0 + 0.01 * jax.random.normal(k, shape, jnp.float32)
    L = DEPTH
    return {
        "x": jax.random.normal(ks[0], (BATCH, SEQ, D_MODEL), jnp.float32),
        "norm_mix_g": gain(ks[1], (L, D_MODEL)),
        "w_in": nrm(ks[2], (L, D_MODEL, C_IN), D_MODEL),
        "cmp_pos_k": 0.02 * jax.random.normal(ks[3], (L, CMP_LEN, NSA_HD), jnp.float32),
        "cmp_pos_v": 0.02 * jax.random.normal(ks[4], (L, CMP_LEN, NSA_HD), jnp.float32),
        "cmp_w1_k": nrm(ks[5], (L, CMP_LEN * NSA_HD, CMP_HIDDEN), CMP_LEN * NSA_HD),
        "cmp_w2_k": nrm(ks[6], (L, CMP_HIDDEN, NSA_HD), CMP_HIDDEN),
        "cmp_w1_v": nrm(ks[7], (L, CMP_LEN * NSA_HD, CMP_HIDDEN), CMP_LEN * NSA_HD),
        "cmp_w2_v": nrm(ks[8], (L, CMP_HIDDEN, NSA_HD), CMP_HIDDEN),
        "w_o_ret": nrm(ks[9], (L, RET_HEADS * RET_DV, D_MODEL), RET_HEADS * RET_DV),
        "w_o_nsa": nrm(ks[10], (L, NSA_HEADS * NSA_HD, D_MODEL), NSA_HEADS * NSA_HD),
        "w_out": nrm(ks[11], (L, D_MODEL, D_MODEL), D_MODEL),
        "norm_ffn_g": gain(ks[12], (L, D_MODEL)),
        "w_ffn_in": nrm(ks[13], (L, D_MODEL, 2 * FFN_HIDDEN), D_MODEL),
        "w_ffn_out": nrm(ks[14], (L, FFN_HIDDEN, D_MODEL), FFN_HIDDEN),
        "rel_bias": 0.2 * jax.random.normal(ks[15], (REL_BUCKETS, NSA_HEADS), jnp.float32),
        "norm_final_g": gain(ks[16], (D_MODEL,)),
    }

def first_block(x, norm_mix_g, w_in, cmp_pos_k, cmp_pos_v, cmp_w1_k, cmp_w2_k, cmp_w1_v, cmp_w2_v,
              w_o_ret, w_o_nsa, w_out, norm_ffn_g, w_ffn_in, w_ffn_out, rel_bias, norm_final_g):
    B, T, _ = x.shape
    pos = jnp.arange(T, dtype=jnp.int32)
    cuts = [int(c) for c in np.cumsum(SPLIT_SIZES)[:-1]]
    for i in range(DEPTH):
        h = rms_norm(x, norm_mix_g[i])
        proj = h @ w_in[i]
        q_r, k_r, v_r, g_r, q_n, kv_n, gate_n, m_a, m_b = jnp.split(proj, cuts, axis=-1)
        qr = rotary(q_r.reshape(B, T, RET_HEADS, RET_DK).astype(jnp.float32), pos)
        kr = rotary(k_r.reshape(B, T, RET_HEADS, RET_DK).astype(jnp.float32), pos) * (RET_DK ** -0.5)
        vr = v_r.reshape(B, T, RET_HEADS, RET_DV).astype(jnp.float32)
        o_r = retention(qr, kr, vr)
        mu = jnp.mean(o_r, -1, keepdims=True)
        var = jnp.mean(jnp.square(o_r - mu), -1, keepdims=True)
        o_r = ((o_r - mu) * lax.rsqrt(var + GN_EPS)).reshape(B, T, RET_HEADS * RET_DV).astype(x.dtype)
        y_ret = (jax.nn.silu(g_r) * o_r) @ w_o_ret[i]
        kv = kv_n.reshape(B, T, 6, NSA_KV_GROUPS, NSA_HD)
        o_n = nsa(q_n.reshape(B, T, NSA_HEADS, NSA_HD),
                  kv[:, :, 0], kv[:, :, 1], kv[:, :, 2], kv[:, :, 3], kv[:, :, 4], kv[:, :, 5],
                  jax.nn.sigmoid(gate_n).reshape(B, T, NSA_HEADS, 3),
                  cmp_pos_k[i], cmp_pos_v[i], cmp_w1_k[i], cmp_w2_k[i], cmp_w1_v[i], cmp_w2_v[i],
                  rel_bias)
        y_nsa = o_n.astype(x.dtype) @ w_o_nsa[i]
        mixed = (jax.nn.sigmoid(m_a) * y_ret + jax.nn.sigmoid(m_b) * y_nsa) @ w_out[i]
        x = x + mixed.astype(x.dtype)
        h = rms_norm(x, norm_ffn_g[i])
        a, b = jnp.split(h @ w_ffn_in[i], 2, axis=-1)
        x = x + ((jax.nn.silu(a) * b) @ w_ffn_out[i]).astype(x.dtype)
    return rms_norm(x, norm_final_g)


CHUNK = 64
Q_BLOCK = 128
HEAD_DIM = 64
A_HEADS = 4
B_HEADS = 8
C_HEADS = 8
IDX_HEADS = 4
IDX_DIM = 64
TOPK_MAX = 256
N_BRANCHES = 3
D_FF = 4 * D_MODEL
PLE_DIM = 256
ROPE_THETA = 10000.0

A_QK = A_HEADS * 2 * HEAD_DIM
A_V = A_HEADS * 2 * HEAD_DIM
A_WIDTH = A_V
B_WIDTH = B_HEADS * HEAD_DIM
C_WIDTH = C_HEADS * HEAD_DIM
IN_SPLITS = (A_QK, A_QK, A_V, B_WIDTH, B_WIDTH, B_WIDTH, C_WIDTH, C_WIDTH, C_WIDTH,
             IDX_HEADS * IDX_DIM, IDX_DIM, IDX_HEADS, N_BRANCHES * D_MODEL)
W_IN_COLS = (2 * A_QK + A_V + 3 * B_WIDTH + 3 * C_WIDTH + IDX_HEADS * IDX_DIM + IDX_DIM
             + IDX_HEADS + N_BRANCHES * D_MODEL)


def rmsnorm(x, g):
    xf = x.astype(jnp.float32)
    y = xf * lax.rsqrt(jnp.mean(xf * xf, axis=-1, keepdims=True) + EPS)
    return (y * g.astype(jnp.float32)).astype(x.dtype)

def rope_tables(positions, dim):
    inv = ROPE_THETA ** (-jnp.arange(0, dim, 2, dtype=jnp.float32) / dim)
    ang = positions.astype(jnp.float32)[..., None] * inv
    return jnp.cos(ang), jnp.sin(ang)

def apply_rope(x, cos, sin):
    c = cos[:, :, None, :]
    s = sin[:, :, None, :]
    xf = x.astype(jnp.float32)
    x1, x2 = jnp.split(xf, 2, axis=-1)
    return jnp.concatenate([x1 * c - x2 * s, x2 * c + x1 * s], axis=-1).astype(x.dtype)

def sweep_query_blocks(fn, *arrays):
    b, s = arrays[0].shape[:2]
    nb = s // Q_BLOCK
    blocks = tuple(jnp.moveaxis(a.reshape((b, nb, Q_BLOCK) + a.shape[2:]), 1, 0) for a in arrays)
    out = lax.map(lambda args: fn(args[0], *args[1:]), (jnp.arange(nb), *blocks))
    return jnp.moveaxis(out, 0, 1).reshape((b, s) + out.shape[3:])

def block_positions(blk, n_keys):
    q_pos = blk * Q_BLOCK + jnp.arange(Q_BLOCK)
    k_pos = jnp.arange(n_keys)
    chunk_ok = (k_pos[None, :] // CHUNK) <= (q_pos[:, None] // CHUNK)
    return q_pos, k_pos, chunk_ok

def diff_attention(q, k, v, lam, lam_init, subln_g):
    n_keys = k.shape[1]
    scale = HEAD_DIM ** -0.5

    def block(blk, qb):
        _, _, chunk_ok = block_positions(blk, n_keys)
        s = jnp.einsum('bqhcd,bkhcd->bhcqk', qb, k).astype(jnp.float32) * scale
        s = jnp.where(chunk_ok, s, -jnp.inf)
        pr = jax.nn.softmax(s, axis=-1)
        attn = (pr[:, :, 0] - lam * pr[:, :, 1]).astype(v.dtype)
        return jnp.einsum('bhqk,bkhe->bqhe', attn, v)

    o = sweep_query_blocks(block, q)
    return rmsnorm(o, subln_g) * (1.0 - lam_init)

def stick_breaking_attention(q, k, v):
    n_keys = k.shape[1]
    scale = HEAD_DIM ** -0.5

    def block(blk, qb):
        q_pos, k_pos, _ = block_positions(blk, n_keys)
        strict = k_pos[None, :] < q_pos[:, None]
        z = jnp.einsum('bqhd,bkhd->bhqk', qb, k).astype(jnp.float32) * scale
        log_beta = jax.nn.log_sigmoid(z)
        log_one_minus = jnp.where(strict, jax.nn.log_sigmoid(-z), 0.0)
        key_axis = log_one_minus.ndim - 1
        later = lax.cumsum(log_one_minus, axis=key_axis, reverse=True) - log_one_minus
        a = jnp.where(strict, jnp.exp(log_beta + later), 0.0).astype(v.dtype)
        return jnp.einsum('bhqk,bkhd->bqhd', a, v)

    return sweep_query_blocks(block, q)

def dsa_attention(q, k, v, qi, ki, wi):
    n_keys = k.shape[1]
    topk = min(TOPK_MAX, n_keys // 4)
    scale = HEAD_DIM ** -0.5

    def block(blk, qb, qib, wib):
        q_pos, _, chunk_ok = block_positions(blk, n_keys)
        idx_s = jnp.einsum('bqhd,bkd->bqhk', qib, ki).astype(jnp.float32) * (IDX_DIM ** -0.5)
        score = jnp.einsum('bqh,bqhk->bqk', wib.astype(jnp.float32) * (IDX_HEADS ** -0.5),
                           jax.nn.relu(idx_s))
        score = jnp.where(chunk_ok, score, -jnp.inf)
        _, sel = lax.top_k(score, topk)
        ok = (sel // CHUNK) <= (q_pos[None, :, None] // CHUNK)
        kg = jax.vmap(lambda kb, ib: kb[ib])(k, sel)
        vg = jax.vmap(lambda vb, ib: vb[ib])(v, sel)
        s = jnp.einsum('bqhd,bqkhd->bhqk', qb, kg).astype(jnp.float32) * scale
        s = jnp.where(ok[:, None], s, -jnp.inf)
        pr = jax.nn.softmax(s, axis=-1).astype(v.dtype)
        return jnp.einsum('bhqk,bqkhd->bqhd', pr, vg)

    return sweep_query_blocks(block, q, qi, wi)

def second_inputs(seed: int = 0) -> dict:
    key = jax.random.key(seed)
    ks = iter(jax.random.split(key, 32))

    def dense(shape, fan_in):
        return jax.random.normal(next(ks), shape, jnp.float32) * (fan_in ** -0.5)

    def gain(shape):
        return 1.0 + 0.05 * jax.random.normal(next(ks), shape, jnp.float32)

    x = jax.random.normal(next(ks), (BATCH, SEQ, D_MODEL), jnp.float32)
    p = jax.random.normal(next(ks), (DEPTH, BATCH, SEQ, PLE_DIM), jnp.float32)
    offset = jax.random.randint(next(ks), (BATCH, 1), 0, 16, dtype=jnp.int32) * CHUNK
    positions = (offset + jnp.arange(SEQ, dtype=jnp.int32)[None, :]).astype(jnp.int32)
    return {
        "x": x,
        "p": p,
        "positions": positions,
        "attn_norm": gain((DEPTH, D_MODEL)),
        "w_in": dense((DEPTH, D_MODEL, W_IN_COLS), D_MODEL),
        "a_q_norm": gain((DEPTH, HEAD_DIM)),
        "a_k_norm": gain((DEPTH, HEAD_DIM)),
        "a_lambda": 0.1 * jax.random.normal(next(ks), (DEPTH, 4, HEAD_DIM), jnp.float32),
        "a_subln": gain((DEPTH, 2 * HEAD_DIM)),
        "c_q_norm": gain((DEPTH, HEAD_DIM)),
        "c_k_norm": gain((DEPTH, HEAD_DIM)),
        "idx_k_norm": gain((DEPTH, IDX_DIM)),
        "w_br_a": dense((DEPTH, A_WIDTH, D_MODEL), A_WIDTH),
        "w_br_b": dense((DEPTH, B_WIDTH, D_MODEL), B_WIDTH),
        "w_br_c": dense((DEPTH, C_WIDTH, D_MODEL), C_WIDTH),
        "w_out": dense((DEPTH, D_MODEL, D_MODEL), D_MODEL),
        "mlp_norm": gain((DEPTH, D_MODEL)),
        "w_up": dense((DEPTH, D_MODEL, D_FF), D_MODEL),
        "w_down": dense((DEPTH, D_FF, D_MODEL), D_FF),
        "ple_norm": gain((DEPTH, D_MODEL)),
        "w_ple_gate": dense((DEPTH, D_MODEL, D_MODEL), D_MODEL),
        "w_ple_proj": dense((DEPTH, PLE_DIM, D_MODEL), PLE_DIM),
    }

def second_block(x, p, positions, attn_norm, w_in, a_q_norm, a_k_norm, a_lambda, a_subln,
              c_q_norm, c_k_norm, idx_k_norm, w_br_a, w_br_b, w_br_c, w_out,
              mlp_norm, w_up, w_down, ple_norm, w_ple_gate, w_ple_proj):
    b, s = x.shape[:2]
    cos, sin = rope_tables(positions, HEAD_DIM)
    offsets = [int(o) for o in np.cumsum(IN_SPLITS)[:-1]]
    for i in range(DEPTH):
        lam_init = 0.8 - 0.6 * math.exp(-0.3 * i)
        h = rmsnorm(x, attn_norm[i])
        proj = h @ w_in[i]
        (aq, ak, av, bq, bk, bv, cq, ck, cv, iq, ik, iw, gl) = jnp.split(proj, offsets, axis=-1)

        aq = apply_rope(rmsnorm(aq.reshape(b, s, 2 * A_HEADS, HEAD_DIM), a_q_norm[i]), cos, sin)
        ak = apply_rope(rmsnorm(ak.reshape(b, s, 2 * A_HEADS, HEAD_DIM), a_k_norm[i]), cos, sin)
        lp = a_lambda[i].astype(jnp.float32)
        lam = jnp.exp(jnp.sum(lp[0] * lp[1])) - jnp.exp(jnp.sum(lp[2] * lp[3])) + lam_init
        y_a = diff_attention(aq.reshape(b, s, A_HEADS, 2, HEAD_DIM),
                             ak.reshape(b, s, A_HEADS, 2, HEAD_DIM),
                             av.reshape(b, s, A_HEADS, 2 * HEAD_DIM),
                             lam, lam_init, a_subln[i]).reshape(b, s, A_WIDTH)

        y_b = stick_breaking_attention(bq.reshape(b, s, B_HEADS, HEAD_DIM),
                                       bk.reshape(b, s, B_HEADS, HEAD_DIM),
                                       bv.reshape(b, s, B_HEADS, HEAD_DIM)).reshape(b, s, B_WIDTH)

        cq = apply_rope(rmsnorm(cq.reshape(b, s, C_HEADS, HEAD_DIM), c_q_norm[i]), cos, sin)
        ck = apply_rope(rmsnorm(ck.reshape(b, s, C_HEADS, HEAD_DIM), c_k_norm[i]), cos, sin)
        iq = apply_rope(iq.reshape(b, s, IDX_HEADS, IDX_DIM), cos, sin)
        ik = apply_rope(rmsnorm(ik, idx_k_norm[i])[:, :, None, :], cos, sin)[:, :, 0]
        y_c = dsa_attention(cq, ck, cv.reshape(b, s, C_HEADS, HEAD_DIM),
                            iq, ik, iw).reshape(b, s, C_WIDTH)

        gates = jax.nn.sigmoid(gl.reshape(b, s, N_BRANCHES, D_MODEL).astype(jnp.float32)).astype(x.dtype)
        merged = (gates[:, :, 0] * (y_a @ w_br_a[i])
                  + gates[:, :, 1] * (y_b @ w_br_b[i])
                  + gates[:, :, 2] * (y_c @ w_br_c[i]))
        x = x + merged @ w_out[i]

        hm = rmsnorm(x, mlp_norm[i])
        x = x + jnp.square(jax.nn.relu(hm @ w_up[i])) @ w_down[i]

        hp = rmsnorm(x, ple_norm[i])
        x = x + jax.nn.sigmoid(hp @ w_ple_gate[i]) * (p[i] @ w_ple_proj[i])
    return x


def setup_inputs(seed=0):
    out = dict(first_inputs(seed))
    for name, value in second_inputs(seed + 1).items():
        if name != "x":
            out[name + "_2"] = value
    return out


def reference(
    x, norm_mix_g, w_in, cmp_pos_k, cmp_pos_v, cmp_w1_k, cmp_w2_k, cmp_w1_v, cmp_w2_v, w_o_ret,
    w_o_nsa, w_out, norm_ffn_g, w_ffn_in, w_ffn_out, rel_bias, norm_final_g, p_2, positions_2,
    attn_norm_2, w_in_2, a_q_norm_2, a_k_norm_2, a_lambda_2, a_subln_2, c_q_norm_2, c_k_norm_2,
    idx_k_norm_2, w_br_a_2, w_br_b_2, w_br_c_2, w_out_2, mlp_norm_2, w_up_2, w_down_2,
    ple_norm_2, w_ple_gate_2, w_ple_proj_2,
):
    x = first_block(
        x, norm_mix_g, w_in, cmp_pos_k, cmp_pos_v, cmp_w1_k, cmp_w2_k, cmp_w1_v, cmp_w2_v,
        w_o_ret, w_o_nsa, w_out, norm_ffn_g, w_ffn_in, w_ffn_out, rel_bias, norm_final_g,
    )
    return second_block(
        x, p_2, positions_2, attn_norm_2, w_in_2, a_q_norm_2, a_k_norm_2, a_lambda_2, a_subln_2,
        c_q_norm_2, c_k_norm_2, idx_k_norm_2, w_br_a_2, w_br_b_2, w_br_c_2, w_out_2, mlp_norm_2,
        w_up_2, w_down_2, ple_norm_2, w_ple_gate_2, w_ple_proj_2,
    )


_drawn_inputs = setup_inputs


def setup_inputs(seed=0):
    import zlib

    import numpy as np

    out = dict(_drawn_inputs(seed))
    spreads = {}
    factors = {'norm_mix_g': 3.096,
     'cmp_pos_k': 8.0,
     'cmp_pos_v': 4.785,
     'norm_ffn_g': 3.227,
     'norm_final_g': 3.292,
     'a_q_norm_2': 2.772,
     'a_k_norm_2': 3.012,
     'a_lambda_2': 2.74,
     'c_q_norm_2': 8.0,
     'c_k_norm_2': 8.0,
     'idx_k_norm_2': 3.05,
     'ple_norm_2': 6.29}
    for name, (base, spread) in spreads.items():
        noise = np.random.default_rng([zlib.crc32(name.encode()), seed]).standard_normal(out[name].shape)
        drawn = base * np.exp(spread * noise) if base else spread * noise
        out[name] = __import__('jax').numpy.asarray(drawn.astype(out[name].dtype))
    for name, factor in factors.items():
        out[name] = (out[name] * factor).astype(out[name].dtype)
    return out
```

```python
from contextlib import ExitStack
import math

import numpy as np

import concourse.bass as bass
from concourse import mybir

F32 = mybir.dt.float32
F32R = mybir.dt.float32r
I32 = mybir.dt.int32
ALU = mybir.AluOpType
ACT = mybir.ActivationFunctionType
AX = mybir.AxisListType.X

P = 128
T = 256
D = 1024
KD = D // P
LAYERS = 2
W = 256
TILE = KD * W
RING = 6
SPLIT = 2
NEG = -1e30

RH, RK, RV = 4, 256, 512
NH, NG, HD = 16, 2, 64
NC = (T - 32) // 16 + 1
FF = 2816
KF = FF // P
ACCS = 3


class Plan:

    def __init__(self, banks, ring):
        self.banks, self.ring, self.names, self.tiles, self.count, self.before = banks, ring, [], {}, 0, {}

    def add(self, name, tiles=0):
        self.before[name] = len(self.names)
        self.names.append(name)
        self.tiles[name] = list(range(self.count, self.count + tiles))
        self.count += tiles

    def n(self, name):
        return self.before[name]

    def bank(self, name):
        return self.before[name] % self.banks

    def units_of_bank(self, b):
        return sum(n % self.banks == b for n in range(len(self.names)))

    def tiles_of_slot(self, s):
        return sum(t % self.ring == s for t in range(self.count))

    def last_user(self, t):
        return [u for u in self.names if t in self.tiles[u]][-1]

    def close(self, *phases):
        self.phase, self.split, self.parts = {}, [], []
        for n, (first, last) in enumerate(phases):
            units = self.names[self.n(first):self.n(last) + 1]
            tiles = [t for u in units for t in self.tiles[u]]
            for i, t in enumerate(tiles):
                self.phase[t] = (n, i, tiles)
            self.split += tiles
            self.parts += [t for u in units for t in self.tiles[u][:-1]]
        return self


class Halves:

    def __init__(self, plan, ring, loaded, unit_done, sem):
        self.plan, self.ring, self.loaded, self.unit_done = plan, ring, loaded, unit_done
        self.high_done, self.low_done, self.part_done = sem("weights_high"), sem("weights_low"), sem("part_done")

    def place(self, high, low):
        self.high, self.low = high, low

    def left(self, eng, L, t):
        p = self.plan
        if t in p.parts:
            eng.wait_ge(self.part_done, L * len(p.parts) + p.parts.index(t) + 1)
        else:
            eng.wait_ge(self.unit_done, L * len(p.names) + p.n(p.last_user(t)) + 1)

    def raw_read(self, eng, L, t):
        eng.wait_ge(self.low_done, 2 * (L * len(self.plan.split) + self.plan.split.index(t) + 1))

    def rows(self, t):
        k = 6 if self.plan.last_user(t).startswith("fo") and t == self.plan.tiles[self.plan.last_user(t)][-1] else KD
        return ((0, 4), (4, k))

    def make_high(self, act, nc, L, ph, i):
        tiles = next(v[2] for v in self.plan.phase.values() if v[0] == ph)
        if i >= len(tiles):
            return
        t = tiles[i]
        if i >= SPLIT:
            self.left(act, L, tiles[i - SPLIT])
        s = t % RING
        act.wait_ge(self.loaded[s], 16 * (L * self.plan.tiles_of_slot(s) + t // RING + 1))
        for a, b in self.rows(t):
            nc.scalar.activation(self.high[ph][:, i % SPLIT, a:b, :], self.ring[:, s, a:b, :], ACT.Copy) \
                .then_inc(self.high_done, 1)

    def make_low(self, dve, nc, L, ph, i):
        tiles = next(v[2] for v in self.plan.phase.values() if v[0] == ph)
        if i >= len(tiles):
            return
        t = tiles[i]
        for n, (a, b) in enumerate(self.rows(t)):
            dve.wait_ge(self.high_done, 2 * (L * len(self.plan.split) + self.plan.split.index(t)) + n + 1)
            nc.vector.tensor_tensor(self.low[ph][:, i % SPLIT, a:b, :], self.ring[:, t % RING, a:b, :],
                                    self.high[ph][:, i % SPLIT, a:b, :].bitcast(F32), ALU.subtract) \
                .then_inc(self.low_done, 1)

    def wait_low(self, pe, L, t, n):
        pe.wait_ge(self.low_done, 2 * (L * len(self.plan.split) + self.plan.split.index(t)) + n + 1)

    def features(self, pe, nc, L, t, ps, operand, first=0, chunks=KD, ready=None):
        ph, i, _ = self.plan.phase[t]
        high, low = self.high[ph], self.low[ph]
        hi, lo = operand
        many = chunks > KD
        for j in range(2):
            for k in range(min(KD, chunks - first)):
                if j == 0 and k % 4 == 0:
                    self.wait_low(pe, L, t, k // 4)
                if j == 0 and ready and k % 2 == 0:
                    pe.wait_ge(ready[0], ready[1] + k // 2 + 1)
                c = first + k
                wh, wl = (w[:, i % SPLIT, k, j * P:(j + 1) * P] for w in (high, low))
                nc.tensor.matmul(ps[:, j, :], wh, hi[:, c, :], start=(c == 0 and (j == 0 or not many)), stop=False)
                nc.tensor.matmul(ps[:, j, :], wh, lo[:, c, :], start=False, stop=False)
                last = nc.tensor.matmul(ps[:, j, :], wl, hi[:, c, :], start=False,
                                        stop=(c == chunks - 1 and (j == 1 or not many)))
        return last


def overlay(nc, *tensors):
    guards = [nc.sbuf_tensor(*t) for t in tensors]
    found = [g.__enter__() for g in guards]
    for g in reversed(guards):
        g.__exit__(None, None, None)
    return found


def first_plan():
    p = Plan(ACCS, RING)
    p.add("norm1")
    for h in range(RH):
        p.add(f"qr{h}", 1)
    for h in range(RH):
        p.add(f"kr{h}", 1)
    for u in range(8):
        p.add(f"vr{u}", 1)
    p.add("keys", 1)
    p.add("vals", 1)
    p.add("rawk", 1)
    p.add("rawv", 1)
    for u in range(4):
        p.add(f"qn{u}", 1)
    p.add("gate")
    p.add("hidk", 2)
    p.add("hidv", 2)
    p.add("cmp")
    for u in range(16):
        p.add(f"side{u}", 1)
    for h in range(RH):
        p.add(f"S{h}")
    for h in range(RH):
        p.add(f"O{h}.0")
        p.add(f"O{h}.1")
        if h >= 1:
            p.add(f"mean{h - 1}")
            p.add(f"wn{h - 1}", 1)
            p.add(f"var{h - 1}")
    p.add("mean3")
    p.add("wn3", 1)
    p.add("var3")
    for u in range(4):
        p.add(f"wr{u}", 2)
    for u in range(4):
        p.add(f"wo{u}", 1)
    p.add("norm2")
    for u in range(FF // W):
        p.add(f"fa{u}", 1)
        p.add(f"fb{u}", 1)
    for u in range(4):
        p.add(f"fo{u}", 3)
    return p.close(("wo0", "fo3"))


M_GATE, M_W2K, M_W2V, M_POSK, M_POSV, M_G1, M_G2 = 0, 384, 512, 640, 656, 672, 680
M1 = 688
C_ID, C_ONE, C_MEAN, C_VAR, C_COS, C_SIN, C_DT, C_ROW, C_EPS, C_EPS4, C_GF = \
    0, 128, 256, 384, 512, 1024, 1536, 3072, 3073, 3074, 3075
C1 = 3083


def first_block(nc, outer, ring, x, x_in, w1, m1, c1, onehot, onehot_rev, flip_in, rel):
    plan = first_plan()
    UNITS = len(plan.names)
    with ExitStack() as ctx:
        def sb(name, shape):
            return ctx.enter_context(nc.sbuf_tensor(name, shape, F32))

        def sem(name):
            return outer.enter_context(nc.semaphore(name))

        high_f, low_f, ffh, ffl, ah, al = overlay(
            nc, ("high_f", [P, SPLIT, KD, W], F32R), ("low_f", [P, SPLIT, KD, W], F32R), ("ffh", [P, KF, T], F32R),
            ("ffl", [P, KF + 2, T], F32R), ("ah", [P, KD, T], F32R), ("al", [P, KD, T], F32R))
        qk = sb("qk", [P, KF, T])
        qr = qk[:, 0:8, :]
        kr = qk[:, 8:16, :]
        sT = qk[:, 16:22, :].rearrange("p c t -> p (c t)").rearrange("p (h n) -> p h n", h=RH)
        vr = sb("vr", [P, 2, RH * RV])
        G = sb("G", [P, 16, T])
        raw = G[:, 0:4, :].rearrange("p (s g) t -> p s g t", s=2)
        wins = G[:, 4:8, :].rearrange("p a b -> p (a b)")[:, 0:2 * NG * NC * 16] \
            .rearrange("p (s g n a) -> p s g n a", s=2, g=NG, n=NC)
        tha = sb("tha", [P, KD, T])
        thb = sb("thb", [P, KD, T])
        on = sb("on", [P, KD, T])
        h = sb("h", [P, KD, T])
        dev = h[:, :, :].rearrange("p (b c) t -> p b c t", b=2)
        qn = sb("qn", [P, KD, T])
        mix = qn
        ks = sb("ks", [P, 2, T])
        vs = sb("vs", [P, 2, W])
        hid = sb("hid", [P, 2, 2, NG * NC])
        kc = sb("kc", [P, 16])
        vc = sb("vc", [P, P])
        bias = sb("bias", [P, NH, T])
        cbias = sb("cbias", [P, NH, 2, 16])
        gates = sb("gates", [P, 2, 48])
        work = sb("work", [P, 2 * 800 + 2 * 1024])
        prob = work[:, 0:1600].rearrange("p (b n) -> p b n", b=2)
        probT = work[:, 1600:3648].rearrange("p (b n) -> p b n", b=2)
        sq = work[:, 0:2048].rearrange("p (c t) -> p c t", c=KD)
        htmp = sq
        ft = work[:, 0:1024].rearrange("p (b n) -> p b n", b=2)
        tf = work[:, 2048:3072].rearrange("p (b n) -> p b n", b=2)
        sqh = work[:, 0:2048].rearrange("p (b c t) -> p b c t", b=2, c=4)
        rot = work[:, 0:2048].rearrange("p (b k n) -> p b k n", b=2, k=2)
        part = work[:, 2048:3072].rearrange("p (b n) -> p b n", b=2)
        th = thb[:, 0:4, :].rearrange("p (b c) t -> p b (c t)", b=2)
        rstd = sb("rstd", [P, 2, T])
        stat = sb("stat", [P, 2, 4, 6])
        misc = sb("misc", [P, M1])
        con = sb("con", [P, C1])
        tab = sb("tab", [33, NH])
        setup = G[:, :, :].rearrange("p a b -> p (a b)")
        oh, ohr, rowb = setup[0:33, 0:511], setup[0:33, 512:896], setup[0:NH, 1024:1408]
        flip = setup[:, 1408:1408 + P]
        biasr = vr[:, :, :].rearrange("p a b -> p (a b)")
        row_dram = nc.dram_tensor("row_bias", [NH, 384], F32)

        acc = [ctx.enter_context(nc.psum_tensor(f"acc{b}", [P, 2, T], F32)) for b in range(ACCS)]
        lga = ctx.enter_context(nc.psum_tensor("lga", [P, 512], F32))
        lgb = ctx.enter_context(nc.psum_tensor("lgb", [P, 512], F32))
        tra = ctx.enter_context(nc.psum_tensor("tra", [P, 512], F32))
        trb = ctx.enter_context(nc.psum_tensor("trb", [P, 512], F32))
        avo = ctx.enter_context(nc.psum_tensor("avo", [P, 512], F32))

        flip_banks = (trb, avo, lga, lgb, tra)
        ident = con[:, C_ID:C_ID + P]
        m_one = con[:, C_ONE:C_ONE + P]
        m_mean = con[:, C_MEAN:C_MEAN + P]
        m_var = con[:, C_VAR:C_VAR + P]
        cosq = con[:, C_COS:C_COS + 512]
        sinq = con[:, C_SIN:C_SIN + 512]
        decay = con[:, C_DT:C_DT + RH * 384].rearrange("p (h n) -> p h n", h=RH)

        loaded = [sem(f"tile_loaded{s}") for s in range(RING)]
        misc_in, con_in, x_in_s = sem("misc_loaded"), sem("con_loaded"), sem("x_loaded")
        row_out, bias_in, flipped, bias_set = sem("row_stored"), sem("bias_loaded"), sem("flipped"), sem("bias_set")
        tab_set, row_made, row_copied, cb_made, cb_copied = (sem(n) for n in (
            "tab_set", "row_made", "row_copied", "cb_made", "cb_copied"))
        unit_done = sem("unit_done")
        bank_read = [sem(f"bank_read{b}") for b in range(ACCS)]
        squares, h_ready, x_final = sem("squares"), sem("h_ready"), sem("x_final")
        rstd_ready, final_root = sem("rstd_ready"), sem("final_root")
        rot_added, wins_ready, gates_set = sem("rot_added"), sem("wins_ready"), sem("gates_set")
        lg_done, lg_read, max_ready, exp_done, coef_ready, prob_ready, tr_done, pta, ptb, av_done, on_ready = (
            sem(n) for n in ("logits_done", "logits_read", "max_ready", "exp_done", "coef_ready", "prob_ready",
                             "transposed", "probT_a", "probT_b", "values_done", "on_ready"))
        halves = Halves(plan, ring, loaded, unit_done, sem)
        halves.place([high_f], [low_f])
        high_a, low_a, ffh_ready, ffl_ready = (sem(n) for n in (
            "operand_high", "operand_low", "ff_high", "ff_low"))
        tanh_g, dsq_ready, y_ready, mix_ready = (sem(n) for n in ("tanh_g", "dsq_ready", "y_ready", "mix_ready"))
        link = {e: sem(f"{e}_link") for e in ("dve", "act", "pool")}

        def unit(name):
            return acc[plan.bank(name)]

        def done(eng, L, name):
            eng.wait_ge(unit_done, L * UNITS + plan.n(name) + 1)

        def raw_read(eng, L, t):
            if t in plan.split:
                halves.raw_read(eng, L, t)
            else:
                done(eng, L, plan.last_user(t))

        def read(name):
            return bank_read[plan.bank(name)]

        def taken(eng, L, name):
            b = plan.bank(name)
            eng.wait_ge(bank_read[b], L * plan.units_of_bank(b) + plan.n(name) // ACCS + 1)

        block = ctx.enter_context(nc.Block())

        @block.sync
        def _(sp):
            sp.dma_start(x[:], x_in).then_inc(x_in_s, 16)
            sp.dma_start(con[:], c1).then_inc(con_in, 16)
            sp.dma_start(tab[0:32, :], rel).then_inc(con_in, 16)
            sp.dma_start(oh, onehot).then_inc(con_in, 16)
            sp.dma_start(ohr, onehot_rev).then_inc(con_in, 16)
            sp.dma_start(flip, flip_in).then_inc(con_in, 16)
            for L in range(LAYERS):
                if L:
                    sp.wait_ge(h_ready, L * 16)
                sp.dma_start(misc[:], m1[L]).then_inc(misc_in, 16)
                for name in plan.names:
                    for j, t in enumerate(plan.tiles[name]):
                        s = t % RING
                        if t >= RING:
                            raw_read(sp, L, t - RING)
                        elif L:
                            raw_read(sp, L - 1, max(v for v in range(plan.count) if v % RING == s))
                        k = 6 if name.startswith("fo") and j == 2 else KD
                        sp.dma_start(ring[:, s, 0:k, :].rearrange("p k n -> p (k n)"), w1[L, t, :, 0:k * W]).then_inc(loaded[s], 16)
                        if L == 0 and t == RING - 1:
                            sp.wait_ge(row_copied, 1)
                            sp.dma_start(row_dram[:, :], rowb).then_inc(row_out, 16)
                            sp.wait_ge(row_out, 16)
                            sp.dma_start(biasr.rearrange("p (h n) -> p h n", h=NH),
                                         bass.AP(tensor=row_dram, offset=0, ap=[[1, P], [384, NH], [1, T]])) \
                                .then_inc(bias_in, 16)
        @block.tensor
        def _(pe):
            mm = nc.tensor.matmul

            def begin(L, name):
                b, n = plan.bank(name), plan.n(name)
                before = L * plan.units_of_bank(b) + n // ACCS
                if before:
                    pe.wait_ge(bank_read[b], before)
                return acc[b]

            def tile(L, t):
                s = t % RING
                pe.wait_ge(loaded[s], 16 * (L * plan.tiles_of_slot(s) + t // RING + 1))
                return ring[:, s]

            def features(L, name, src, chunks=KD):
                ps = begin(L, name)
                ws = [tile(L, t) for t in plan.tiles[name]]
                for j in range(2):
                    for k in range(chunks):
                        last = mm(ps[:, j, :], ws[k // KD][:, k % KD, j * P:(j + 1) * P], src[:, k, :],
                                  start=(k == 0), stop=(k == chunks - 1))
                last.then_inc(unit_done, 1)

            def split_features(L, name, operand, chunks=KD, ready=None):
                ps = begin(L, name)
                tiles = plan.tiles[name]
                for i, t in enumerate(tiles):
                    last = halves.features(pe, nc, L, t, ps, operand, i * KD, chunks, ready)
                    last.then_inc(unit_done if t == tiles[-1] else halves.part_done, 1)

            def tokens(L, name, src):
                ps = begin(L, name)
                w = tile(L, plan.tiles[name][0])
                for j in range(2):
                    for k in range(KD):
                        last = mm(ps[:, j, :], src[:, k, j * P:(j + 1) * P], w[:, k, :],
                                  start=(k == 0), stop=(k == KD - 1))
                last.then_inc(unit_done, 1)

            def norm(L, name, base):
                ps = begin(L, name)
                for k in range(KD):
                    if k % 2 == 0:
                        pe.wait_ge(squares, base + k // 2 + 1)
                    last = mm(ps[:, 0, :], m_one, sq[:, k, :], start=(k == 0), stop=(k == KD - 1))
                last.then_inc(unit_done, 1)

            pe.wait_ge(con_in, 80)
            pe.wait_ge(tab_set, 1)
            for qt in range(2):
                for n in range(NC):
                    o = 255 + P * qt - 16 * n - 31
                    last = mm((lga, lgb)[qt][:, n * NH:(n + 1) * NH], oh[:, o:o + P], tab[:, :], start=True, stop=True)
            last.then_inc(cb_made, 1)
            mm(tra[0:NH, 0:384], tab[:, :], ohr, start=True, stop=True).then_inc(row_made, 1)

            for L in range(LAYERS):
                norm(L, "norm1", L * 8)
                pe.wait_ge(h_ready, L * 16 + KD)
                for u in range(RH):
                    features(L, f"qr{u}", h)
                for u in range(RH):
                    features(L, f"kr{u}", h)
                if L == 0:
                    pe.wait_ge(bias_in, 16)
                    pe.wait_ge(cb_copied, 2)
                    pe.wait_ge(row_copied, 1)
                    for i in range(8):
                        if i >= len(flip_banks):
                            pe.wait_ge(bias_set, i - len(flip_banks) + 1)
                        mm(flip_banks[i % len(flip_banks)][:, :], flip, biasr[:, i * 512:(i + 1) * 512],
                           start=True, stop=True).then_inc(flipped, 1)
                for u in range(8):
                    tokens(L, f"vr{u}", h)
                features(L, "keys", h)
                tokens(L, "vals", h)
                features(L, "rawk", h)
                features(L, "rawv", h)
                for u in range(4):
                    features(L, f"qn{u}", h)
                pe.wait_ge(misc_in, 16 * (L + 1))
                ps = begin(L, "gate")
                for j in range(2):
                    for k in range(KD):
                        last = mm(ps[:, j, 0:48], h[:, k, j * P:(j + 1) * P],
                                  misc[:, M_GATE + k * 48:M_GATE + (k + 1) * 48], start=(k == 0), stop=(k == KD - 1))
                last.then_inc(unit_done, 1)
                for s, name in enumerate(("hidk", "hidv")):
                    ps = begin(L, name)
                    ws = [tile(L, t) for t in plan.tiles[name]]
                    pe.wait_ge(wins_ready, L * 2 + s + 1)
                    rhs = wins[:, s].rearrange("p g n a -> p (g n) a")
                    for j in range(2):
                        for a in range(16):
                            last = mm(ps[:, j, 0:NG * NC], ws[a // KD][:, a % KD, j * P:(j + 1) * P], rhs[:, :, a],
                                      start=(a == 0), stop=(a == 15))
                    last.then_inc(unit_done, 1)
                ps = begin(L, "cmp")
                taken(pe, L, "hidk")
                taken(pe, L, "hidv")
                for g in range(NG):
                    for j in range(2):
                        mm(ps[g * 64:(g + 1) * 64, 0, 0:NC], misc[:, M_W2K + j * 64:M_W2K + (j + 1) * 64],
                           hid[:, 0, j, g * NC:(g + 1) * NC], start=(j == 0), stop=(j == 1))
                for g in range(NG):
                    for j in range(2):
                        last = mm(ps[0:NC, 1, g * 64:(g + 1) * 64], hid[:, 1, j, g * NC:(g + 1) * NC],
                                  misc[:, M_W2V + j * 64:M_W2V + (j + 1) * 64], start=(j == 0), stop=(j == 1))
                last.then_inc(unit_done, 1)
                taken(pe, L, "cmp")
                if L == 0:
                    pe.wait_ge(bias_set, 8)
                for n in range(NH + 2):
                    if n < NH:
                        c, g = n // 2, n % 2
                        q = qn[g * 64:(g + 1) * 64, c, :]
                        k = ks[g * 64:(g + 1) * 64]
                        if L * NH + n:
                            pe.wait_ge(lg_read, L * NH + n)
                        mm(lga[:, 0:T], q[:, P:T], k[:, 0, :], start=True, stop=True)
                        mm(lga[:, T:2 * T], q[:, P:T], k[:, 1, :], start=True, stop=True)
                        mm(lgb[:, 0:P], q[:, 0:P], k[:, 0, 0:P], start=True, stop=True)
                        mm(lgb[:, P:2 * P], q[:, 0:P], k[:, 1, 0:P], start=True, stop=True)
                        mm(lgb[:, 256:256 + NC], q[:, 0:P], kc[g * 64:(g + 1) * 64, 0:NC], start=True, stop=True)
                        mm(lgb[:, 272:272 + NC], q[:, P:T], kc[g * 64:(g + 1) * 64, 0:NC], start=True, stop=True) \
                            .then_inc(lg_done, 1)
                        features(L, f"side{n}", h)
                    if 1 <= n <= NH:
                        b = (n - 1) % 2
                        pe.wait_ge(prob_ready, L * NH + n)
                        if L * NH + n - 1:
                            pe.wait_ge(pta, L * NH + n - 1)
                            pe.wait_ge(ptb, L * NH + n - 1)
                        tr = nc.tensor.transpose
                        tr(tra[:, 0:P], prob[:, b, 512:640], ident)
                        tr(tra[:, P:2 * P], prob[:, b, 0:P], ident)
                        tr(tra[:, 2 * P:3 * P], prob[:, b, 640:768], ident)
                        tr(tra[:, 3 * P:4 * P], prob[:, b, 256:384], ident)
                        tr(trb[:, 0:P], prob[:, b, P:2 * P], ident)
                        tr(trb[:, P:2 * P], prob[:, b, 384:512], ident)
                        tr(trb[0:NC, 2 * P:3 * P], prob[:, b, 768:768 + NC], ident)
                        tr(trb[0:NC, 3 * P:4 * P], prob[:, b, 784:784 + NC], ident).then_inc(tr_done, 1)
                    if n >= 2:
                        m = n - 2
                        b, g = m % 2, m % 2
                        pe.wait_ge(pta, L * NH + m + 1)
                        pe.wait_ge(ptb, L * NH + m + 1)
                        if g == 0 and L * 8 + m // 2:
                            pe.wait_ge(on_ready, L * 8 + m // 2)
                        o = avo[g * 64:(g + 1) * 64, 0:T]
                        mm(o, vs[:, 0, g * 64:(g + 1) * 64], probT[:, b, 0:T], start=True, stop=False)
                        mm(o, vs[:, 0, P + g * 64:P + (g + 1) * 64], probT[:, b, T:2 * T], start=False, stop=False)
                        mm(o[:, P:T], vs[:, 1, g * 64:(g + 1) * 64], probT[:, b, 512:640], start=False, stop=False)
                        mm(o[:, P:T], vs[:, 1, P + g * 64:P + (g + 1) * 64], probT[:, b, 640:768],
                           start=False, stop=False)
                        mm(o, vc[0:NC, g * 64:(g + 1) * 64], probT[0:NC, b, 768:1024], start=False, stop=True) \
                            .then_inc(av_done, 1)
                pe.wait_ge(rot_added, L * 8 + 8)
                for u in range(RH):
                    ps = begin(L, f"S{u}").rearrange("p a b -> p (a b)")
                    for k in range(2):
                        mm(ps[:, 0:T], kr[:, 2 * u + k, 0:P], qr[:, 2 * u + k, :], start=(k == 0), stop=(k == 1))
                    for k in range(2):
                        last = mm(ps[:, T:T + P], kr[:, 2 * u + k, P:T], qr[:, 2 * u + k, P:T],
                                  start=(k == 0), stop=(k == 1))
                    last.then_inc(unit_done, 1)

                def heads_out(u, e2):
                    ps = begin(L, f"O{u}.{e2}")
                    taken(pe, L, f"S{u}")
                    for j in range(2):
                        at = u * RV + (2 * e2 + j) * P
                        mm(ps[:, j, :], vr[:, 0, at:at + P], sT[:, u, 0:T], start=True, stop=False)
                        last = mm(ps[:, j, P:T], vr[:, 1, at:at + P], sT[:, u, T:T + P], start=False, stop=True)
                    last.then_inc(unit_done, 1)

                def mean(u):
                    ps = begin(L, f"mean{u}")
                    taken(pe, L, f"O{u}.1")
                    for e in range(4):
                        last = mm(ps[:, 0, :], m_mean, dev[:, u % 2, e, :], start=(e == 0), stop=(e == 3))
                    last.then_inc(unit_done, 1)

                def var(u):
                    ps = begin(L, f"var{u}")
                    pe.wait_ge(dsq_ready, L * RH + u + 1)
                    for e in range(4):
                        last = mm(ps[:, 0, :], m_var, sqh[:, u % 2, e, :], start=(e == 0), stop=(e == 3))
                    last.then_inc(unit_done, 1)

                for u in range(RH):
                    heads_out(u, 0)
                    heads_out(u, 1)
                    if u == 1:
                        pe.wait_ge(on_ready, L * 8 + 8)
                    if u >= 1:
                        mean(u - 1)
                        features(L, f"wn{u - 1}", on)
                        var(u - 1)
                mean(3)
                features(L, "wn3", on)
                var(3)
                pe.wait_ge(y_ready, L * RH + 4)
                for u in range(4):
                    features(L, f"wr{u}", G, 16)
                for u in range(4):
                    split_features(L, f"wo{u}", (ah, al), ready=None if u else (low_a, L * 8))
                norm(L, "norm2", L * 8 + 4)
                for u in range(FF // W):
                    split_features(L, f"fa{u}", (ah, al), ready=None if u else (low_a, L * 8 + 4))
                    split_features(L, f"fb{u}", (ah, al))
                pe.wait_ge(ffl_ready, (L + 1) * (FF // W))
                for u in range(4):
                    split_features(L, f"fo{u}", (ffh, ffl), KF)
            pe.wait_ge(bank_read[0], LAYERS * plan.units_of_bank(0))
            for k in range(KD):
                pe.wait_ge(squares, LAYERS * 8 + k // 2 + 1)
                last = mm(acc[0][:, 0, :], m_one, sq[:, k, :], start=(k == 0), stop=(k == KD - 1))
            last.then_inc(unit_done, 1)

        @block.scalar
        def _(act):
            op = nc.scalar.activation

            def squares_of():
                for p in range(4):
                    yield p
                    op(sq[:, 2 * p:2 * p + 2, :], x[:, 2 * p:2 * p + 2, :], ACT.Square).then_inc(squares, 1)

            def root(name, L):
                done(act, L, name)
                op(rstd[:, 0, :], unit(name)[:, 0, :], ACT.Sqrt, bias=con[:, C_EPS:C_EPS + 1]).then_inc(read(name), 1)

            act.wait_ge(con_in, 80)
            act.wait_ge(cb_made, 1)
            for qt in range(2):
                src = (lga, lgb)[qt][:, 0:NC * NH].rearrange("p (n h) -> p h n", n=NC)
                op(cbias[:, :, qt, 0:NC], src, ACT.Copy).then_inc(cb_copied, 1)
            act.wait_ge(row_made, 1)
            op(rowb, tra[0:NH, 0:384], ACT.Copy).then_inc(row_copied, 1)
            act.wait_ge(x_in_s, 16)
            for L in range(LAYERS):
                for p in squares_of():
                    if L:
                        taken(act, L - 1, f"fo{p}")
                root("norm1", L)
                for u in range(8):
                    done(act, L, f"vr{u}")
                    op(vr[:, :, u * W:(u + 1) * W], unit(f"vr{u}")[:], ACT.Copy).then_inc(read(f"vr{u}"), 1)
                done(act, L, "keys")
                op(ks[:], unit("keys")[:], ACT.Copy).then_inc(read("keys"), 1)
                done(act, L, "vals")
                op(vs[:], unit("vals")[:], ACT.Copy).then_inc(read("vals"), 1)
                for u in range(4):
                    done(act, L, f"qn{u}")
                    op(qn[:, 2 * u:2 * u + 2, :], unit(f"qn{u}")[:], ACT.Copy, scale=HD ** -0.5) \
                        .then_inc(read(f"qn{u}"), 1)
                done(act, L, "gate")
                op(gates[:], unit("gate")[:, :, 0:48], ACT.Tanh, scale=0.5).then_inc(read("gate"), 1)
                for s, name in enumerate(("hidk", "hidv")):
                    done(act, L, name)
                    op(hid[:, s], unit(name)[:, :, 0:NG * NC], ACT.Gelu_apprx_tanh).then_inc(read(name), 1)
                done(act, L, "cmp")
                op(kc[:, 0:NC], unit("cmp")[:, 0, 0:NC], ACT.Copy)
                op(vc[0:NC, :], unit("cmp")[0:NC, 1, 0:P], ACT.Copy).then_inc(read("cmp"), 1)
                for n in range(NH + 2):
                    if n < NH:
                        b = n % 2
                        act.wait_ge(max_ready, L * NH + n + 1)
                        for j, (at, w) in enumerate(((768, NC), (784, NC), (512, P), (0, T), (640, P), (256, T))):
                            last = op(prob[:, b, at:at + w], prob[:, b, at:at + w], ACT.Exp,
                                      bias=stat[:, b, 0, j:j + 1], accum_out=stat[:, b, 1, j:j + 1])
                        last.then_inc(exp_done, 1)
                        name = f"side{n}"
                        done(act, L, name)
                        if n < 8:
                            if n >= 2:
                                taken(act, L, f"side{n - 2}")
                            op(th[:, b, :], unit(name)[:], ACT.Tanh, scale=0.5).then_inc(tanh_g, 1)
                        else:
                            m = (n - 8) % 4
                            op((tha if n < 12 else thb)[:, 2 * m:2 * m + 2, :], unit(name)[:], ACT.Tanh, scale=0.5) \
                                .then_inc(read(name), 1)
                    if 1 <= n <= NH:
                        m, b = n - 1, (n - 1) % 2
                        act.wait_ge(tr_done, L * NH + m + 1)
                        if L * NH + m >= 2:
                            act.wait_ge(av_done, L * NH + m - 1)
                        op(probT[:, b, 0:512], tra[:, :], ACT.Copy).then_inc(pta, 1)
                    if n >= 2 and n % 2 == 1:
                        act.wait_ge(av_done, L * NH + n - 1)
                        op(on[:, (n - 2) // 2, :], avo[:, 0:T], ACT.Copy).then_inc(on_ready, 1)

                def take_heads(u):
                    if u >= 2:
                        act.wait_ge(y_ready, L * RH + u - 1)
                    for e2 in range(2):
                        done(act, L, f"O{u}.{e2}")
                        op(dev[:, u % 2, 2 * e2:2 * e2 + 2, :], unit(f"O{u}.{e2}")[:], ACT.Copy) \
                            .then_inc(read(f"O{u}.{e2}"), 1)

                def square_devs(u):
                    taken(act, L, f"mean{u}")
                    op(sqh[:, u % 2], dev[:, u % 2], ACT.Square).then_inc(dsq_ready, 1)

                def head_root(u):
                    done(act, L, f"var{u}")
                    if u >= 2:
                        act.wait_ge(y_ready, L * RH + u - 1)
                    op(rstd[:, u % 2, :], unit(f"var{u}")[:, 0, :], ACT.Sqrt, bias=con[:, C_EPS4:C_EPS4 + 1]) \
                        .then_inc(read(f"var{u}"), 1)

                take_heads(0)
                take_heads(1)
                square_devs(0)
                head_root(0)
                take_heads(2)
                square_devs(1)
                head_root(1)
                take_heads(3)
                square_devs(2)
                head_root(2)
                square_devs(3)
                head_root(3)
                for i in range(SPLIT):
                    halves.make_high(act, nc, L, 0, i)
                for p in range(4):
                    act.wait_ge(mix_ready, L * 4 + p + 1)
                    op(ah[:, 2 * p:2 * p + 2, :], mix[:, 2 * p:2 * p + 2, :], ACT.Copy).then_inc(high_a, 1)
                for p in squares_of():
                    halves.make_high(act, nc, L, 0, p + SPLIT)
                    taken(act, L, f"wo{p}")
                root("norm2", L)
                for p in range(4):
                    act.wait_ge(h_ready, L * 16 + 8 + 2 * p + 2)
                    op(ah[:, 2 * p:2 * p + 2, :], htmp[:, 2 * p:2 * p + 2, :], ACT.Copy).then_inc(high_a, 1)

                def ff_high(u):
                    taken(act, L, f"fb{u}")
                    op(ffh[:, 2 * u:2 * u + 2, :], ft[:, u % 2, :].rearrange("p (a t) -> p a t", a=2), ACT.Copy) \
                        .then_inc(ffh_ready, 1)

                for u in range(FF // W):
                    halves.make_high(act, nc, L, 0, 4 + 2 * u + SPLIT)
                    done(act, L, f"fa{u}")
                    if u >= 2:
                        taken(act, L, f"fb{u - 2}")
                    op(tf[:, u % 2, :], unit(f"fa{u}")[:], ACT.Silu).then_inc(read(f"fa{u}"), 1)
                    if u:
                        ff_high(u - 1)
                    halves.make_high(act, nc, L, 0, 5 + 2 * u + SPLIT)
                ff_high(FF // W - 1)
                for i in range(12):
                    halves.make_high(act, nc, L, 0, 4 + 2 * (FF // W) + i + SPLIT)
            for p in squares_of():
                taken(act, LAYERS - 1, f"fo{p}")
            act.wait_ge(unit_done, LAYERS * UNITS + 1)
            op(rstd[:, 0, :], acc[0][:, 0, :], ACT.Sqrt, bias=con[:, C_EPS:C_EPS + 1]).then_inc(final_root, 1)

        @block.vector
        def _(dve):
            v = nc.vector
            links = [0]

            def linked(ins):
                links[0] += 1
                ins.then_inc(link["dve"], 1)
                dve.wait_ge(link["dve"], links[0])

            def norm(L, name, gain, h):
                taken(dve, L, name)
                linked(v.reciprocal(rstd[:, 0, :], rstd[:, 0, :]))
                for k in range(KD):
                    v.scalar_tensor_tensor(out=h[:, k, :], in0=x[:, k, :], scalar=misc[:, gain + k:gain + k + 1],
                                           in1=rstd[:, 0, :], op0=ALU.mult, op1=ALU.mult).then_inc(h_ready, 1)

            dve.wait_ge(con_in, 80)
            for L in range(LAYERS):
                dve.wait_ge(misc_in, 16 * (L + 1))
                norm(L, "norm1", M_G1, h)
                for n in range(8):
                    name = f"{'qk'[n // 4]}r{n % 4}"
                    done(dve, L, name)
                    if n >= 2:
                        dve.wait_ge(rot_added, L * 8 + n - 1)
                    ps = unit(name)
                    v.tensor_tensor(rot[:, n % 2, 0].rearrange("p (a t) -> p a t", a=2), ps[:],
                                    cosq.rearrange("p (a t) -> p a t", a=2), ALU.mult)
                    v.tensor_tensor(rot[:, n % 2, 1].rearrange("p (a t) -> p a t", a=2), ps[:, ::-1, :],
                                    sinq.rearrange("p (a t) -> p a t", a=2), ALU.mult).then_inc(read(name), 1)
                if L == 0:
                    for i in range(8):
                        dve.wait_ge(flipped, i + 1)
                        v.tensor_copy(bias[:, 2 * i:2 * i + 2, :].rearrange("p a t -> p (a t)"),
                                      flip_banks[i % len(flip_banks)][:, :]).then_inc(bias_set, 1)
                for s, name in enumerate(("rawk", "rawv")):
                    done(dve, L, name)
                    v.tensor_copy(raw[0:64, s], unit(name)[0:64])
                    v.tensor_copy(raw[64:P, s, :, 0:T - 1], unit(name)[64:P, :, 1:T]).then_inc(read(name), 1)
                taken(dve, L, "gate")
                linked(v.tensor_scalar(gates[:], gates[:], 1.0, 0.5, ALU.add, ALU.mult))
                first = gates[:, 0, :].rearrange("p (h b) -> p h b", b=3)[:, :, 0]
                v.tensor_scalar(first, first, con[:, C_ROW:C_ROW + 1], None, ALU.mult).then_inc(gates_set, 1)
                dve.wait_ge(gates_set, L + 1)
                dve.wait_ge(rot_added, L * 8 + 8)
                if L == 0:
                    dve.wait_ge(cb_copied, 2)
                    dve.wait_ge(bias_set, 8)
                for n in range(NH + 2):
                    if n < NH:
                        b = n % 2
                        hd = (n % 2) * 8 + n // 2
                        dve.wait_ge(lg_done, L * NH + n + 1)
                        if L * NH + n >= 2:
                            dve.wait_ge(tr_done, L * NH + n - 1)
                        s_hi = prob[:, b, 0:512].rearrange("p (s k) -> p s k", s=2)
                        s_lo = prob[:, b, 512:768].rearrange("p (s k) -> p s k", s=2)
                        s_c = prob[:, b, 768:800].rearrange("p (s k) -> p s k", s=2)[:, :, 0:NC]
                        v.tensor_tensor(s_hi, lga[:].rearrange("p (s k) -> p s k", s=2),
                                        bias[:, hd, :].unsqueeze(1).broadcast_to([P, 2, T]), ALU.add)
                        v.tensor_tensor(s_lo, lgb[:, 0:256].rearrange("p (s k) -> p s k", s=2),
                                        bias[:, hd, P:T].unsqueeze(1).broadcast_to([P, 2, P]), ALU.add)
                        v.tensor_tensor(s_c, lgb[:, 256:288].rearrange("p (s k) -> p s k", s=2)[:, :, 0:NC],
                                        cbias[:, hd, :, 0:NC], ALU.add).then_inc(lg_read, 1)
                        dve.wait_ge(lg_read, L * NH + n + 1)
                        v.tensor_reduce(stat[:, b, 0, 3:6:2], s_hi, AX, ALU.max, negate=True)
                        v.tensor_reduce(stat[:, b, 0, 2:5:2], s_lo, AX, ALU.max, negate=True)
                        v.tensor_reduce(stat[:, b, 0, 0:2], s_c, AX, ALU.max, negate=True).then_inc(max_ready, 1)
                    if 1 <= n <= NH:
                        m, b = n - 1, (n - 1) % 2
                        hd = (m % 2) * 8 + m // 2
                        dve.wait_ge(exp_done, L * NH + m + 1)
                        linked(v.reciprocal(stat[:, b, 3, :], stat[:, b, 1, :]))
                        v.tensor_tensor(stat[:, b, 2, :].rearrange("p (b q) -> p b q", q=2),
                                        stat[:, b, 3, :].rearrange("p (b q) -> p b q", q=2),
                                        gates[:, :, 3 * hd:3 * hd + 3].rearrange("p q b -> p b q"), ALU.mult) \
                            .then_inc(coef_ready, 1)
                    if n >= 2:
                        m, b = n - 2, n % 2
                        dve.wait_ge(tr_done, L * NH + m + 1)
                        if L * NH + m >= 2:
                            dve.wait_ge(av_done, L * NH + m - 1)
                        v.tensor_copy(probT[:, b, 512:768], trb[:, 0:256])
                        v.tensor_copy(probT[0:NC, b, 768:1024], trb[0:NC, 256:512]).then_inc(ptb, 1)
                    if n < 8:
                        dve.wait_ge(tanh_g, L * 8 + n + 1)
                        v.scalar_tensor_tensor(out=G[:, 2 * n:2 * n + 2, :], in0=th[:, n % 2, :].rearrange("p (a t) -> p a t", a=2), scalar=1.0,
                                               in1=unit(f"side{n}")[:], op0=ALU.add, op1=ALU.mult) \
                            .then_inc(read(f"side{n}"), 1)
                for u in range(RH):
                    done(dve, L, f"S{u}")
                    v.tensor_tensor(sT[:, u, :], unit(f"S{u}")[:].rearrange("p a t -> p (a t)")[:, 0:384],
                                    decay[:, u, :], ALU.mult).then_inc(read(f"S{u}"), 1)

                def deviations(u):
                    done(dve, L, f"mean{u}")
                    v.tensor_tensor(dev[:, u % 2], dev[:, u % 2],
                                    unit(f"mean{u}")[:, 0, :].unsqueeze(1).broadcast_to([P, 4, T]), ALU.subtract) \
                        .then_inc(read(f"mean{u}"), 1)

                def head_rstd(u):
                    taken(dve, L, f"var{u}")
                    v.reciprocal(rstd[:, u % 2, :], rstd[:, u % 2, :]).then_inc(rstd_ready, 1)

                def take_nsa(u):
                    done(dve, L, f"wn{u}")
                    v.scalar_tensor_tensor(out=mix[:, 2 * u:2 * u + 2, :], in0=thb[:, 2 * u:2 * u + 2, :], scalar=1.0,
                                           in1=unit(f"wn{u}")[:], op0=ALU.add, op1=ALU.mult) \
                        .then_inc(read(f"wn{u}"), 1)

                for u in range(RH):
                    deviations(u)
                    take_nsa(u)
                    head_rstd(u)
                for i in range(SPLIT):
                    halves.make_low(dve, nc, L, 0, i)
                for u in range(4):
                    done(dve, L, f"wr{u}")
                    if u >= 2:
                        dve.wait_ge(mix_ready, L * 4 + u - 1)
                    v.scalar_tensor_tensor(out=part[:, u % 2, :].rearrange("p (a t) -> p a t", a=2),
                                           in0=tha[:, 2 * u:2 * u + 2, :], scalar=1.0,
                                           in1=unit(f"wr{u}")[:], op0=ALU.add, op1=ALU.mult) \
                        .then_inc(read(f"wr{u}"), 1)
                def low_halves(src, base):
                    for p in range(4):
                        dve.wait_ge(high_a, L * 8 + base + p + 1)
                        c = slice(2 * p, 2 * p + 2)
                        v.tensor_tensor(al[:, c, :], src[:, c, :], ah[:, c, :].bitcast(F32), ALU.subtract) \
                            .then_inc(low_a, 1)

                low_halves(mix, 0)
                for u in range(4):
                    done(dve, L, f"wo{u}")
                    v.scalar_tensor_tensor(out=x[:, 2 * u:2 * u + 2, :], in0=unit(f"wo{u}")[:], scalar=0.5,
                                           in1=x[:, 2 * u:2 * u + 2, :], op0=ALU.mult, op1=ALU.add) \
                        .then_inc(read(f"wo{u}"), 1)
                    halves.make_low(dve, nc, L, 0, u + SPLIT)
                norm(L, "norm2", M_G2, htmp)
                low_halves(htmp, 4)
                for u in range(FF // W):
                    halves.make_low(dve, nc, L, 0, 4 + 2 * u + SPLIT)
                    done(dve, L, f"fb{u}")
                    taken(dve, L, f"fa{u}")
                    if u >= 2:
                        dve.wait_ge(ffl_ready, L * (FF // W) + u - 1)
                    v.tensor_tensor(ft[:, u % 2, :].rearrange("p (a t) -> p a t", a=2), unit(f"fb{u}")[:],
                                    tf[:, u % 2, :].rearrange("p (a t) -> p a t", a=2), ALU.mult) \
                        .then_inc(read(f"fb{u}"), 1)
                    halves.make_low(dve, nc, L, 0, 5 + 2 * u + SPLIT)
                for u in range(4):
                    for i in range(3):
                        halves.make_low(dve, nc, L, 0, 4 + 2 * (FF // W) + 3 * u + i + SPLIT)
                    done(dve, L, f"fo{u}")
                    v.tensor_tensor(x[:, 2 * u:2 * u + 2, :], unit(f"fo{u}")[:], x[:, 2 * u:2 * u + 2, :], ALU.add) \
                        .then_inc(read(f"fo{u}"), 1)
            dve.wait_ge(final_root, 1)
            linked(v.reciprocal(rstd[:, 0, :], rstd[:, 0, :]))
            for k in range(KD):
                last = v.scalar_tensor_tensor(out=x[:, k, :], in0=x[:, k, :], scalar=con[:, C_GF + k:C_GF + k + 1],
                                              in1=rstd[:, 0, :], op0=ALU.mult, op1=ALU.mult)
            last.then_inc(x_final, 1)
            dve.wait_ge(x_final, 1)

        @block.gpsimd
        def _(pool):
            g_ = nc.gpsimd
            links = [0]

            def linked(ins):
                links[0] += 1
                ins.then_inc(link["pool"], 1)
                pool.wait_ge(link["pool"], links[0])

            g_.memset(tab[32:33, :], NEG).then_inc(tab_set, 1)
            for L in range(LAYERS):
                for n in range(8):
                    taken(pool, L, f"{'qk'[n // 4]}r{n % 4}")
                    dst = (qr if n < 4 else kr)[:, 2 * (n % 4):2 * (n % 4) + 2, :]
                    g_.tensor_tensor(dst, rot[:, n % 2, 0].rearrange("p (a t) -> p a t", a=2),
                                     rot[:, n % 2, 1].rearrange("p (a t) -> p a t", a=2), ALU.add) \
                        .then_inc(rot_added, 1)
                pool.wait_ge(misc_in, 16 * (L + 1))
                for s, name in enumerate(("rawk", "rawv")):
                    taken(pool, L, name)
                    for g in range(NG):
                        r = raw[:, s, g, :]
                        win = bass.AP(tensor=r.tensor, offset=r.offset, ap=[list(r.ap[0]), [16, NC], [2, 16]])
                        pos = misc[:, M_POSK + 16 * s:M_POSK + 16 * s + 16].unsqueeze(1).broadcast_to([P, NC, 16])
                        last = g_.tensor_tensor(wins[:, s, g], win, pos, ALU.add)
                    last.then_inc(wins_ready, 1)
                for n in range(NH):
                    b = n % 2
                    pool.wait_ge(coef_ready, L * NH + n + 1)
                    for at, w, j in ((0, T, 3), (512, P, 2)):
                        p = prob[:, b, at:at + 2 * w].rearrange("p (s k) -> p s k", s=2)
                        g_.tensor_tensor(p, p, stat[:, b, 2, j:j + 3:2].unsqueeze(2).broadcast_to([P, 2, w]), ALU.mult)
                    p = prob[:, b, 768:800].rearrange("p (s k) -> p s k", s=2)[:, :, 0:NC]
                    g_.tensor_tensor(p, p, stat[:, b, 2, 0:2].unsqueeze(2).broadcast_to([P, 2, NC]), ALU.mult) \
                        .then_inc(prob_ready, 1)
                for u in range(RH):
                    pool.wait_ge(rstd_ready, L * RH + u + 1)
                    linked(g_.tensor_tensor(dev[:, u % 2], dev[:, u % 2],
                                            rstd[:, u % 2, :].unsqueeze(1).broadcast_to([P, 4, T]), ALU.mult))
                    g_.tensor_tensor(G[:, 4 * u:4 * u + 4, :], G[:, 4 * u:4 * u + 4, :], dev[:, u % 2], ALU.mult) \
                        .then_inc(y_ready, 1)
                for u in range(4):
                    taken(pool, L, f"wr{u}")
                    g_.tensor_tensor(mix[:, 2 * u:2 * u + 2, :], mix[:, 2 * u:2 * u + 2, :],
                                     part[:, u % 2, :].rearrange("p (a t) -> p a t", a=2), ALU.add) \
                        .then_inc(mix_ready, 1)
                for u in range(FF // W):
                    pool.wait_ge(ffh_ready, L * (FF // W) + u + 1)
                    c = slice(2 * u, 2 * u + 2)
                    g_.tensor_tensor(ffl[:, c, :], ft[:, u % 2, :].rearrange("p (a t) -> p a t", a=2),
                                     ffh[:, c, :].bitcast(F32), ALU.subtract).then_inc(ffl_ready, 1)


def chunked(w):
    k, n = w.shape
    return w.reshape(k // P, P, n).transpose(1, 0, 2)


def weight_tiles(w):
    k, n = w.shape
    out = []
    for u in range(n // W):
        for r in range(0, k, D):
            t = np.zeros((P, KD, W), np.float32)
            c = chunked(w[r:r + D, u * W:(u + 1) * W])
            t[:, :c.shape[1]] = c
            out.append(t.reshape(P, TILE))
    return out


def first_weights(i, w_in, w1k, w1v, w_o_ret, w_o_nsa, w_out, w_ffn_in, w_ffn_out):
    w = w_in[i]
    q_n, kv = 6144, 7168
    heads = [np.arange(hd * HD, (hd + 1) * HD) for hd in range(NH)]
    order = np.concatenate([np.concatenate([heads[c], heads[8 + c]]) for c in range(8)])
    kvc = lambda s, g=None: kv + s * P + (np.arange(P) if g is None else g * HD + np.arange(HD))
    out = weight_tiles(w[:, 0:4096])
    out += weight_tiles(w[:, np.concatenate([kvc(2), kvc(4)])])
    out += weight_tiles(w[:, np.concatenate([kvc(3), kvc(5)])])
    for s in (0, 1):
        out += weight_tiles(w[:, np.concatenate([kvc(s, 0), kvc(s, 0), kvc(s, 1), kvc(s, 1)])])
    out += weight_tiles(w[:, q_n + order])
    out += weight_tiles(w1k[i]) + weight_tiles(w1v[i])
    out += weight_tiles(w[:, 4096:6144]) + weight_tiles(w[:, 7984:7984 + 2048])
    out += weight_tiles(w_o_nsa[i][order]) + weight_tiles(w_o_ret[i]) + weight_tiles(w_out[i])
    a, b = weight_tiles(w_ffn_in[i][:, :FF]), weight_tiles(w_ffn_in[i][:, FF:])
    for u in range(FF // W):
        out += [a[u], b[u]]
    out += weight_tiles(w_ffn_out[i])
    return np.stack(out)


def first_misc(i, w_in, pos_k, pos_v, w2k, w2v, g1, g2):
    m = np.zeros((P, M1), np.float32)
    m[:, M_GATE:M_GATE + 384] = chunked(w_in[i][:, 7936:7984]).reshape(P, 384)
    m[:, M_W2K:M_W2K + 128] = chunked(w2k[i]).reshape(P, 128)
    m[:, M_W2V:M_W2V + 128] = chunked(w2v[i]).reshape(P, 128)
    for at, pos in ((M_POSK, pos_k), (M_POSV, pos_v)):
        m[:, at:at + 16] = pos[i].reshape(16, P).T
    m[:, M_G1:M_G1 + KD] = g1[i].reshape(KD, P).T
    m[:, M_G2:M_G2 + KD] = g2[i].reshape(KD, P).T
    return m


def first_constants(norm_final_g):
    c = np.zeros((P, C1), np.float32)
    c[:, C_ID:C_ID + P] = np.eye(P)
    c[:, C_ONE:C_ONE + P] = 1 / D
    c[:, C_MEAN:C_MEAN + P] = 1 / RV
    c[:, C_VAR:C_VAR + P] = 4 / RV
    f = np.float32(10000.0) ** (-np.arange(P, dtype=np.float32) / P)
    ang = (np.arange(T, dtype=np.float32)[None] * f[:, None]).astype(np.float64)
    c[:, C_COS:C_COS + 512] = np.concatenate([np.cos(ang)] * 2, 1)
    c[:, C_SIN:C_SIN + 512] = np.concatenate([-np.sin(ang), np.sin(ang)], 1)
    for hd in range(RH):
        lg = math.log(1 - 2.0 ** (-5 - hd))
        m, n = np.arange(P)[:, None], np.arange(T)[None]
        full = np.where(n >= m, np.exp(lg * np.maximum(n - m, 0)), 0) / 16
        c[:, C_DT + hd * 384:C_DT + hd * 384 + T] = full
        c[:, C_DT + hd * 384 + T:C_DT + (hd + 1) * 384] = full[:, 0:P]
    c[:, C_ROW] = np.arange(P) >= 31
    c[:, C_EPS], c[:, C_EPS4] = 1e-6, 4e-5
    c[:, C_GF:C_GF + KD] = norm_final_g.reshape(KD, P).T
    return c


def distance_rows(dist):
    d = np.maximum(dist, 1).astype(np.float32)
    large = 16 + (np.log(d / 16) / np.float32(math.log(8)) * 16).astype(np.int32)
    b = np.where(dist < 16, np.maximum(dist, 0), np.minimum(large, 31))
    b = np.where(dist < 0, 32, b)
    return (np.arange(33)[:, None] == b[None]).astype(np.float32)


AH, BH, CH = 4, 8, 8
HID = 4 * D
KH = HID // P
TOP = 64
ACCS2 = 4
GONE = -3e38
QK_ITEMS = ("ik", "iq", "ck0", "ck1", "cq0", "cq1", "ak0", "ak1", "aq0", "aq1")


def second_plan():
    p = Plan(ACCS2, RING)

    def norm_rot(i):
        if QK_ITEMS[i] != "iq":
            p.add(f"ms_{QK_ITEMS[i]}")
        p.add(f"rot_{QK_ITEMS[i]}")

    p.add("norm1")
    p.add("ik", 1)
    p.add("iq", 1)
    p.add("iw")
    norm_rot(0)
    for i in range(2, len(QK_ITEMS)):
        p.add(QK_ITEMS[i], 1)
        norm_rot(i - 1)
    p.add("bq0", 1)
    norm_rot(len(QK_ITEMS) - 1)
    for name in ("bq1", "bk0", "bk1", "cv0", "cv1", "av0", "av1", "bv0", "bv1"):
        p.add(name, 1)
    for u in range(12):
        p.add(f"gl{u}", 1)

    def branch(name, u):
        p.add(f"{name}{u}", 1 - u % 2)
        if u % 2:
            p.tiles[f"{name}{u}"] = p.tiles[f"{name}{u - 1}"]

    for u in range(4):
        branch("bb", u)
    for u in range(AH):
        branch("bc", u)
        if u >= 2:
            p.add(f"msa{u - 2}")
    p.add("msa2")
    p.add("msa3")
    for u in range(4):
        branch("ba", u)
    for u in range(4):
        p.add(f"wo{u}", 1)
    p.add("norm2")
    for u in range(HID // W):
        p.add(f"up{u}", 1)
    for u in range(4):
        p.add(f"dn{u}", 4)
    p.add("norm3")
    for u in range(4):
        p.add(f"pg{u}", 1)
    for u in range(4):
        p.add(f"pp{u}", 1 if u == 0 else 0)
        p.tiles[f"pp{u}"] = p.tiles["pp0"]
    return p.close(("wo0", "pg3"))


N_IW, N_GAIN, N_SUB, N_LAM, N_G1, N_G2, N_G3, N_LINIT, N_LREST = 0, 32, 37, 38, 294, 302, 310, 318, 319
M2 = 320
GAIN_OF = {"ik": 0, "ck": 1, "cq": 2, "ak": 3, "aq": 4}
E_ID, E_ONE, E_G1, E_G64, E_HEAD, E_ROT, E_TRI, E_NEG, E_CH, E_S01, E_SNEG, E_FREQ, E_EPS, E_EPS64 = \
    0, 128, 256, 384, 512, 640, 768, 896, 1024, 1408, 1792, 2176, 2177, 2178
C2 = 2179
TWO_PI_1 = 6.28125
TWO_PI_2 = float((np.float32(2 * math.pi - TWO_PI_1).view(np.uint32) & np.uint32(0xfffff000)).view(np.float32))
TWO_PI_3 = 2 * math.pi - TWO_PI_1 - TWO_PI_2
MAGIC = 12582912.0


def second_block(nc, outer, ring, x, w2, m2, c2, pos, pt, out):
    plan = second_plan()
    UNITS = len(plan.names)
    with ExitStack() as ctx:
        def sb(name, shape, dt=F32):
            return ctx.enter_context(nc.sbuf_tensor("b_" + name, shape, dt))

        def sem(name):
            return outer.enter_context(nc.semaphore("b_" + name))

        def pairs(ap):
            return ap.rearrange("p (a t) -> p a t", a=2)

        high_f, low_f, hidh, hidl, _, al, ah = overlay(
            nc, ("b_high_f", [P, SPLIT, KD, W], F32R), ("b_low_f", [P, SPLIT, KD, W], F32R),
            ("b_hidh", [P, KH, T], F32R), ("b_hidl", [P, KH, T], F32R), ("b_gap", [P, 8, T], F32),
            ("b_al", [P, KD, T], F32R), ("b_ah", [P, KD, T], F32R))
        qkv = sb("qkv", [P, 36, T])
        cq, ck, aq, ak, bq, bk = (qkv[:, 4 * i:4 * i + 4, :] for i in range(6))
        av, bv, cv = (qkv[:, 24 + 4 * i:28 + 4 * i, :].rearrange("p a b -> p (a b)")
                      .rearrange("p (j n) -> p j n", j=2) for i in range(3))
        gates = sb("gates", [P, 24, T])
        rel = gates[:, 0:6, :].rearrange("p a b -> p (a b)")
        sg = gates[:, 0:8, :]
        ya, yb, yc = (sb(f"y{c}", [P, 4, T]) for c in "abc")
        mrg = sb("mrg", [P, KD, T])
        qkw = sb("qkw", [P, 3, 2, 512])
        att = sb("att", [P, 4608])
        h = sb("h", [P, KD, T])
        iq = sb("iq", [P, 2, T])
        lnb = att[:, 0:768].rearrange("p (b n) -> p b n", b=2)
        spb = att[:, 768:1536].rearrange("p (b n) -> p b n", b=2)
        eb = att[:, 1536:2304].rearrange("p (b n) -> p b n", b=2)
        prob = att[:, 2304:3840].rearrange("p (b n) -> p b n", b=2)
        probT = att[:, 3840:4608].rearrange("p (b n) -> p b n", b=2)
        sq = htmp = att[:, 1024:3072].rearrange("p (c t) -> p c t", c=KD)
        sqa = att[:, 0:512].rearrange("p (b n) -> p b n", b=2)
        rsa = att[:, 512:1024].rearrange("p (b n) -> p b n", b=2)
        ft = att[:, 1024:2048].rearrange("p (b n) -> p b n", b=2)
        part = sb("part", [P, 2, 512])
        ik = sb("ik", [P, T])
        iw = sb("iw", [P, 2, 4])
        score = sb("score", [P, 384])
        mx8 = sb("mx8", [P, 2, 8])
        chosen = sb("chosen", [P, 384])
        rstd = sb("rstd", [P, T])
        stat = sb("stat", [P, 2, 3, 4])
        cosb = sb("cosb", [P, T])
        sinb = sb("sinb", [P, T])
        posi = sb("posi", [P, T], I32)
        ang = mrg[:, 0, :]
        turn = mrg[:, 1:3, :]
        angs = mrg[:, 3:5, :]
        misc = sb("misc", [P, M2])
        lam = sb("lam", [P, 8])
        lamp = sb("lamp", [P, 2, 64])
        pin = sb("pin", [P, 2, T])
        con = sb("con", [P, C2])

        acc = [ctx.enter_context(nc.psum_tensor(f"b_acc{b}", [P, 2, T], F32)) for b in range(ACCS2)]
        lg = [ctx.enter_context(nc.psum_tensor(f"b_lg{b}", [P, 512], F32)) for b in range(2)]
        tr = ctx.enter_context(nc.psum_tensor("b_tr", [P, 512], F32))
        avo = ctx.enter_context(nc.psum_tensor("b_avo", [P, 512], F32))

        def aprob(c, b):
            return prob[:, b, 384 * c:384 * c + 384]

        def cmat(at):
            return con[:, at:at + P]

        loaded = [sem(f"tile_loaded{s}") for s in range(RING)]
        misc_in, con_in, p_in, out_stored = sem("misc_loaded"), sem("con_loaded"), sem("p_loaded"), sem("out_stored")
        unit_done = sem("unit_done")
        bank_read = [sem(f"bank_read{b}") for b in range(ACCS2)]
        angles, rope_set = sem("angles"), sem("rope_set")
        squares, h_ready, x_ple = sem("squares"), sem("h_ready"), sem("x_ple")
        qk_rstd, qk_out = sem("qk_rstd"), sem("qk_out")
        idx_done, rel_ready, chosen_ready, lam_exp = sem("idx_done"), sem("rel_ready"), sem("chosen"), sem("lam_exp")
        lam_in, lam_set = sem("lam_in"), sem("lam_set")
        z_done, ln_ready, z_read, sp_ready, zs_done, e_ready, a_ready, bo_done, yb_ready = (sem(n) for n in (
            "z_done", "ln_ready", "z_read", "sp_ready", "zs_done", "e_ready", "a_ready", "bo_done", "yb_ready"))
        c_lg, c_read, c_max, c_exp, c_coef, c_prob, c_tr, c_pt, c_av, yc_ready = (sem("c_" + n) for n in (
            "logits", "read", "max", "exp", "coef", "prob", "transposed", "probT", "values", "y"))
        a_lg, a_read, a_max, a_exp, a_coef, a_prob, a_tr, a_pt, a_av, a_raw, a_rstd, ya_ready = (
            sem("a_" + n) for n in ("logits", "read", "max", "exp", "coef", "prob", "transposed", "probT", "values",
                                    "raw", "rstd", "y"))
        mrg_ready, relu_ready = sem("mrg_ready"), sem("relu_ready")
        halves = Halves(plan, ring, loaded, unit_done, sem)
        halves.place([high_f], [low_f])
        high_a, low_a, hidh_ready, hidl_ready = (sem(n) for n in (
            "operand_high", "operand_low", "hidden_high", "hidden_low"))
        link = {e: sem(f"{e}_link") for e in ("dve", "act", "pool")}

        def unit(name):
            return acc[plan.bank(name)]

        def done(eng, L, name):
            eng.wait_ge(unit_done, L * UNITS + plan.n(name) + 1)

        def raw_read(eng, L, t):
            if t in plan.split:
                halves.raw_read(eng, L, t)
            else:
                done(eng, L, plan.last_user(t))

        def read(name):
            return bank_read[plan.bank(name)]

        def taken(eng, L, name):
            b = plan.bank(name)
            eng.wait_ge(bank_read[b], L * plan.units_of_bank(b) + plan.n(name) // ACCS2 + 1)

        block = ctx.enter_context(nc.Block())

        @block.sync
        def _(sp):
            sp.dma_start(con[:], c2).then_inc(con_in, 16)
            sp.dma_start(posi[:], pos).then_inc(con_in, 16)
            for L in range(LAYERS):
                for t in range(plan.count):
                    s = t % RING
                    if t >= RING:
                        raw_read(sp, L, t - RING)
                    elif L:
                        raw_read(sp, L - 1, max(v for v in range(plan.count) if v % RING == s))
                    sp.dma_start(ring[:, s, :, :].rearrange("p k n -> p (k n)"), w2[L, t]).then_inc(loaded[s], 16)
                    if t == RING - 1:
                        if L:
                            sp.wait_ge(h_ready, L * 24)
                            sp.wait_ge(x_ple, L * 4)
                        sp.dma_start(misc[:], m2[L]).then_inc(misc_in, 16)
                        sp.dma_start(pin[:], pt[L]).then_inc(p_in, 16)
            sp.wait_ge(x_ple, LAYERS * 4)
            sp.dma_start(out, x[:]).then_inc(out_stored, 16)
            sp.wait_ge(out_stored, 16)

        @block.tensor
        def _(pe):
            mm = nc.tensor.matmul

            def begin(L, name):
                b, n = plan.bank(name), plan.n(name)
                before = L * plan.units_of_bank(b) + n // ACCS2
                if before:
                    pe.wait_ge(bank_read[b], before)
                return acc[b]

            def tile(L, t):
                s = t % RING
                pe.wait_ge(loaded[s], 16 * (L * plan.tiles_of_slot(s) + t // RING + 1))
                return ring[:, s]

            def features(L, name, src, chunks=KD):
                ps = begin(L, name)
                ws = [tile(L, t) for t in plan.tiles[name]]
                for j in range(2):
                    for k in range(chunks):
                        last = mm(ps[:, j, :], ws[k // KD][:, k % KD, j * P:(j + 1) * P], src[:, k, :],
                                  start=(k == 0), stop=(k == chunks - 1))
                last.then_inc(unit_done, 1)

            def split_features(L, name, operand, chunks=KD, ready=None):
                ps = begin(L, name)
                tiles = plan.tiles[name]
                for i, t in enumerate(tiles):
                    last = halves.features(pe, nc, L, t, ps, operand, i * KD, chunks, ready)
                    last.then_inc(unit_done if t == tiles[-1] else halves.part_done, 1)

            def narrow(L, name, src, chunks, at):
                ps = begin(L, name)
                w = tile(L, plan.tiles[name][0]).rearrange("p k n -> p (k n)").rearrange("p (k n) -> p k n", k=chunks)
                for j in range(2):
                    for k in range(chunks):
                        last = mm(ps[:, j, :], w[:, k, at + j * P:at + (j + 1) * P], src[:, k, :],
                                  start=(k == 0), stop=(k == chunks - 1))
                last.then_inc(unit_done, 1)

            def tokens(L, name, src):
                ps = begin(L, name)
                w = tile(L, plan.tiles[name][0])
                for j in range(2):
                    for k in range(KD):
                        last = mm(ps[:, j, :], src[:, k, j * P:(j + 1) * P], w[:, k, :],
                                  start=(k == 0), stop=(k == KD - 1))
                last.then_inc(unit_done, 1)

            def norm(L, name, base):
                ps = begin(L, name)
                for k in range(KD):
                    if k % 2 == 0:
                        pe.wait_ge(squares, base + k // 2 + 1)
                    last = mm(ps[:, 0, :], cmat(E_ONE), sq[:, k, :], start=(k == 0), stop=(k == KD - 1))
                last.then_inc(unit_done, 1)

            def norm_rot(L, i):
                name = QK_ITEMS[i]
                w = T if name == "ik" else 2 * T
                if name != "iq":
                    ps = begin(L, f"ms_{name}").rearrange("p a b -> p (a b)")
                    taken(pe, L, name)
                    mm(ps[:, 0:w], cmat(E_G64 if name[1] == "q" else E_G1), qkw[:, 0, i % 2, 0:w],
                       start=True, stop=True).then_inc(unit_done, 1)
                ps = begin(L, f"rot_{name}").rearrange("p a b -> p (a b)")
                taken(pe, L, name)
                mm(ps[:, 0:w], cmat(E_ROT), qkw[:, 1, i % 2, 0:w], start=True, stop=True).then_inc(unit_done, 1)

            def logits(ps, q, k):
                mm(ps[:, 0:P], q[:, 0:P], k[:, 0:P], start=True, stop=True)
                return mm(ps[:, P:P + T], q[:, P:T], k, start=True, stop=True)

            def transposes(b):
                t = nc.tensor.transpose
                t(tr[:, 0:P], prob[:, b, 0:P], cmat(E_ID))
                t(tr[:, P:2 * P], prob[:, b, P:2 * P], cmat(E_ID))
                return t(tr[:, 2 * P:3 * P], prob[:, b, 2 * P:3 * P], cmat(E_ID))

            pe.wait_ge(con_in, 32)
            for L in range(LAYERS):
                norm(L, "norm1", L * 12)
                pe.wait_ge(h_ready, L * 24 + KD)
                features(L, "ik", h)
                features(L, "iq", h)
                pe.wait_ge(misc_in, 16 * (L + 1))
                ps = begin(L, "iw")
                for j in range(2):
                    for k in range(KD):
                        last = mm(ps[:, j, 0:4], h[:, k, j * P:(j + 1) * P], misc[:, N_IW + 4 * k:N_IW + 4 * k + 4],
                                  start=(k == 0), stop=(k == KD - 1))
                last.then_inc(unit_done, 1)
                norm_rot(L, 0)
                for i in range(2, len(QK_ITEMS)):
                    features(L, QK_ITEMS[i], h)
                    norm_rot(L, i - 1)
                    if i == 3:
                        pe.wait_ge(qk_out, L * 10 + 2)
                        for hd in range(4):
                            r = slice((hd % 2) * 64, (hd % 2) * 64 + 64)
                            q = iq[r, hd // 2, :]
                            mm(lg[hd % 2][:, (hd // 2) * T:(hd // 2) * T + T], q[:, P:T], ik[r, :],
                               start=True, stop=True)
                        for hd in range(4):
                            r = slice((hd % 2) * 64, (hd % 2) * 64 + 64)
                            last = mm((tr, avo)[hd % 2][:, (hd // 2) * P:(hd // 2 + 1) * P], iq[r, hd // 2, 0:P], ik[r, 0:P],
                                      start=True, stop=True)
                        last.then_inc(idx_done, 1)
                features(L, "bq0", h)
                norm_rot(L, len(QK_ITEMS) - 1)
                for name in ("bq1", "bk0", "bk1"):
                    features(L, name, h)
                for name in ("cv0", "cv1", "av0", "av1", "bv0", "bv1"):
                    tokens(L, name, h)
                taken(pe, L, "bv1")
                pe.wait_ge(rel_ready, L + 1)
                for n in range(BH + 1):
                    if n < BH:
                        r = slice((n % 2) * 64, (n % 2) * 64 + 64)
                        if L * BH + n:
                            pe.wait_ge(z_read, L * BH + n)
                        mm(lg[0][:, 0:T], bk[r, n // 2, 0:P], bq[r, n // 2, :], start=True, stop=True)
                        mm(lg[0][:, T:T + P], bk[r, n // 2, P:T], bq[r, n // 2, P:T], start=True, stop=True) \
                            .then_inc(z_done, 1)
                    if n >= 1:
                        m, b = n - 1, (n - 1) % 2
                        r = slice((m % 2) * 64, (m % 2) * 64 + 64)
                        pe.wait_ge(sp_ready, L * BH + m + 1)
                        if L * BH + m:
                            pe.wait_ge(e_ready, L * BH + m)
                        e = lg[1]
                        mm(e[:, 0:T], bk[r, m // 2, 0:P], bq[r, m // 2, :], start=True, stop=False)
                        mm(e[:, 0:T], cmat(E_TRI), spb[:, b, 0:T], start=False, stop=False)
                        mm(e[:, P:T], cmat(E_NEG), spb[:, b, T:T + P], start=False, stop=True)
                        mm(e[:, T:T + P], bk[r, m // 2, P:T], bq[r, m // 2, P:T], start=True, stop=False)
                        mm(e[:, T:T + P], cmat(E_TRI), spb[:, b, T:T + P], start=False, stop=True) \
                            .then_inc(zs_done, 1)
                    if n < BH:
                        features(L, f"gl{n}", h)
                    if n >= 1:
                        m, b = n - 1, (n - 1) % 2
                        pe.wait_ge(a_ready, L * BH + m + 1)
                        if m % 2 == 0:
                            if m:
                                pe.wait_ge(yb_ready, L * 4 + m // 2)
                            elif L:
                                pe.wait_ge(a_raw, L * AH)
                        o = avo[(m % 2) * 64:(m % 2) * 64 + 64, 0:T]
                        mm(o, bv[:, 0, m * 64:(m + 1) * 64], eb[:, b, 0:T], start=True, stop=False)
                        mm(o[:, P:T], bv[:, 1, m * 64:(m + 1) * 64], eb[:, b, T:T + P], start=False, stop=True) \
                            .then_inc(bo_done, 1)
                pe.wait_ge(e_ready, (L + 1) * BH)
                pe.wait_ge(z_read, (L + 1) * BH)
                for n in range(CH + 2):
                    if n < CH:
                        r = slice((n % 2) * 64, (n % 2) * 64 + 64)
                        if n >= 2:
                            pe.wait_ge(c_read, L * CH + n - 1)
                        logits(lg[n % 2], cq[r, n // 2, :], ck[r, n // 2, :]).then_inc(c_lg, 1)
                        if n < 4:
                            features(L, f"gl{8 + n}", h)
                        else:
                            if n == 4:
                                pe.wait_ge(yb_ready, (L + 1) * 4)
                            narrow(L, f"bb{n - 4}", yb, 4, (n % 2) * W)
                    if 1 <= n <= CH:
                        pe.wait_ge(c_prob, L * CH + n)
                        if n >= 2:
                            pe.wait_ge(c_pt, L * CH + n - 1)
                        transposes((n - 1) % 2).then_inc(c_tr, 1)
                    if n >= 2:
                        m, b = n - 2, n % 2
                        pe.wait_ge(c_pt, L * CH + m + 1)
                        if m % 2 == 0:
                            if m:
                                pe.wait_ge(yc_ready, L * 4 + m // 2)
                            else:
                                pe.wait_ge(yb_ready, (L + 1) * 4)
                        o = avo[(m % 2) * 64:(m % 2) * 64 + 64, 0:T]
                        mm(o, cv[:, 0, m * 64:(m + 1) * 64], probT[:, b, 0:T], start=True, stop=False)
                        mm(o[:, P:T], cv[:, 1, m * 64:(m + 1) * 64], probT[:, b, T:T + P], start=False, stop=True) \
                            .then_inc(c_av, 1)
                pe.wait_ge(c_read, (L + 1) * CH)
                pe.wait_ge(yc_ready, (L + 1) * 4)
                for n in range(AH + 2):
                    if n < AH:
                        if n:
                            pe.wait_ge(a_read, L * AH + n)
                        logits(lg[0], aq[0:64, n, :], ak[0:64, n, :])
                        logits(lg[1], aq[64:P, n, :], ak[64:P, n, :]).then_inc(a_lg, 1)
                        narrow(L, f"bc{n}", yc, 4, (n % 2) * W)
                    if 1 <= n <= AH:
                        pe.wait_ge(a_prob, L * AH + n)
                        if n >= 2:
                            pe.wait_ge(a_pt, L * AH + n - 1)
                        transposes((n - 1) % 2).then_inc(a_tr, 1)
                        m, b = n - 1, (n - 1) % 2
                        pe.wait_ge(a_pt, L * AH + m + 1)
                        if m:
                            pe.wait_ge(a_raw, L * AH + m)
                        mm(avo[:, 0:T], av[:, 0, m * P:(m + 1) * P], probT[:, b, 0:T], start=True, stop=False)
                        mm(avo[:, P:T], av[:, 1, m * P:(m + 1) * P], probT[:, b, T:T + P], start=False, stop=True) \
                            .then_inc(a_av, 1)
                    if n >= 2:
                        m = n - 2
                        ps = begin(L, f"msa{m}")
                        pe.wait_ge(a_raw, L * AH + m + 1)
                        mm(ps[:, 0, :], cmat(E_HEAD), sqa[:, m % 2, :], start=True, stop=True).then_inc(unit_done, 1)
                pe.wait_ge(ya_ready, (L + 1) * AH)
                for u in range(4):
                    narrow(L, f"ba{u}", ya, 4, (u % 2) * W)
                for u in range(4):
                    split_features(L, f"wo{u}", (ah, al), ready=None if u else (low_a, L * 12))
                norm(L, "norm2", L * 12 + 4)
                for u in range(HID // W):
                    split_features(L, f"up{u}", (ah, al), ready=None if u else (low_a, L * 12 + 4))
                pe.wait_ge(hidl_ready, (L + 1) * (HID // W))
                for u in range(4):
                    split_features(L, f"dn{u}", (hidh, hidl), KH)
                norm(L, "norm3", L * 12 + 8)
                for u in range(4):
                    split_features(L, f"pg{u}", (ah, al), ready=None if u else (low_a, L * 12 + 8))
                pe.wait_ge(p_in, 16 * (L + 1))
                for u in range(4):
                    narrow(L, f"pp{u}", pin, 2, u * W)

        @block.scalar
        def _(act):
            op = nc.scalar.activation
            links = [0]

            def linked(ins):
                links[0] += 1
                ins.then_inc(link["act"], 1)
                act.wait_ge(link["act"], links[0])

            def squares_of():
                for p in range(4):
                    yield p
                    op(sq[:, 2 * p:2 * p + 2, :], x[:, 2 * p:2 * p + 2, :], ACT.Square).then_inc(squares, 1)

            def root(L, name):
                done(act, L, name)
                op(rstd[:, :], unit(name)[:, 0, :], ACT.Sqrt, bias=con[:, E_EPS:E_EPS + 1]).then_inc(read(name), 1)

            def raw_item(L, i):
                name = QK_ITEMS[i]
                w = T if name == "ik" else 2 * T
                done(act, L, name)
                if i >= 2:
                    act.wait_ge(qk_out, L * 10 + i - 1)
                ps = unit(name)[:].rearrange("p a b -> p (a b)")[:, 0:w]
                if name == "iq":
                    op(qkw[:, 1, i % 2, 0:w], ps, ACT.Copy).then_inc(read(name), 1)
                else:
                    g = N_GAIN + GAIN_OF[name[:2]]
                    op(qkw[:, 0, i % 2, 0:w], ps, ACT.Square)
                    op(qkw[:, 1, i % 2, 0:w], ps, ACT.Copy, scale=misc[:, g:g + 1]).then_inc(read(name), 1)

            def root_item(L, i):
                name = QK_ITEMS[i]
                if name != "iq":
                    w = T if name == "ik" else 2 * T
                    done(act, L, f"ms_{name}")
                    e = E_EPS64 if name[1] == "q" else E_EPS
                    op(qkw[:, 0, i % 2, 0:w], unit(f"ms_{name}")[:].rearrange("p a b -> p (a b)")[:, 0:w], ACT.Sqrt,
                       bias=con[:, e:e + 1]).then_inc(read(f"ms_{name}"), 1)

            act.wait_ge(con_in, 32)
            act.wait_ge(angles, 1)
            op(sinb[:, :], angs[:, 0, :], ACT.Sin)
            op(cosb[:, :], angs[:, 1, :], ACT.Sin).then_inc(rope_set, 1)
            for L in range(LAYERS):
                for p in squares_of():
                    if L:
                        act.wait_ge(x_ple, (L - 1) * 4 + p + 1)
                root(L, "norm1")
                act.wait_ge(misc_in, 16 * (L + 1))
                raw_item(L, 0)
                raw_item(L, 1)
                done(act, L, "iw")
                op(iw[:], unit("iw")[:, :, 0:4], ACT.Copy, scale=0.5).then_inc(read("iw"), 1)
                root_item(L, 0)
                for i in range(2, len(QK_ITEMS)):
                    raw_item(L, i)
                    root_item(L, i - 1)
                    if i == 3:
                        act.wait_ge(idx_done, L + 1)
                        op(rel[:, 0:512], lg[0][:, :], ACT.Relu, scale=HD ** -0.5)
                        op(rel[:, 512:1024], lg[1][:, :], ACT.Relu, scale=HD ** -0.5)
                        op(rel[:, 1024:1280], tr[:, 0:T], ACT.Relu, scale=HD ** -0.5)
                        op(rel[:, 1280:1536], avo[:, 0:T], ACT.Relu, scale=HD ** -0.5).then_inc(rel_ready, 1)
                done(act, L, "bq0")
                op(bq[:, 0:2, :], unit("bq0")[:], ACT.Copy, scale=HD ** -0.5).then_inc(read("bq0"), 1)
                root_item(L, len(QK_ITEMS) - 1)
                for name, dst, s in (("bq1", bq[:, 2:4, :], HD ** -0.5), ("bk0", bk[:, 0:2, :], 1.0),
                                     ("bk1", bk[:, 2:4, :], 1.0),
                                     ("cv0", cv[:, :, 0:W], 1.0), ("cv1", cv[:, :, W:2 * W], 1.0),
                                     ("av0", av[:, :, 0:W], 1.0), ("av1", av[:, :, W:2 * W], 1.0),
                                     ("bv0", bv[:, :, 0:W], 1.0), ("bv1", bv[:, :, W:2 * W], 1.0)):
                    done(act, L, name)
                    op(dst, unit(name)[:], ACT.Copy, scale=s).then_inc(read(name), 1)
                act.wait_ge(lam_in, L + 1)
                op(lam[:, 2:4], lam[:, 0:2], ACT.Exp).then_inc(lam_exp, 1)
                act.wait_ge(chosen_ready, L + 1)
                for n in range(BH + 1):
                    if n < BH:
                        b = n % 2
                        act.wait_ge(z_done, L * BH + n + 1)
                        if L * BH + n >= 2:
                            act.wait_ge(z_read, L * BH + n - 1)
                        linked(op(lnb[:, b, :], lg[0][:, 0:384], ACT.Abs))
                        linked(op(lnb[:, b, :], lnb[:, b, :], ACT.Exp, scale=-1.0))
                        op(lnb[:, b, :], lnb[:, b, :], ACT.Ln, bias=1.0).then_inc(ln_ready, 1)
                    if n >= 1:
                        act.wait_ge(e_ready, L * BH + n)
                        b = (n - 1) % 2
                        op(eb[:, b, :], eb[:, b, :], ACT.Exp).then_inc(a_ready, 1)
                    if n < BH:
                        done(act, L, f"gl{n}")
                        op(gates[:, 2 * n:2 * n + 2, :], unit(f"gl{n}")[:], ACT.Tanh, scale=0.5) \
                            .then_inc(read(f"gl{n}"), 1)
                    if n >= 2 and n % 2 == 0:
                        act.wait_ge(bo_done, L * BH + n)
                        op(yb[:, n // 2 - 1, :], avo[:, 0:T], ACT.Copy).then_inc(yb_ready, 1)
                for n in range(CH + 2):
                    if n < CH:
                        b = n % 2
                        act.wait_ge(c_max, L * CH + n + 1)
                        op(prob[:, b, 0:P], prob[:, b, 0:P], ACT.Exp, bias=stat[:, b, 0, 0:1],
                           accum_out=stat[:, b, 1, 0:1])
                        op(prob[:, b, P:384], prob[:, b, P:384], ACT.Exp, bias=stat[:, b, 0, 1:2],
                           accum_out=stat[:, b, 1, 1:2]).then_inc(c_exp, 1)
                        if n < 4:
                            done(act, L, f"gl{8 + n}")
                            op(gates[:, 16 + 2 * n:18 + 2 * n, :], unit(f"gl{8 + n}")[:], ACT.Tanh, scale=0.5) \
                                .then_inc(read(f"gl{8 + n}"), 1)
                    if 1 <= n <= CH:
                        m, b = n - 1, (n - 1) % 2
                        act.wait_ge(c_tr, L * CH + n)
                        if m >= 2:
                            act.wait_ge(c_av, L * CH + m - 1)
                        op(probT[:, b, :], tr[:, 0:384], ACT.Copy).then_inc(c_pt, 1)
                    if n >= 3 and n % 2 == 1:
                        act.wait_ge(c_av, L * CH + n - 1)
                        op(yc[:, (n - 3) // 2, :], avo[:, 0:T], ACT.Copy).then_inc(yc_ready, 1)
                act.wait_ge(c_av, (L + 1) * CH)
                for n in range(AH + 2):
                    if n < AH:
                        b = n % 2
                        act.wait_ge(a_max, L * AH + n + 1)
                        for c in range(2):
                            for t, (lo, hi) in enumerate(((0, P), (P, 384))):
                                p = aprob(c, b)[:, lo:hi]
                                last = op(p, p, ACT.Exp, bias=stat[:, b, 0, 2 * c + t:2 * c + t + 1],
                                          accum_out=stat[:, b, 1, 2 * c + t:2 * c + t + 1])
                        last.then_inc(a_exp, 1)
                    if 1 <= n <= AH:
                        m, b = n - 1, (n - 1) % 2
                        act.wait_ge(a_tr, L * AH + n)
                        op(probT[:, b, :], tr[:, 0:384], ACT.Copy).then_inc(a_pt, 1)
                        act.wait_ge(a_av, L * AH + n)
                        if m >= 2:
                            done(act, L, f"msa{m - 2}")
                        op(sqa[:, b, :], avo[:, 0:T], ACT.Square)
                        op(ya[:, m, :], avo[:, 0:T], ACT.Copy).then_inc(a_raw, 1)
                    if n >= 2:
                        m = n - 2
                        done(act, L, f"msa{m}")
                        if m >= 2:
                            act.wait_ge(ya_ready, L * AH + m - 1)
                        op(rsa[:, m % 2, :], unit(f"msa{m}")[:, 0, :], ACT.Sqrt, bias=con[:, E_EPS:E_EPS + 1]) \
                            .then_inc(read(f"msa{m}"), 1)
                act.wait_ge(ya_ready, (L + 1) * AH)
                for i in range(SPLIT):
                    halves.make_high(act, nc, L, 0, i)

                def high_halves(src, p):
                    op(ah[:, 2 * p:2 * p + 2, :], src[:, 2 * p:2 * p + 2, :], ACT.Copy).then_inc(high_a, 1)

                for p in range(4):
                    act.wait_ge(mrg_ready, L * 8 + 4 + p + 1)
                    high_halves(mrg, p)
                for p in squares_of():
                    halves.make_high(act, nc, L, 0, p + SPLIT)
                    taken(act, L, f"wo{p}")
                root(L, "norm2")
                for p in range(4):
                    act.wait_ge(h_ready, L * 24 + 8 + 2 * p + 2)
                    high_halves(htmp, p)

                def hidden_high(u):
                    taken(act, L, f"up{u}")
                    op(hidh[:, 2 * u:2 * u + 2, :], pairs(ft[:, u % 2, :]), ACT.Copy).then_inc(hidh_ready, 1)

                for u in range(HID // W):
                    halves.make_high(act, nc, L, 0, 4 + u + SPLIT)
                    done(act, L, f"up{u}")
                    if u >= 2:
                        taken(act, L, f"up{u - 2}")
                    op(pairs(part[:, u % 2, :]), unit(f"up{u}")[:], ACT.Relu).then_inc(relu_ready, 1)
                    if u:
                        hidden_high(u - 1)
                hidden_high(HID // W - 1)
                for p in squares_of():
                    for i in range(4):
                        halves.make_high(act, nc, L, 0, 4 + HID // W + 4 * p + i + SPLIT)
                    taken(act, L, f"dn{p}")
                root(L, "norm3")
                for p in range(4):
                    act.wait_ge(h_ready, L * 24 + 16 + 2 * p + 2)
                    high_halves(htmp, p)
                for u in range(4):
                    halves.make_high(act, nc, L, 0, 20 + HID // W + u + SPLIT)
                    done(act, L, f"pg{u}")
                    op(sg[:, 2 * u:2 * u + 2, :], unit(f"pg{u}")[:], ACT.Tanh, scale=0.5).then_inc(read(f"pg{u}"), 1)

        @block.vector
        def _(dve):
            v = nc.vector
            links = [0]

            def linked(ins):
                links[0] += 1
                ins.then_inc(link["dve"], 1)
                dve.wait_ge(link["dve"], links[0])

            def norm(L, name, gain, h):
                taken(dve, L, name)
                linked(v.reciprocal(rstd[:, :], rstd[:, :]))
                for k in range(KD):
                    v.scalar_tensor_tensor(out=h[:, k, :], in0=x[:, k, :], scalar=misc[:, gain + k:gain + k + 1],
                                           in1=rstd[:, :], op0=ALU.mult, op1=ALU.mult).then_inc(h_ready, 1)

            def item(L, i):
                name = QK_ITEMS[i]
                w = T if name == "ik" else 2 * T
                a = w // T
                done(dve, L, f"rot_{name}")
                if i >= 2:
                    dve.wait_ge(qk_out, L * 10 + i - 1)
                v.tensor_tensor(qkw[:, 2, i % 2, 0:w].rearrange("p (a t) -> p a t", a=a),
                                unit(f"rot_{name}")[:, 0:a, :], sinb[:].unsqueeze(1).broadcast_to([P, a, T]),
                                ALU.mult).then_inc(read(f"rot_{name}"), 1)
                if name != "iq":
                    taken(dve, L, f"ms_{name}")
                    v.reciprocal(qkw[:, 0, i % 2, 0:w], qkw[:, 0, i % 2, 0:w]).then_inc(qk_rstd, 1)

            def index_score(L):
                dve.wait_ge(rel_ready, L + 1)
                taken(dve, L, "iw")
                for j, (lo, hi, base, w) in enumerate(((0, P, 1024, P), (P, 384, 0, T))):
                    s = score[:, lo:hi]
                    for hd in range(4):
                        at = base + ((hd % 2) * 2 + hd // 2) * w
                        r = rel[:, at:at + w]
                        if hd == 0:
                            linked(v.tensor_scalar(s, r, iw[:, j, 0:1], 0.0, ALU.mult, ALU.add))
                        else:
                            linked(v.scalar_tensor_tensor(out=s, in0=r, scalar=iw[:, j, hd:hd + 1], in1=s,
                                                          op0=ALU.mult, op1=ALU.add))
                linked(v.tensor_tensor(score[:, :], score[:, :], con[:, E_CH:E_CH + 384], ALU.add))

            def top_eight():
                for j, (lo, hi) in enumerate(((0, P), (P, 384))):
                    linked(v.max(mx8[:, j, :], score[:, lo:hi]))
                    linked(v.match_replace(score[:, lo:hi], mx8[:, j, :], score[:, lo:hi], GONE))

            dve.wait_ge(con_in, 32)
            linked(v.tensor_copy(ang, posi[:, :]))
            linked(v.tensor_scalar(ang, ang, con[:, E_FREQ:E_FREQ + 1], None, ALU.mult))
            for j, quarter in ((0, 0.0), (1, 0.25)):
                linked(v.tensor_scalar(turn[:, j, :], ang, 1 / (2 * math.pi), quarter, ALU.mult, ALU.add))
                linked(v.tensor_scalar(turn[:, j, :], turn[:, j, :], MAGIC, None, ALU.add))
                linked(v.tensor_scalar(turn[:, j, :], turn[:, j, :], -MAGIC, None, ALU.add))
                linked(v.scalar_tensor_tensor(out=angs[:, j, :], in0=turn[:, j, :], scalar=-TWO_PI_1, in1=ang,
                                              op0=ALU.mult, op1=ALU.add))
                for c in (TWO_PI_2, TWO_PI_3):
                    linked(v.scalar_tensor_tensor(out=angs[:, j, :], in0=turn[:, j, :], scalar=-c,
                                                  in1=angs[:, j, :], op0=ALU.mult, op1=ALU.add))
                if j:
                    linked(v.tensor_scalar(angs[:, j, :], angs[:, j, :], math.pi / 2, None, ALU.add))
                ins = v.tensor_scalar(angs[:, j, :], angs[:, j, :], -3.1415925, 3.1415925, ALU.max, ALU.min)
                if j:
                    ins.then_inc(angles, 1)
            for L in range(LAYERS):
                dve.wait_ge(misc_in, 16 * (L + 1))
                norm(L, "norm1", N_G1, h)
                l4 = misc[:, N_LAM:N_LAM + 256].rearrange("p (a b d) -> p a b d", a=2, b=2)
                linked(v.tensor_tensor(lamp[:], l4[:, :, 0, :], l4[:, :, 1, :], ALU.mult))
                v.tensor_reduce(lam[:, 0:2], lamp[:], AX, ALU.add).then_inc(lam_in, 1)
                if L == 0:
                    dve.wait_ge(rope_set, 1)
                for i in range(4):
                    item(L, i)
                index_score(L)
                for i in range(4, len(QK_ITEMS)):
                    top_eight()
                    item(L, i)
                for _ in range(TOP // 8 - (len(QK_ITEMS) - 4)):
                    top_eight()
                v.tensor_scalar(chosen[:, :], score[:, :], GONE / 2, NEG, ALU.is_gt, ALU.mult) \
                    .then_inc(chosen_ready, 1)
                dve.wait_ge(chosen_ready, L + 1)
                dve.wait_ge(lam_exp, L + 1)
                linked(v.tensor_tensor(lam[:, 4:5], lam[:, 3:4], lam[:, 2:3], ALU.subtract))
                linked(v.tensor_tensor(lam[:, 5:6], lam[:, 4:5], misc[:, N_LINIT:N_LINIT + 1], ALU.subtract))
                v.tensor_tensor(lam[:, 6:7], misc[:, N_SUB:N_SUB + 1], misc[:, N_LREST:N_LREST + 1], ALU.mult) \
                    .then_inc(lam_set, 1)
                dve.wait_ge(lam_set, L + 1)
                for n in range(BH + 1):
                    if n < BH:
                        b = n % 2
                        dve.wait_ge(ln_ready, L * BH + n + 1)
                        if n >= 2:
                            dve.wait_ge(zs_done, L * BH + n - 1)
                        v.scalar_tensor_tensor(out=spb[:, b, :], in0=lg[0][:, 0:384], scalar=0.0, in1=lnb[:, b, :],
                                               op0=ALU.max, op1=ALU.add).then_inc(z_read, 1)
                    if n >= 1:
                        m, b = n - 1, (n - 1) % 2
                        dve.wait_ge(zs_done, L * BH + n)
                        if m >= 2:
                            dve.wait_ge(bo_done, L * BH + m - 1)
                        v.tensor_tensor(eb[:, b, :], lg[1][:, 0:384], con[:, E_SNEG:E_SNEG + 384], ALU.add) \
                            .then_inc(e_ready, 1)
                for n in range(CH + 1):
                    if n < CH:
                        b = n % 2
                        dve.wait_ge(c_lg, L * CH + n + 1)
                        if n >= 2:
                            dve.wait_ge(c_tr, L * CH + n - 1)
                        v.tensor_tensor(prob[:, b, 0:384], lg[b][:, 0:384], chosen[:, :], ALU.add).then_inc(c_read, 1)
                        dve.wait_ge(c_read, L * CH + n + 1)
                        v.tensor_reduce(stat[:, b, 0, 0:1], prob[:, b, 0:P], AX, ALU.max, negate=True)
                        v.tensor_reduce(stat[:, b, 0, 1:2], prob[:, b, P:384], AX, ALU.max, negate=True) \
                            .then_inc(c_max, 1)
                    if n >= 1:
                        b = (n - 1) % 2
                        dve.wait_ge(c_exp, L * CH + n)
                        v.reciprocal(stat[:, b, 2, 0:2], stat[:, b, 1, 0:2]).then_inc(c_coef, 1)
                    if 4 <= n < CH:
                        u = n - 4
                        done(dve, L, f"bb{u}")
                        v.scalar_tensor_tensor(out=mrg[:, 2 * u:2 * u + 2, :], in0=gates[:, 8 + 2 * u:10 + 2 * u, :],
                                               scalar=1.0, in1=unit(f"bb{u}")[:], op0=ALU.add, op1=ALU.mult) \
                            .then_inc(read(f"bb{u}"), 1)

                def gated(L, name, gate, n):
                    done(dve, L, name)
                    if n >= 2:
                        dve.wait_ge(mrg_ready, L * 8 + n - 1)
                    v.scalar_tensor_tensor(out=pairs(part[:, n % 2, :]), in0=gates[:, gate:gate + 2, :], scalar=1.0,
                                           in1=unit(name)[:], op0=ALU.add, op1=ALU.mult).then_inc(read(name), 1)

                def head_norm(L, m):
                    taken(dve, L, f"msa{m}")
                    linked(v.reciprocal(rsa[:, m % 2, :], rsa[:, m % 2, :]))
                    v.scalar_tensor_tensor(out=ya[:, m, :], in0=ya[:, m, :], scalar=lam[:, 6:7], in1=rsa[:, m % 2, :],
                                           op0=ALU.mult, op1=ALU.mult).then_inc(ya_ready, 1)

                dve.wait_ge(c_tr, (L + 1) * CH)
                for n in range(AH + 2):
                    if n < AH:
                        b = n % 2
                        dve.wait_ge(a_lg, L * AH + n + 1)
                        if n >= 2:
                            dve.wait_ge(a_tr, L * AH + n - 1)
                        for c in range(2):
                            last = v.tensor_tensor(aprob(c, b), lg[c][:, 0:384], con[:, E_CH:E_CH + 384], ALU.add)
                        last.then_inc(a_read, 1)
                        dve.wait_ge(a_read, L * AH + n + 1)
                        for c in range(2):
                            for t, (lo, hi) in enumerate(((0, P), (P, 384))):
                                last = v.tensor_reduce(stat[:, b, 0, 2 * c + t:2 * c + t + 1], aprob(c, b)[:, lo:hi],
                                                       AX, ALU.max, negate=True)
                        last.then_inc(a_max, 1)
                        dve.wait_ge(a_exp, L * AH + n + 1)
                        linked(v.reciprocal(stat[:, b, 2, :], stat[:, b, 1, :]))
                        v.tensor_scalar(stat[:, b, 2, 2:4], stat[:, b, 2, 2:4], lam[:, 5:6], None, ALU.mult) \
                            .then_inc(a_coef, 1)
                        gated(L, f"bc{n}", 16 + 2 * n, n)
                    if n >= 2:
                        head_norm(L, n - 2)
                for u in range(4):
                    gated(L, f"ba{u}", 2 * u, 4 + u)
                    if u < SPLIT:
                        halves.make_low(dve, nc, L, 0, u)

                def low_halves(src, base):
                    for p in range(4):
                        dve.wait_ge(high_a, L * 12 + base + p + 1)
                        c = slice(2 * p, 2 * p + 2)
                        v.tensor_tensor(al[:, c, :], src[:, c, :], ah[:, c, :].bitcast(F32), ALU.subtract) \
                            .then_inc(low_a, 1)

                low_halves(mrg, 0)
                for u in range(4):
                    done(dve, L, f"wo{u}")
                    v.scalar_tensor_tensor(out=x[:, 2 * u:2 * u + 2, :], in0=unit(f"wo{u}")[:], scalar=0.5,
                                           in1=x[:, 2 * u:2 * u + 2, :], op0=ALU.mult, op1=ALU.add) \
                        .then_inc(read(f"wo{u}"), 1)
                    halves.make_low(dve, nc, L, 0, u + SPLIT)
                norm(L, "norm2", N_G2, htmp)
                low_halves(htmp, 4)
                for u in range(HID // W):
                    dve.wait_ge(relu_ready, L * (HID // W) + u + 1)
                    if u >= 2:
                        dve.wait_ge(hidl_ready, L * (HID // W) + u - 1)
                    v.tensor_tensor(pairs(ft[:, u % 2, :]), pairs(part[:, u % 2, :]), unit(f"up{u}")[:], ALU.mult) \
                        .then_inc(read(f"up{u}"), 1)
                    halves.make_low(dve, nc, L, 0, 4 + u + SPLIT)
                for u in range(4):
                    for i in range(4):
                        halves.make_low(dve, nc, L, 0, 4 + HID // W + 4 * u + i + SPLIT)
                    done(dve, L, f"dn{u}")
                    v.tensor_tensor(x[:, 2 * u:2 * u + 2, :], unit(f"dn{u}")[:], x[:, 2 * u:2 * u + 2, :], ALU.add) \
                        .then_inc(read(f"dn{u}"), 1)
                norm(L, "norm3", N_G3, htmp)
                low_halves(htmp, 8)
                for u in range(4):
                    halves.make_low(dve, nc, L, 0, 20 + HID // W + u + SPLIT)
                for u in range(4):
                    done(dve, L, f"pp{u}")
                    taken(dve, L, f"pg{u}")
                    v.scalar_tensor_tensor(out=pairs(part[:, u % 2, :]), in0=sg[:, 2 * u:2 * u + 2, :], scalar=1.0,
                                           in1=unit(f"pp{u}")[:], op0=ALU.add, op1=ALU.mult) \
                        .then_inc(read(f"pp{u}"), 1)
                    taken(dve, L, f"pp{u}")
                    v.scalar_tensor_tensor(out=x[:, 2 * u:2 * u + 2, :], in0=pairs(part[:, u % 2, :]), scalar=0.5,
                                           in1=x[:, 2 * u:2 * u + 2, :], op0=ALU.mult, op1=ALU.add).then_inc(x_ple, 1)

        @block.gpsimd
        def _(pool):
            g_ = nc.gpsimd
            links = [0]

            def linked(ins):
                links[0] += 1
                ins.then_inc(link["pool"], 1)
                pool.wait_ge(link["pool"], links[0])

            pool.wait_ge(con_in, 32)
            pool.wait_ge(rope_set, 1)
            dest = {"ik": ik[:].unsqueeze(1), "iq": iq[:], "ck0": ck[:, 0:2, :], "ck1": ck[:, 2:4, :],
                    "cq0": cq[:, 0:2, :], "cq1": cq[:, 2:4, :], "ak0": ak[:, 0:2, :], "ak1": ak[:, 2:4, :],
                    "aq0": aq[:, 0:2, :], "aq1": aq[:, 2:4, :]}
            for L in range(LAYERS):
                for i, name in enumerate(QK_ITEMS):
                    a = 1 if name == "ik" else 2
                    view = [qkw[:, c, i % 2, 0:a * T].rearrange("p (a t) -> p a t", a=a) for c in range(3)]
                    taken(pool, L, f"rot_{name}")
                    linked(g_.tensor_tensor(view[1], view[1], cosb[:].unsqueeze(1).broadcast_to([P, a, T]), ALU.mult))
                    if name == "iq":
                        g_.tensor_tensor(dest[name], view[1], view[2], ALU.add).then_inc(qk_out, 1)
                    else:
                        linked(g_.tensor_tensor(view[1], view[1], view[2], ALU.add))
                        pool.wait_ge(qk_rstd, L * 9 + (1 if i == 0 else i))
                        g_.tensor_tensor(dest[name], view[1], view[0], ALU.mult).then_inc(qk_out, 1)
                for n in range(BH):
                    pool.wait_ge(z_read, L * BH + n + 1)
                    g_.tensor_tensor(spb[:, n % 2, :], spb[:, n % 2, :], con[:, E_S01:E_S01 + 384], ALU.mult) \
                        .then_inc(sp_ready, 1)
                for n in range(CH):
                    b = n % 2
                    pool.wait_ge(c_coef, L * CH + n + 1)
                    for j, (lo, hi) in enumerate(((0, P), (P, 384))):
                        last = g_.tensor_scalar(prob[:, b, lo:hi], prob[:, b, lo:hi], stat[:, b, 2, j:j + 1], None,
                                                ALU.mult)
                    last.then_inc(c_prob, 1)
                for n in range(AH):
                    b = n % 2
                    pool.wait_ge(a_coef, L * AH + n + 1)
                    for c in range(2):
                        for j, (lo, hi) in enumerate(((0, P), (P, 384))):
                            p = aprob(c, b)[:, lo:hi]
                            last = g_.tensor_scalar(p, p, stat[:, b, 2, 2 * c + j:2 * c + j + 1], None, ALU.mult)
                    linked(last)
                    g_.tensor_tensor(aprob(0, b), aprob(0, b), aprob(1, b), ALU.add).then_inc(a_prob, 1)
                    u = n
                    taken(pool, L, f"bc{u}")
                    g_.tensor_tensor(mrg[:, 2 * u:2 * u + 2, :], mrg[:, 2 * u:2 * u + 2, :],
                                     pairs(part[:, u % 2, :]), ALU.add).then_inc(mrg_ready, 1)
                for u in range(4):
                    taken(pool, L, f"ba{u}")
                    g_.tensor_tensor(mrg[:, 2 * u:2 * u + 2, :], mrg[:, 2 * u:2 * u + 2, :],
                                     pairs(part[:, u % 2, :]), ALU.add).then_inc(mrg_ready, 1)
                for u in range(HID // W):
                    pool.wait_ge(hidh_ready, L * (HID // W) + u + 1)
                    c = slice(2 * u, 2 * u + 2)
                    g_.tensor_tensor(hidl[:, c, :], pairs(ft[:, u % 2, :]), hidh[:, c, :].bitcast(F32), ALU.subtract) \
                        .then_inc(hidl_ready, 1)


def second_weights(i, w_in, w_br_a, w_br_b, w_br_c, w_out, w_up, w_down, w_gate, w_proj):
    w = w_in[i]
    ik = np.zeros((D, W), np.float32)
    ik[:, 0:64] = ik[:, 64:128] = w[:, 4864:4928]
    out = weight_tiles(ik) + weight_tiles(w[:, 4608:4864])
    for at in (3584, 3072, 512, 0, 1536, 2048):
        out += weight_tiles(w[:, at:at + 512])
    for at in (4096, 1024, 2560):
        out += weight_tiles(w[:, at:at + 512])
    out += weight_tiles(w[:, 4932:8004])
    for b in (w_br_b, w_br_c, w_br_a):
        for c in range(2):
            out.append(chunked(b[i][:, c * 512:(c + 1) * 512]).reshape(P, TILE))
    out += weight_tiles(w_out[i]) + weight_tiles(w_up[i])
    out += weight_tiles(w_down[i]) + weight_tiles(w_gate[i])
    out.append(chunked(w_proj[i]).reshape(P, TILE))
    return np.stack(out)


def second_misc(i, w_in, gains, subln, a_lambda, g1, g2, g3):
    m = np.zeros((P, M2), np.float32)
    m[:, N_IW:N_IW + 32] = chunked(w_in[i][:, 4928:4932]).reshape(P, 32)
    for j, g in enumerate(gains):
        m[:, N_GAIN + j] = np.concatenate([g[i], g[i]])
    m[:, N_SUB] = subln[i]
    m[:, N_LAM:N_LAM + 256] = a_lambda[i].reshape(1, 256)
    for at, g in ((N_G1, g1), (N_G2, g2), (N_G3, g3)):
        m[:, at:at + KD] = g[i].reshape(KD, P).T
    init = 0.8 - 0.6 * math.exp(-0.3 * i)
    m[:, N_LINIT], m[:, N_LREST] = init, 1 - init
    return m


def second_constants():
    c = np.zeros((P, C2), np.float32)
    i = np.arange(P)
    c[:, E_ID:E_ID + P] = np.eye(P)
    c[:, E_ONE:E_ONE + P] = 1 / D
    same = (i[:, None] // 64 == i[None] // 64)
    c[:, E_G1:E_G1 + P], c[:, E_G64:E_G64 + P] = same / 64, same
    c[:, E_HEAD:E_HEAD + P] = 1 / P
    for m in range(P):
        if m % 64 < 32:
            c[m + 32, E_ROT + m] = -1
        else:
            c[m - 32, E_ROT + m] = 1
    c[:, E_TRI:E_TRI + P] = -(i[:, None] >= i[None]).astype(np.float32)
    c[:, E_NEG:E_NEG + P] = -1
    q, k = i[:, None], np.arange(T)[None]
    c[:, E_CH:E_CH + P] = np.where(k[:, :P] // 64 <= q // 64, 0, NEG)
    c[:, E_CH + P:E_CH + 384] = np.where(k // 64 <= (q + P) // 64, 0, NEG)
    kk, qq = i[:, None], np.arange(T)[None]
    strict = np.concatenate([kk < qq, (kk + P < qq)[:, P:]], 1)
    c[:, E_S01:E_S01 + 384] = strict
    c[:, E_SNEG:E_SNEG + 384] = np.where(strict, 0, NEG)
    inv = np.float32(10000.0) ** (-np.arange(0, 64, 2, dtype=np.float32) / 64)
    c[:, E_FREQ] = inv[i % 32]
    c[:, E_EPS], c[:, E_EPS64] = 1e-6, 64e-6
    return c


def program(nc, x, w1, m1, c1, onehot, onehot_rev, flip, rel, w2, m2, c2, pos, pt, out):
    with ExitStack() as outer:
        ring = outer.enter_context(nc.sbuf_tensor("ring", [P, RING, KD, W], F32))
        x_sb = outer.enter_context(nc.sbuf_tensor("x", [P, KD, T], F32))
        first_block(nc, outer, ring, x_sb, x, w1, m1, c1, onehot, onehot_rev, flip, rel)
        second_block(nc, outer, ring, x_sb, w2, m2, c2, pos, pt, out)


def kernel(**inputs):
    import concourse.bacc as bacc
    from concourse.bass_utils import run_bass_kernel_spmd

    a = {name: np.asarray(value) for name, value in inputs.items()}
    layers = range(LAYERS)
    first = [a[n] for n in ("w_in", "cmp_w1_k", "cmp_w1_v", "w_o_ret", "w_o_nsa", "w_out", "w_ffn_in", "w_ffn_out")]
    second = [a[n + "_2"] for n in ("w_in", "w_br_a", "w_br_b", "w_br_c", "w_out", "w_up", "w_down", "w_ple_gate",
                                    "w_ple_proj")]
    gains = [a[n + "_2"] for n in ("idx_k_norm", "c_k_norm", "c_q_norm", "a_k_norm", "a_q_norm")]
    arrays = {
        "x_t": chunked(np.ascontiguousarray(a["x"][0].T)),
        "w1": np.stack([first_weights(i, *first) for i in layers]),
        "m1": np.stack([first_misc(i, a["w_in"], a["cmp_pos_k"], a["cmp_pos_v"], a["cmp_w2_k"], a["cmp_w2_v"],
                                   a["norm_mix_g"], a["norm_ffn_g"]) for i in layers]),
        "c1": first_constants(a["norm_final_g"]),
        "onehot": distance_rows(np.arange(-255, 256)),
        "onehot_rev": distance_rows(255 - np.arange(384)),
        "flip": np.eye(P, dtype=np.float32)[::-1],
        "rel": a["rel_bias"],
        "w2": np.stack([second_weights(i, *second) for i in layers]),
        "m2": np.stack([second_misc(i, a["w_in_2"], gains, a["a_subln_2"], a["a_lambda_2"], a["attn_norm_2"],
                                    a["mlp_norm_2"], a["ple_norm_2"]) for i in layers]),
        "c2": second_constants(),
        "pos": np.broadcast_to(a["positions_2"].astype(np.int32), (P, T)),
        "p_t": np.stack([chunked(np.ascontiguousarray(a["p_2"][i, 0].T)) for i in layers]),
    }
    arrays = {f"in_{n}": np.ascontiguousarray(v) for n, v in arrays.items()}
    nc = bacc.Bacc("TRN2", target_bir_lowering=False, num_devices=1)
    args = [nc.dram_tensor(n, v.shape, I32 if v.dtype.kind == "i" else F32, kind="ExternalInput").ap()
            for n, v in arrays.items()]
    out = nc.dram_tensor("out_t", (P, KD, T), F32, kind="ExternalOutput").ap()
    program(nc, *args, out)
    r = run_bass_kernel_spmd(nc, [arrays], core_ids=[0])
    got = np.asarray(r.results[0]["out_t"])
    return np.ascontiguousarray(got.transpose(2, 1, 0)).reshape(1, T, D)
```

```python
from contextlib import ExitStack
import math

import numpy as np

import concourse.bass as bass
from concourse import mybir

F32 = mybir.dt.float32
F32R = mybir.dt.float32r
I32 = mybir.dt.int32
ALU = mybir.AluOpType
ACT = mybir.ActivationFunctionType
AX = mybir.AxisListType.X

P = 128
T = 256
D = 1024
KD = D // P
LAYERS = 2
W = 256
TILE = KD * W
RING = 5
SPLIT = 2
NEG = -1e30

RH, RK, RV = 4, 256, 512
NH, NG, HD = 16, 2, 64
NC = (T - 32) // 16 + 1
FF = 2816
KF = FF // P
ACCS = 3


class Plan:

    def __init__(self, banks, ring):
        self.banks, self.ring, self.names, self.tiles, self.count, self.before = banks, ring, [], {}, 0, {}

    def add(self, name, tiles=0):
        self.before[name] = len(self.names)
        self.names.append(name)
        self.tiles[name] = list(range(self.count, self.count + tiles))
        self.count += tiles

    def n(self, name):
        return self.before[name]

    def bank(self, name):
        return self.before[name] % self.banks

    def units_of_bank(self, b):
        return sum(n % self.banks == b for n in range(len(self.names)))

    def tiles_of_slot(self, s):
        return sum(t % self.ring == s for t in range(self.count))

    def last_user(self, t):
        return [u for u in self.names if t in self.tiles[u]][-1]

    def close(self, phases, plain=()):
        self.phase, self.split, self.parts = {}, [], []
        for n, (first, last) in enumerate(phases):
            units = [u for u in self.names[self.n(first):self.n(last) + 1] if not u.startswith(tuple(plain))]
            tiles = [t for u in units for t in self.tiles[u]]
            for i, t in enumerate(tiles):
                self.phase[t] = (n, i, tiles)
            self.split += tiles
            self.parts += [t for u in units for t in self.tiles[u][:-1]]
        return self


class Halves:

    def __init__(self, plan, ring, loaded, unit_done, sem):
        self.plan, self.ring, self.loaded, self.unit_done = plan, ring, loaded, unit_done
        self.high_done, self.low_done, self.part_done = sem("weights_high"), sem("weights_low"), sem("part_done")

    def place(self, high, low):
        self.high, self.low = high, low

    def left(self, eng, L, t):
        p = self.plan
        if t in p.parts:
            eng.wait_ge(self.part_done, L * len(p.parts) + p.parts.index(t) + 1)
        else:
            eng.wait_ge(self.unit_done, L * len(p.names) + p.n(p.last_user(t)) + 1)

    def raw_read(self, eng, L, t):
        eng.wait_ge(self.low_done, 2 * (L * len(self.plan.split) + self.plan.split.index(t) + 1))

    def rows(self, t):
        k = 6 if self.plan.last_user(t).startswith("fo") and t == self.plan.tiles[self.plan.last_user(t)][-1] else KD
        return ((0, 4), (4, k))

    def make_high(self, act, nc, L, ph, i):
        tiles = next(v[2] for v in self.plan.phase.values() if v[0] == ph)
        if i >= len(tiles):
            return
        t = tiles[i]
        if i >= SPLIT:
            self.left(act, L, tiles[i - SPLIT])
        s = t % RING
        act.wait_ge(self.loaded[s], 16 * (L * self.plan.tiles_of_slot(s) + t // RING + 1))
        for a, b in self.rows(t):
            nc.scalar.activation(self.high[ph][:, i % SPLIT, a:b, :], self.ring[:, s, a:b, :], ACT.Copy) \
                .then_inc(self.high_done, 1)

    def make_low(self, dve, nc, L, ph, i):
        tiles = next(v[2] for v in self.plan.phase.values() if v[0] == ph)
        if i >= len(tiles):
            return
        t = tiles[i]
        for n, (a, b) in enumerate(self.rows(t)):
            dve.wait_ge(self.high_done, 2 * (L * len(self.plan.split) + self.plan.split.index(t)) + n + 1)
            nc.vector.tensor_tensor(self.low[ph][:, i % SPLIT, a:b, :], self.ring[:, t % RING, a:b, :],
                                    self.high[ph][:, i % SPLIT, a:b, :].bitcast(F32), ALU.subtract) \
                .then_inc(self.low_done, 1)

    def wait_low(self, pe, L, t, n):
        pe.wait_ge(self.low_done, 2 * (L * len(self.plan.split) + self.plan.split.index(t)) + n + 1)

    def features(self, pe, nc, L, t, ps, operand, first=0, chunks=KD, ready=None):
        ph, i, _ = self.plan.phase[t]
        high, low = self.high[ph], self.low[ph]
        hi, lo = operand
        many = chunks > KD
        for j in range(2):
            for k in range(min(KD, chunks - first)):
                if j == 0 and k % 4 == 0:
                    self.wait_low(pe, L, t, k // 4)
                c = first + k
                if j == 0 and ready and k % 2 == 0:
                    pe.wait_ge(ready[0], ready[1] + c // 2 + 1)
                wh, wl = (w[:, i % SPLIT, k, j * P:(j + 1) * P] for w in (high, low))
                nc.tensor.matmul(ps[:, j, :], wh, hi[:, c, :], start=(c == 0 and (j == 0 or not many)), stop=False)
                nc.tensor.matmul(ps[:, j, :], wh, lo[:, c, :], start=False, stop=False)
                last = nc.tensor.matmul(ps[:, j, :], wl, hi[:, c, :], start=False,
                                        stop=(c == chunks - 1 and (j == 1 or not many)))
        return last

    def tokens(self, pe, nc, L, t, ps, operand):
        ph, i, _ = self.plan.phase[t]
        wh, wl = (w[:, i % SPLIT] for w in (self.high[ph], self.low[ph]))
        hi, lo = operand
        for j in range(2):
            for k in range(KD):
                if j == 0 and k % 4 == 0:
                    self.wait_low(pe, L, t, k // 4)
                q = slice(j * P, (j + 1) * P)
                nc.tensor.matmul(ps[:, j, :], hi[:, k, q], wh[:, k, :], start=(k == 0), stop=False)
                nc.tensor.matmul(ps[:, j, :], lo[:, k, q], wh[:, k, :], start=False, stop=False)
                last = nc.tensor.matmul(ps[:, j, :], hi[:, k, q], wl[:, k, :], start=False, stop=(k == KD - 1))
        return last


def overlay(nc, *tensors):
    guards = [nc.sbuf_tensor(*t) for t in tensors]
    found = [g.__enter__() for g in guards]
    for g in reversed(guards):
        g.__exit__(None, None, None)
    return found


def first_plan():
    p = Plan(ACCS, RING)
    for name, tiles in [("norm1", 0), ("gate", 0), ("rawk", 1), ("rawv", 1), ("qr0", 1), ("qr1", 1), ("gate_t", 0),
                        ("qr2", 1), ("qr3", 1)] + [
            (f"kr{u}", 1) for u in range(RH)] + [
            ("hidk", 2), ("hidv", 2), ("vr0", 1), ("vr1", 1), ("cmp", 0)] + [(f"vr{u}", 1) for u in range(2, 8)] + [
            ("S0", 0), ("S1", 0), ("S2", 0), ("S3", 0), ("keys", 1), ("O0.0", 0), ("O0.1", 0), ("vals", 1),
            ("O1.0", 0), ("O1.1", 0), ("mean0", 0), ("qn0", 1), ("O2.0", 0), ("O2.1", 0), ("mean1", 0), ("var0", 0),
            ("qn1", 1), ("O3.0", 0), ("O3.1", 0), ("mean2", 0), ("var1", 0), ("qn2", 1), ("mean3", 0), ("var2", 0),
            ("qn3", 1), ("var3", 0)] + [(f"side{u}", 1) for u in range(NH)] + [(f"wr{u}", 2) for u in range(4)] + [
            (f"wn{u}", 1) for u in range(4)]:
        p.add(name, tiles)
    for u in range(4):
        p.add(f"wo{u}", 1)
    for u in range(FF // W):
        p.add(f"fa{u}", 1)
        if u == 0:
            p.add("norm2")
        p.add(f"fb{u}", 1)
    for u in range(4):
        p.add(f"fo{u}", 3)
    return p.close((("rawk", "qn3"), ("side0", "fo3")), plain=("hid", "wr"))


M_GATE, M_W2K, M_W2V, M_POSK, M_POSV, M_G1, M_G2 = 0, 384, 512, 640, 656, 672, 680
M1 = 688
C_ONE, C_EPS, C_EPS4, C_ROW, C_GF, C_COS, C_SIN, C_ID, C_MEAN, C_VAR, C_DT = \
    0, 128, 129, 130, 131, 139, 651, 1163, 1291, 1419, 1547
C_FIRST = C_COS
C1 = 3083


def first_block(nc, outer, ring, x, x_in, w1, m1, c1, onehot, onehot_rev, flip_in, rel):
    plan = first_plan()
    UNITS = len(plan.names)
    with ExitStack() as ctx:
        def sb(name, shape):
            return ctx.enter_context(nc.sbuf_tensor(name, shape, F32))

        def sem(name):
            return outer.enter_context(nc.semaphore(name))

        _, high_p, low_p = overlay(nc, ("before_p", [P, (KF + 32) * T], F32), ("high_p", [P, SPLIT, KD, W], F32R),
                                   ("low_p", [P, SPLIT, KD, W], F32R))
        high_f, low_f, ffh, ffl = overlay(
            nc, ("high_f", [P, SPLIT, KD, W], F32R), ("low_f", [P, SPLIT, KD, W], F32R), ("ffh", [P, KF, T], F32R),
            ("ffl", [P, KF, T], F32R))
        qk = sb("qk", [P, KF, T])
        qr = qk[:, 0:8, :]
        kr = qk[:, 8:16, :]
        sT = qk[:, 16:22, :].rearrange("p c t -> p (c t)").rearrange("p (h n) -> p h n", h=RH)
        vr = sb("vr", [P, 2, RH * RV])
        dev = sb("dev", [P, 16, T])
        raw = dev[:, 0:4, :].rearrange("p (s g) t -> p s g t", s=2)
        wins = dev[:, 4:8, :].rearrange("p a b -> p (a b)")[:, 0:2 * NG * NC * 16] \
            .rearrange("p (s g n a) -> p s g n a", s=2, g=NG, n=NC)
        tha = sb("tha", [P, KD, T])
        thb = sb("thb", [P, KD, T])
        on = sb("on", [P, KD, T])
        work_b = sb("work_b", [P, 2048])
        work = sb("work", [P, 2048])
        qn = sb("qn", [P, KD, T])
        mix = qn
        ah, al = (ctx.enter_context(nc.sbuf_tensor(n, [P, KD, T], F32R)) for n in ("ah", "al"))
        ks = sb("ks", [P, 2, T])
        vs = sb("vs", [P, 2, W])
        hid = sb("hid", [P, 2, 2, NG * NC])
        kc = sb("kc", [P, 16])
        vc = sb("vc", [P, P])
        bias = sb("bias", [P, NH, T])
        cbias = sb("cbias", [P, NH, 2, 16])
        gates = sb("gates", [P, 2, 48])
        prob = work[:, 0:1600].rearrange("p (b n) -> p b n", b=2)
        probT = work_b[:, :].rearrange("p (b n) -> p b n", b=2)
        sq = htmp = work[:, :].rearrange("p (c t) -> p c t", c=KD)
        sqh = work[:, :].rearrange("p (b c t) -> p b c t", b=2, c=4)
        rot = work[:, :].rearrange("p (b k n) -> p b k n", b=2, k=2)
        ft = work[:, 0:1024].rearrange("p (b n) -> p b n", b=2)
        part = tf = work_b[:, 0:1024].rearrange("p (b n) -> p b n", b=2)
        th = thb[:, 0:4, :].rearrange("p (b c) t -> p b (c t)", b=2)
        gt = tha[:, 0:4, :].rearrange("p (b c) t -> p b (c t)", b=2)
        rstd = sb("rstd", [P, 2, T])
        early = sb("early", [P, 1])
        stat = sb("stat", [P, 2, 4, 6])
        misc = sb("misc", [P, M1])
        con = sb("con", [P, C1])
        tab = sb("tab", [33, NH])
        setup = dev[:, 8:16, :].rearrange("p a b -> p (a b)")
        oh, ohr, rowb = setup[0:33, 0:511], setup[0:33, 512:896], setup[0:NH, 1024:1408]
        flip = setup[:, 1408:1408 + P]
        biasr = vr[:, :, :].rearrange("p a b -> p (a b)")
        row_dram = nc.dram_tensor("row_bias", [NH, 384], F32)

        acc = [ctx.enter_context(nc.psum_tensor(f"acc{b}", [P, 2, T], F32)) for b in range(ACCS)]
        lga = ctx.enter_context(nc.psum_tensor("lga", [P, 512], F32))
        lgb = ctx.enter_context(nc.psum_tensor("lgb", [P, 512], F32))
        tra = ctx.enter_context(nc.psum_tensor("tra", [P, 512], F32))
        trb = ctx.enter_context(nc.psum_tensor("trb", [P, 512], F32))
        avo = ctx.enter_context(nc.psum_tensor("avo", [P, 512], F32))

        flip_banks = (trb, avo, lga, lgb, tra)
        ident = con[:, C_ID:C_ID + P]
        m_one = con[:, C_ONE:C_ONE + P]
        m_mean = con[:, C_MEAN:C_MEAN + P]
        m_var = con[:, C_VAR:C_VAR + P]
        cosq = con[:, C_COS:C_COS + 512]
        sinq = con[:, C_SIN:C_SIN + 512]
        decay = con[:, C_DT:C_DT + RH * 384].rearrange("p (h n) -> p h n", h=RH)

        loaded = [sem(f"tile_loaded{s}") for s in range(RING)]
        tables_in = sem("tables_loaded")
        misc_in, con_in, x_in_s, set_up_in = (sem(n) for n in ("misc_loaded", "con_loaded", "x_loaded", "set_up_loaded"))
        row_out, bias_in, flipped, bias_set = sem("row_stored"), sem("bias_loaded"), sem("flipped"), sem("bias_set")
        tab_set, row_made, row_copied, cb_made, cb_copied = (sem(n) for n in (
            "tab_set", "row_made", "row_copied", "cb_made", "cb_copied"))
        unit_done = sem("unit_done")
        bank_read = [sem(f"bank_read{b}") for b in range(ACCS)]
        squares, h_ready, x_final = sem("squares"), sem("h_ready"), sem("x_final")
        rstd_ready, final_root = sem("rstd_ready"), sem("final_root")
        rot_added, wins_ready, gates_set = sem("rot_added"), sem("wins_ready"), sem("gates_set")
        lg_done, lg_read, max_ready, exp_done, coef_ready, prob_ready, tr_done, pta, ptb, av_done, on_ready = (
            sem(n) for n in ("logits_done", "logits_read", "max_ready", "exp_done", "coef_ready", "prob_ready",
                             "transposed", "probT_a", "probT_b", "values_done", "on_ready"))
        halves = Halves(plan, ring, loaded, unit_done, sem)
        halves.place([high_p, high_f], [low_p, low_f])
        silu_done, ff_made = sem("silu_done"), sem("ff_made")
        high_a, low_a, ffh_ready, ffl_ready = (sem(n) for n in (
            "operand_high", "operand_low", "ff_high", "ff_low"))
        tanh_g, dsq_ready, normed, y_ready, mix_ready = (sem(n) for n in (
            "tanh_g", "dsq_ready", "heads_normed", "y_ready", "mix_ready"))
        link = {e: sem(f"{e}_link") for e in ("dve", "act", "pool")}

        def unit(name):
            return acc[plan.bank(name)]

        def done(eng, L, name):
            eng.wait_ge(unit_done, L * UNITS + plan.n(name) + 1)

        def raw_read(eng, L, t):
            if t in plan.split:
                halves.raw_read(eng, L, t)
            else:
                done(eng, L, plan.last_user(t))

        def read(name):
            return bank_read[plan.bank(name)]

        def taken(eng, L, name):
            b = plan.bank(name)
            eng.wait_ge(bank_read[b], L * plan.units_of_bank(b) + plan.n(name) // ACCS + 1)

        block = ctx.enter_context(nc.Block())

        @block.sync
        def _(sp):
            sp.dma_start(x[:], x_in).then_inc(x_in_s, 16)
            sp.dma_start(con[:, 0:C_FIRST], c1[:, 0:C_FIRST]).then_inc(con_in, 16)
            for L in range(LAYERS):
                if L:
                    sp.wait_ge(low_a, L * 16)
                sp.dma_start(misc[:], m1[L]).then_inc(misc_in, 16)
                for name in plan.names:
                    for j, t in enumerate(plan.tiles[name]):
                        s = t % RING
                        if t >= RING:
                            raw_read(sp, L, t - RING)
                        elif L:
                            raw_read(sp, L - 1, max(v for v in range(plan.count) if v % RING == s))
                        k = 6 if name.startswith("fo") and j == 2 else KD
                        sp.dma_start(ring[:, s, 0:k, :].rearrange("p k n -> p (k n)"), w1[L, t, :, 0:k * W]) \
                            .then_inc(loaded[s], 16)
                        if L == 0 and t == 1:
                            sp.dma_start(con[:, C_FIRST:], c1[:, C_FIRST:]).then_inc(tables_in, 16)
                        if L == 0 and t == RING - 1:
                            sp.dma_start(tab[0:32, :], rel).then_inc(set_up_in, 16)
                            sp.dma_start(oh, onehot).then_inc(set_up_in, 16)
                            sp.dma_start(ohr, onehot_rev).then_inc(set_up_in, 16)
                            sp.dma_start(flip, flip_in).then_inc(set_up_in, 16)
                        if L == 0 and t == RING + 1:
                            sp.wait_ge(row_copied, 1)
                            sp.dma_start(row_dram[:, :], rowb).then_inc(row_out, 16)
                            sp.wait_ge(row_out, 16)
                            sp.dma_start(biasr.rearrange("p (h n) -> p h n", h=NH),
                                         bass.AP(tensor=row_dram, offset=0, ap=[[1, P], [384, NH], [1, T]])) \
                                .then_inc(bias_in, 16)
        @block.tensor
        def _(pe):
            mm = nc.tensor.matmul

            def begin(L, name):
                b, n = plan.bank(name), plan.n(name)
                before = L * plan.units_of_bank(b) + n // ACCS
                if before:
                    pe.wait_ge(bank_read[b], before)
                return acc[b]

            def tile(L, t):
                s = t % RING
                pe.wait_ge(loaded[s], 16 * (L * plan.tiles_of_slot(s) + t // RING + 1))
                return ring[:, s]

            def features(L, name, src, chunks=KD):
                ps = begin(L, name)
                ws = [tile(L, t) for t in plan.tiles[name]]
                for j in range(2):
                    for k in range(chunks):
                        last = mm(ps[:, j, :], ws[k // KD][:, k % KD, j * P:(j + 1) * P], src[:, k, :],
                                  start=(k == 0), stop=(k == chunks - 1))
                last.then_inc(unit_done, 1)

            def split_features(L, name, operand, chunks=KD, ready=None):
                ps = begin(L, name)
                tiles = plan.tiles[name]
                for i, t in enumerate(tiles):
                    last = halves.features(pe, nc, L, t, ps, operand, i * KD, chunks, ready)
                    last.then_inc(unit_done if t == tiles[-1] else halves.part_done, 1)

            def split_tokens(L, name):
                ps = begin(L, name)
                halves.tokens(pe, nc, L, plan.tiles[name][0], ps, (ah, al)).then_inc(unit_done, 1)

            def few_features(L, name, w, n, before):
                ps = begin(L, name)
                for k in range(KD):
                    pe.wait_ge(h_ready, before + k + 1)
                    last = mm(ps[0:n, 0, :], w[:, n * k:n * (k + 1)], htmp[:, k, :], start=(k == 0), stop=(k == KD - 1))
                last.then_inc(unit_done, 1)

            def turned(L, name, src, of, n):
                ps = begin(L, name)
                taken(pe, L, of)
                for j in range(2):
                    last = nc.tensor.transpose(ps[:, j, 0:n], src[0:n, j * P:(j + 1) * P], ident[0:n, 0:n])
                last.then_inc(unit_done, 1)

            def norm(L, name, base):
                ps = begin(L, name)
                for k in range(KD):
                    if k % 2 == 0:
                        pe.wait_ge(squares, base + k // 2 + 1)
                    last = mm(ps[:, 0, :], m_one, sq[:, k, :], start=(k == 0), stop=(k == KD - 1))
                last.then_inc(unit_done, 1)

            def set_up():
                pe.wait_ge(set_up_in, 64)
                pe.wait_ge(tab_set, 1)
                for qt in range(2):
                    for n in range(NC):
                        o = 255 + P * qt - 16 * n - 31
                        last = mm((lga, lgb)[qt][:, n * NH:(n + 1) * NH], oh[:, o:o + P], tab[:, :],
                                  start=True, stop=True)
                last.then_inc(cb_made, 1)
                mm(tra[0:NH, 0:384], tab[:, :], ohr, start=True, stop=True).then_inc(row_made, 1)

            pe.wait_ge(con_in, 16)
            for L in range(LAYERS):
                norm(L, "norm1", L * 8)
                pe.wait_ge(misc_in, 16 * (L + 1))
                few_features(L, "gate", misc[:, M_GATE:M_GATE + 384], 48, L * 8)
                split_features(L, "rawk", (ah, al), ready=(low_a, L * 16))
                split_features(L, "rawv", (ah, al))
                split_features(L, "qr0", (ah, al))
                split_features(L, "qr1", (ah, al))
                if L == 0:
                    pe.wait_ge(tables_in, 16)
                turned(L, "gate_t", qn[:, 0, :], "gate", 48)
                if L == 0:
                    set_up()
                split_features(L, "qr2", (ah, al))
                split_features(L, "qr3", (ah, al))
                for u in range(RH):
                    split_features(L, f"kr{u}", (ah, al))
                if L == 0:
                    pe.wait_ge(bias_in, 16)
                    pe.wait_ge(cb_copied, 2)
                    pe.wait_ge(row_copied, 1)
                    for i in range(8):
                        if i >= len(flip_banks):
                            pe.wait_ge(bias_set, i - len(flip_banks) + 1)
                        mm(flip_banks[i % len(flip_banks)][:, :], flip, biasr[:, i * 512:(i + 1) * 512],
                           start=True, stop=True).then_inc(flipped, 1)
                pe.wait_ge(misc_in, 16 * (L + 1))
                for s, name in enumerate(("hidk", "hidv")):
                    ps = begin(L, name)
                    ws = [tile(L, t) for t in plan.tiles[name]]
                    pe.wait_ge(wins_ready, L * 2 + s + 1)
                    rhs = wins[:, s].rearrange("p g n a -> p (g n) a")
                    for j in range(2):
                        for a in range(16):
                            last = mm(ps[:, j, 0:NG * NC], ws[a // KD][:, a % KD, j * P:(j + 1) * P], rhs[:, :, a],
                                      start=(a == 0), stop=(a == 15))
                    last.then_inc(unit_done, 1)
                split_tokens(L, "vr0")
                split_tokens(L, "vr1")
                ps = begin(L, "cmp")
                taken(pe, L, "hidk")
                taken(pe, L, "hidv")
                for g in range(NG):
                    for j in range(2):
                        mm(ps[g * 64:(g + 1) * 64, 0, 0:NC], misc[:, M_W2K + j * 64:M_W2K + (j + 1) * 64],
                           hid[:, 0, j, g * NC:(g + 1) * NC], start=(j == 0), stop=(j == 1))
                for g in range(NG):
                    for j in range(2):
                        last = mm(ps[0:NC, 1, g * 64:(g + 1) * 64], hid[:, 1, j, g * NC:(g + 1) * NC],
                                  misc[:, M_W2V + j * 64:M_W2V + (j + 1) * 64], start=(j == 0), stop=(j == 1))
                last.then_inc(unit_done, 1)
                for u in range(2, 8):
                    split_tokens(L, f"vr{u}")
                pe.wait_ge(tables_in, 16)
                pe.wait_ge(rot_added, L * 8 + 8)
                for u in range(RH):
                    ps = begin(L, f"S{u}").rearrange("p a b -> p (a b)")
                    for k in range(2):
                        mm(ps[:, 0:T], kr[:, 2 * u + k, 0:P], qr[:, 2 * u + k, :], start=(k == 0), stop=(k == 1))
                    for k in range(2):
                        last = mm(ps[:, T:T + P], kr[:, 2 * u + k, P:T], qr[:, 2 * u + k, P:T],
                                  start=(k == 0), stop=(k == 1))
                    last.then_inc(unit_done, 1)

                def heads_out(u, e2):
                    ps = begin(L, f"O{u}.{e2}")
                    taken(pe, L, f"S{u}")
                    for j in range(2):
                        at = u * RV + (2 * e2 + j) * P
                        mm(ps[:, j, :], vr[:, 0, at:at + P], sT[:, u, 0:T], start=True, stop=False)
                        last = mm(ps[:, j, P:T], vr[:, 1, at:at + P], sT[:, u, T:T + P], start=False, stop=True)
                    last.then_inc(unit_done, 1)

                def mean(u):
                    ps = begin(L, f"mean{u}")
                    taken(pe, L, f"O{u}.1")
                    for e in range(4):
                        last = mm(ps[:, 0, :], m_mean, dev[:, 4 * u + e, :], start=(e == 0), stop=(e == 3))
                    last.then_inc(unit_done, 1)

                def var(u):
                    ps = begin(L, f"var{u}")
                    pe.wait_ge(dsq_ready, L * RH + u + 1)
                    for e in range(4):
                        last = mm(ps[:, 0, :], m_var, sqh[:, u % 2, e, :], start=(e == 0), stop=(e == 3))
                    last.then_inc(unit_done, 1)

                split_features(L, "keys", (ah, al))
                heads_out(0, 0)
                heads_out(0, 1)
                split_tokens(L, "vals")
                heads_out(1, 0)
                heads_out(1, 1)
                mean(0)
                split_features(L, "qn0", (ah, al))
                heads_out(2, 0)
                heads_out(2, 1)
                mean(1)
                var(0)
                split_features(L, "qn1", (ah, al))
                heads_out(3, 0)
                heads_out(3, 1)
                mean(2)
                var(1)
                split_features(L, "qn2", (ah, al))
                mean(3)
                var(2)
                split_features(L, "qn3", (ah, al))
                var(3)
                taken(pe, L, "qn3")
                if L == 0:
                    pe.wait_ge(bias_set, 8)
                for n in range(NH + 2):
                    if n < NH:
                        c, g = n // 2, n % 2
                        q = qn[g * 64:(g + 1) * 64, c, :]
                        k = ks[g * 64:(g + 1) * 64]
                        if L * NH + n:
                            pe.wait_ge(lg_read, L * NH + n)
                        mm(lga[:, 0:T], q[:, P:T], k[:, 0, :], start=True, stop=True)
                        mm(lga[:, T:2 * T], q[:, P:T], k[:, 1, :], start=True, stop=True)
                        mm(lgb[:, 0:P], q[:, 0:P], k[:, 0, 0:P], start=True, stop=True)
                        mm(lgb[:, P:2 * P], q[:, 0:P], k[:, 1, 0:P], start=True, stop=True)
                        mm(lgb[:, 256:256 + NC], q[:, 0:P], kc[g * 64:(g + 1) * 64, 0:NC], start=True, stop=True)
                        mm(lgb[:, 272:272 + NC], q[:, P:T], kc[g * 64:(g + 1) * 64, 0:NC], start=True, stop=True) \
                            .then_inc(lg_done, 1)
                        split_features(L, f"side{n}", (ah, al))
                    if n == NH:
                        pe.wait_ge(y_ready, L * 8 + 8)
                    if n >= NH:
                        features(L, f"wr{n - NH}", dev, 16)
                    if 1 <= n <= NH:
                        b = (n - 1) % 2
                        pe.wait_ge(prob_ready, L * NH + n)
                        if L * NH + n - 1:
                            pe.wait_ge(pta, L * NH + n - 1)
                            pe.wait_ge(ptb, L * NH + n - 1)
                        tr = nc.tensor.transpose
                        tr(tra[:, 0:P], prob[:, b, 512:640], ident)
                        tr(tra[:, P:2 * P], prob[:, b, 0:P], ident)
                        tr(tra[:, 2 * P:3 * P], prob[:, b, 640:768], ident)
                        tr(tra[:, 3 * P:4 * P], prob[:, b, 256:384], ident)
                        tr(trb[:, 0:P], prob[:, b, P:2 * P], ident)
                        tr(trb[:, P:2 * P], prob[:, b, 384:512], ident)
                        tr(trb[0:NC, 2 * P:3 * P], prob[:, b, 768:768 + NC], ident)
                        tr(trb[0:NC, 3 * P:4 * P], prob[:, b, 784:784 + NC], ident).then_inc(tr_done, 1)
                    if n >= 2:
                        m = n - 2
                        b, g = m % 2, m % 2
                        pe.wait_ge(pta, L * NH + m + 1)
                        pe.wait_ge(ptb, L * NH + m + 1)
                        if g == 0 and L * 8 + m // 2:
                            pe.wait_ge(on_ready, L * 8 + m // 2)
                        o = avo[g * 64:(g + 1) * 64, 0:T]
                        mm(o, vs[:, 0, g * 64:(g + 1) * 64], probT[:, b, 0:T], start=True, stop=False)
                        mm(o, vs[:, 0, P + g * 64:P + (g + 1) * 64], probT[:, b, T:2 * T], start=False, stop=False)
                        mm(o[:, P:T], vs[:, 1, g * 64:(g + 1) * 64], probT[:, b, 512:640], start=False, stop=False)
                        mm(o[:, P:T], vs[:, 1, P + g * 64:P + (g + 1) * 64], probT[:, b, 640:768],
                           start=False, stop=False)
                        mm(o, vc[0:NC, g * 64:(g + 1) * 64], probT[0:NC, b, 768:1024], start=False, stop=True) \
                            .then_inc(av_done, 1)
                features(L, "wr2", dev, 16)
                features(L, "wr3", dev, 16)
                for u in range(4):
                    split_features(L, f"wn{u}", (ah, al), ready=None if u else (low_a, L * 16 + 4))
                for u in range(4):
                    split_features(L, f"wo{u}", (ah, al), ready=None if u else (low_a, L * 16 + 8))
                for u in range(FF // W):
                    split_features(L, f"fa{u}", (ah, al), ready=None if u else (low_a, L * 16 + 12))
                    if u == 0:
                        norm(L, "norm2", L * 8 + 4)
                    split_features(L, f"fb{u}", (ah, al))
                for u in range(4):
                    split_features(L, f"fo{u}", (ffh, ffl), KF, ready=None if u else (ffl_ready, L * (FF // W)))
            pe.wait_ge(bank_read[0], LAYERS * plan.units_of_bank(0))
            for k in range(KD):
                pe.wait_ge(squares, LAYERS * 8 + k // 2 + 1)
                last = mm(acc[0][:, 0, :], m_one, sq[:, k, :], start=(k == 0), stop=(k == KD - 1))
            last.then_inc(unit_done, 1)

        @block.scalar
        def _(act):
            op = nc.scalar.activation

            def squares_of():
                for p in range(4):
                    yield p
                    op(sq[:, 2 * p:2 * p + 2, :], x[:, 2 * p:2 * p + 2, :], ACT.Square).then_inc(squares, 1)

            def root(name, L):
                op(early[:, :], con[:, C_EPS:C_EPS + 1], ACT.Sqrt)
                done(act, L, name)
                op(rstd[:, 0, :], unit(name)[:, 0, :], ACT.Sqrt, bias=con[:, C_EPS:C_EPS + 1]).then_inc(read(name), 1)

            def set_up():
                act.wait_ge(cb_made, 1)
                for qt in range(2):
                    src = (lga, lgb)[qt][:, 0:NC * NH].rearrange("p (n h) -> p h n", n=NC)
                    op(cbias[:, :, qt, 0:NC], src, ACT.Copy).then_inc(cb_copied, 1)
                act.wait_ge(row_made, 1)
                op(rowb, tra[0:NH, 0:384], ACT.Copy).then_inc(row_copied, 1)

            act.wait_ge(con_in, 16)
            act.wait_ge(x_in_s, 16)
            for L in range(LAYERS):
                def take_heads(u):
                    for e2 in range(2):
                        done(act, L, f"O{u}.{e2}")
                        op(dev[:, 4 * u + 2 * e2:4 * u + 2 * e2 + 2, :], unit(f"O{u}.{e2}")[:], ACT.Copy) \
                            .then_inc(read(f"O{u}.{e2}"), 1)

                def square_devs(u):
                    taken(act, L, f"mean{u}")
                    op(sqh[:, u % 2], dev[:, 4 * u:4 * u + 4, :], ACT.Square).then_inc(dsq_ready, 1)

                def head_root(u):
                    done(act, L, f"var{u}")
                    if u >= 2:
                        act.wait_ge(normed, L * RH + u - 1)
                    op(rstd[:, u % 2, :], unit(f"var{u}")[:, 0, :], ACT.Sqrt, bias=con[:, C_EPS4:C_EPS4 + 1]) \
                        .then_inc(read(f"var{u}"), 1)

                def take_query(u):
                    done(act, L, f"qn{u}")
                    op(qn[:, 2 * u:2 * u + 2, :], unit(f"qn{u}")[:], ACT.Copy, scale=HD ** -0.5) \
                        .then_inc(read(f"qn{u}"), 1)
                    halves.make_high(act, nc, L, 0, 22 + u)

                def scaled_high(p):
                    for c in (2 * p, 2 * p + 1):
                        last = op(ah[:, c, :], x[:, c, :], ACT.Copy, scale=misc[:, M_G2 + c:M_G2 + c + 1])
                    last.then_inc(high_a, 1)

                def high_halves(src, p):
                    op(ah[:, 2 * p:2 * p + 2, :], src[:, 2 * p:2 * p + 2, :], ACT.Copy).then_inc(high_a, 1)

                for p in squares_of():
                    if L:
                        taken(act, L - 1, f"fo{p}")
                root("norm1", L)
                halves.make_high(act, nc, L, 0, 0)
                for p in range(4):
                    act.wait_ge(h_ready, L * 8 + 2 * p + 2)
                    high_halves(htmp, p)
                halves.make_high(act, nc, L, 0, 1)
                done(act, L, "gate")
                op(qn[0:48, 0, :], unit("gate")[0:48, 0, :], ACT.Copy).then_inc(read("gate"), 1)
                for i in range(2, 12):
                    halves.make_high(act, nc, L, 0, i)
                    if i == 5:
                        done(act, L, "gate_t")
                        op(gates[:], unit("gate_t")[:, :, 0:48], ACT.Tanh, scale=0.5).then_inc(read("gate_t"), 1)
                    if L == 0 and i == 5:
                        set_up()
                for s, name in enumerate(("hidk", "hidv")):
                    done(act, L, name)
                    op(hid[:, s], unit(name)[:, :, 0:NG * NC], ACT.Gelu_apprx_tanh).then_inc(read(name), 1)
                for u in range(8):
                    done(act, L, f"vr{u}")
                    op(vr[:, :, u * W:(u + 1) * W], unit(f"vr{u}")[:], ACT.Copy).then_inc(read(f"vr{u}"), 1)
                    halves.make_high(act, nc, L, 0, 12 + u)
                    if u == 1:
                        done(act, L, "cmp")
                        op(kc[:, 0:NC], unit("cmp")[:, 0, 0:NC], ACT.Copy)
                        op(vc[0:NC, :], unit("cmp")[0:NC, 1, 0:P], ACT.Copy).then_inc(read("cmp"), 1)
                done(act, L, "keys")
                op(ks[:], unit("keys")[:], ACT.Copy).then_inc(read("keys"), 1)
                halves.make_high(act, nc, L, 0, 20)
                take_heads(0)
                done(act, L, "vals")
                op(vs[:], unit("vals")[:], ACT.Copy).then_inc(read("vals"), 1)
                halves.make_high(act, nc, L, 0, 21)
                take_heads(1)
                square_devs(0)
                take_query(0)
                take_heads(2)
                head_root(0)
                square_devs(1)
                take_query(1)
                take_heads(3)
                head_root(1)
                square_devs(2)
                take_query(2)
                head_root(2)
                square_devs(3)
                take_query(3)
                head_root(3)
                for i in range(SPLIT):
                    halves.make_high(act, nc, L, 1, i)
                for n in range(NH + 2):
                    if n < NH:
                        b = n % 2
                        act.wait_ge(max_ready, L * NH + n + 1)
                        for j, (at, w) in enumerate(((768, NC), (784, NC), (512, P), (0, T), (640, P), (256, T))):
                            last = op(prob[:, b, at:at + w], prob[:, b, at:at + w], ACT.Exp,
                                      bias=stat[:, b, 0, j:j + 1], accum_out=stat[:, b, 1, j:j + 1])
                        last.then_inc(exp_done, 1)
                        name = f"side{n}"
                        done(act, L, name)
                        if n < 8:
                            if n >= 2:
                                taken(act, L, f"side{n - 2}")
                            op(th[:, b, :], unit(name)[:], ACT.Tanh, scale=0.5).then_inc(tanh_g, 1)
                        else:
                            m = (n - 8) % 4
                            if n == 8:
                                act.wait_ge(y_ready, L * 8 + 8)
                            op((tha if n < 12 else thb)[:, 2 * m:2 * m + 2, :], unit(name)[:], ACT.Tanh, scale=0.5) \
                                .then_inc(read(name), 1)
                        if n < NH - SPLIT:
                            halves.make_high(act, nc, L, 1, n + SPLIT)
                    if 1 <= n <= NH:
                        m, b = n - 1, (n - 1) % 2
                        act.wait_ge(tr_done, L * NH + m + 1)
                        if L * NH + m >= 2:
                            act.wait_ge(av_done, L * NH + m - 1)
                        op(probT[:, b, 0:512], tra[:, :], ACT.Copy).then_inc(pta, 1)
                    if n >= 2 and n % 2 == 1:
                        act.wait_ge(av_done, L * NH + n - 1)
                        op(on[:, (n - 2) // 2, :], avo[:, 0:T], ACT.Copy).then_inc(on_ready, 1)

                for p in range(4):
                    act.wait_ge(on_ready, L * 8 + 2 * p + 2)
                    high_halves(on, p)
                for u in range(3 + SPLIT):
                    halves.make_high(act, nc, L, 1, 16 + u)
                done(act, L, "wn3")
                for p in range(4):
                    act.wait_ge(mix_ready, L * 4 + p + 1)
                    high_halves(mix, p)
                halves.make_high(act, nc, L, 1, 19 + SPLIT)
                for p in squares_of():
                    if p:
                        halves.make_high(act, nc, L, 1, 19 + p + SPLIT)
                    if p == 3:
                        done(act, L, "wo3")
                        for q in range(3):
                            scaled_high(q)
                    taken(act, L, f"wo{p}")
                scaled_high(3)
                halves.make_high(act, nc, L, 1, 23 + SPLIT)
                root("norm2", L)

                def ff_high(u):
                    act.wait_ge(ff_made, L * (FF // W) + u + 1)
                    op(ffh[:, 2 * u:2 * u + 2, :], ft[:, u % 2, :].rearrange("p (a t) -> p a t", a=2), ACT.Copy) \
                        .then_inc(ffh_ready, 1)

                for u in range(FF // W):
                    halves.make_high(act, nc, L, 1, 24 + 2 * u + SPLIT)
                    taken(act, L, f"fa{u}")
                    op(tf[:, u % 2, :], tf[:, u % 2, :], ACT.Silu).then_inc(silu_done, 1)
                    if u:
                        ff_high(u - 1)
                    halves.make_high(act, nc, L, 1, 25 + 2 * u + SPLIT)
                ff_high(FF // W - 1)
                for i in range(12):
                    halves.make_high(act, nc, L, 1, 24 + 2 * (FF // W) + i + SPLIT)
            for p in squares_of():
                taken(act, LAYERS - 1, f"fo{p}")
            act.wait_ge(unit_done, LAYERS * UNITS + 1)
            op(rstd[:, 0, :], acc[0][:, 0, :], ACT.Sqrt, bias=con[:, C_EPS:C_EPS + 1]).then_inc(final_root, 1)

        @block.vector
        def _(dve):
            v = nc.vector
            links = [0]

            def linked(ins):
                links[0] += 1
                ins.then_inc(link["dve"], 1)
                dve.wait_ge(link["dve"], links[0])

            def norm(L, name, gain, h):
                taken(dve, L, name)
                linked(v.reciprocal(rstd[:, 0, :], rstd[:, 0, :]))
                for k in range(KD):
                    v.scalar_tensor_tensor(out=h[:, k, :], in0=x[:, k, :], scalar=misc[:, gain + k:gain + k + 1],
                                           in1=rstd[:, 0, :], op0=ALU.mult, op1=ALU.mult).then_inc(h_ready, 1)

            dve.wait_ge(con_in, 16)
            for L in range(LAYERS):
                def deviations(u):
                    done(dve, L, f"mean{u}")
                    v.tensor_tensor(dev[:, 4 * u:4 * u + 4, :], dev[:, 4 * u:4 * u + 4, :],
                                    unit(f"mean{u}")[:, 0, :].unsqueeze(1).broadcast_to([P, 4, T]), ALU.subtract) \
                        .then_inc(read(f"mean{u}"), 1)

                def head_rstd(u):
                    taken(dve, L, f"var{u}")
                    v.reciprocal(rstd[:, u % 2, :], rstd[:, u % 2, :]).then_inc(rstd_ready, 1)

                def low_halves(src, base):
                    for p in range(4):
                        dve.wait_ge(high_a, L * 16 + base + p + 1)
                        c = slice(2 * p, 2 * p + 2)
                        v.tensor_tensor(al[:, c, :], src[:, c, :], ah[:, c, :].bitcast(F32), ALU.subtract) \
                            .then_inc(low_a, 1)

                dve.wait_ge(misc_in, 16 * (L + 1))
                norm(L, "norm1", M_G1, htmp)
                halves.make_low(dve, nc, L, 0, 0)
                low_halves(htmp, 0)
                halves.make_low(dve, nc, L, 0, 1)
                for s, name in enumerate(("rawk", "rawv")):
                    done(dve, L, name)
                    v.tensor_copy(raw[0:64, s], unit(name)[0:64])
                    v.tensor_copy(raw[64:P, s, :, 0:T - 1], unit(name)[64:P, :, 1:T]).then_inc(read(name), 1)
                    halves.make_low(dve, nc, L, 0, s + SPLIT)
                if L == 0:
                    dve.wait_ge(tables_in, 16)
                for n in range(8):
                    name = f"{'qk'[n // 4]}r{n % 4}"
                    done(dve, L, name)
                    if n >= 2:
                        dve.wait_ge(rot_added, L * 8 + n - 1)
                    ps = unit(name)
                    v.tensor_tensor(rot[:, n % 2, 0].rearrange("p (a t) -> p a t", a=2), ps[:],
                                    cosq.rearrange("p (a t) -> p a t", a=2), ALU.mult)
                    v.tensor_tensor(rot[:, n % 2, 1].rearrange("p (a t) -> p a t", a=2), ps[:, ::-1, :],
                                    sinq.rearrange("p (a t) -> p a t", a=2), ALU.mult).then_inc(read(name), 1)
                    if n < 7:
                        halves.make_low(dve, nc, L, 0, 2 + n + SPLIT)
                if L == 0:
                    for i in range(8):
                        dve.wait_ge(flipped, i + 1)
                        v.tensor_copy(bias[:, 2 * i:2 * i + 2, :].rearrange("p a t -> p (a t)"),
                                      flip_banks[i % len(flip_banks)][:, :]).then_inc(bias_set, 1)
                for i in range(11, 20):
                    halves.make_low(dve, nc, L, 0, i)
                dve.wait_ge(rot_added, L * 8 + 8)
                for u in range(RH):
                    done(dve, L, f"S{u}")
                    v.tensor_tensor(sT[:, u, :], unit(f"S{u}")[:].rearrange("p a t -> p (a t)")[:, 0:384],
                                    decay[:, u, :], ALU.mult).then_inc(read(f"S{u}"), 1)
                halves.make_low(dve, nc, L, 0, 20)
                halves.make_low(dve, nc, L, 0, 21)
                deviations(0)
                halves.make_low(dve, nc, L, 0, 22)
                deviations(1)
                head_rstd(0)
                halves.make_low(dve, nc, L, 0, 23)
                deviations(2)
                head_rstd(1)
                deviations(3)
                head_rstd(2)
                head_rstd(3)
                for i in range(SPLIT):
                    halves.make_low(dve, nc, L, 1, i)
                taken(dve, L, "gate_t")
                linked(v.tensor_scalar(gates[:], gates[:], 1.0, 0.5, ALU.add, ALU.mult))
                first = gates[:, 0, :].rearrange("p (h b) -> p h b", b=3)[:, :, 0]
                v.tensor_scalar(first, first, con[:, C_ROW:C_ROW + 1], None, ALU.mult).then_inc(gates_set, 1)
                dve.wait_ge(gates_set, L + 1)
                dve.wait_ge(rot_added, L * 8 + 8)
                if L == 0:
                    dve.wait_ge(cb_copied, 2)
                    dve.wait_ge(bias_set, 8)
                for n in range(NH + 2):
                    if n < NH:
                        b = n % 2
                        hd = (n % 2) * 8 + n // 2
                        dve.wait_ge(lg_done, L * NH + n + 1)
                        if L * NH + n >= 2:
                            dve.wait_ge(tr_done, L * NH + n - 1)
                        s_hi = prob[:, b, 0:512].rearrange("p (s k) -> p s k", s=2)
                        s_lo = prob[:, b, 512:768].rearrange("p (s k) -> p s k", s=2)
                        s_c = prob[:, b, 768:800].rearrange("p (s k) -> p s k", s=2)[:, :, 0:NC]
                        v.tensor_tensor(s_hi, lga[:].rearrange("p (s k) -> p s k", s=2),
                                        bias[:, hd, :].unsqueeze(1).broadcast_to([P, 2, T]), ALU.add)
                        v.tensor_tensor(s_lo, lgb[:, 0:256].rearrange("p (s k) -> p s k", s=2),
                                        bias[:, hd, P:T].unsqueeze(1).broadcast_to([P, 2, P]), ALU.add)
                        v.tensor_tensor(s_c, lgb[:, 256:288].rearrange("p (s k) -> p s k", s=2)[:, :, 0:NC],
                                        cbias[:, hd, :, 0:NC], ALU.add).then_inc(lg_read, 1)
                        dve.wait_ge(lg_read, L * NH + n + 1)
                        v.tensor_reduce(stat[:, b, 0, 3:6:2], s_hi, AX, ALU.max, negate=True)
                        v.tensor_reduce(stat[:, b, 0, 2:5:2], s_lo, AX, ALU.max, negate=True)
                        v.tensor_reduce(stat[:, b, 0, 0:2], s_c, AX, ALU.max, negate=True).then_inc(max_ready, 1)
                    if 1 <= n <= NH:
                        m, b = n - 1, (n - 1) % 2
                        hd = (m % 2) * 8 + m // 2
                        dve.wait_ge(exp_done, L * NH + m + 1)
                        linked(v.reciprocal(stat[:, b, 3, :], stat[:, b, 1, :]))
                        v.tensor_tensor(stat[:, b, 2, :].rearrange("p (b q) -> p b q", q=2),
                                        stat[:, b, 3, :].rearrange("p (b q) -> p b q", q=2),
                                        gates[:, :, 3 * hd:3 * hd + 3].rearrange("p q b -> p b q"), ALU.mult) \
                            .then_inc(coef_ready, 1)
                    if n >= 2:
                        m, b = n - 2, n % 2
                        dve.wait_ge(tr_done, L * NH + m + 1)
                        if L * NH + m >= 2:
                            dve.wait_ge(av_done, L * NH + m - 1)
                        v.tensor_copy(probT[:, b, 512:768], trb[:, 0:256])
                        v.tensor_copy(probT[0:NC, b, 768:1024], trb[0:NC, 256:512]).then_inc(ptb, 1)
                    if n < 8:
                        dve.wait_ge(tanh_g, L * 8 + n + 1)
                        if n >= 2:
                            dve.wait_ge(y_ready, L * 8 + n - 1)
                        v.scalar_tensor_tensor(out=gt[:, n % 2, :].rearrange("p (a t) -> p a t", a=2),
                                               in0=th[:, n % 2, :].rearrange("p (a t) -> p a t", a=2), scalar=1.0,
                                               in1=unit(f"side{n}")[:], op0=ALU.add, op1=ALU.mult) \
                            .then_inc(read(f"side{n}"), 1)
                    if n < NH - SPLIT:
                        halves.make_low(dve, nc, L, 1, n + SPLIT)
                for u in range(4):
                    done(dve, L, f"wr{u}")
                    v.scalar_tensor_tensor(out=mix[:, 2 * u:2 * u + 2, :], in0=tha[:, 2 * u:2 * u + 2, :], scalar=1.0,
                                           in1=unit(f"wr{u}")[:], op0=ALU.add, op1=ALU.mult) \
                        .then_inc(read(f"wr{u}"), 1)
                    if u == 1:
                        low_halves(on, 4)
                    if u >= 2:
                        halves.make_low(dve, nc, L, 1, 14 + u)
                for u in range(4):
                    done(dve, L, f"wn{u}")
                    if u >= 2:
                        dve.wait_ge(mix_ready, L * 4 + u - 1)
                    v.scalar_tensor_tensor(out=part[:, u % 2, :].rearrange("p (a t) -> p a t", a=2),
                                           in0=thb[:, 2 * u:2 * u + 2, :], scalar=1.0,
                                           in1=unit(f"wn{u}")[:], op0=ALU.add, op1=ALU.mult) \
                        .then_inc(read(f"wn{u}"), 1)
                    if u < 3:
                        halves.make_low(dve, nc, L, 1, 16 + u + SPLIT)
                low_halves(mix, 8)
                halves.make_low(dve, nc, L, 1, 19 + SPLIT)
                for u in range(4):
                    done(dve, L, f"wo{u}")
                    v.scalar_tensor_tensor(out=x[:, 2 * u:2 * u + 2, :], in0=unit(f"wo{u}")[:], scalar=0.5,
                                           in1=x[:, 2 * u:2 * u + 2, :], op0=ALU.mult, op1=ALU.add) \
                        .then_inc(read(f"wo{u}"), 1)
                    if u < 3:
                        halves.make_low(dve, nc, L, 1, 20 + u + SPLIT)
                for c in range(KD):
                    if c % 2 == 0:
                        dve.wait_ge(high_a, L * 16 + 12 + c // 2 + 1)
                    last = v.scalar_tensor_tensor(out=al[:, c, :], in0=x[:, c, :], scalar=misc[:, M_G2 + c:M_G2 + c + 1],
                                                  in1=ah[:, c, :].bitcast(F32), op0=ALU.mult, op1=ALU.subtract)
                    if c % 2:
                        last.then_inc(low_a, 1)
                halves.make_low(dve, nc, L, 1, 23 + SPLIT)
                taken(dve, L, "norm2")
                linked(v.reciprocal(rstd[:, 0, :], rstd[:, 0, :]))

                def over_rms(dst, name):
                    done(dve, L, name)
                    v.tensor_tensor(dst.rearrange("p (a t) -> p a t", a=2), unit(name)[:],
                                    rstd[:, 0, :].unsqueeze(1).broadcast_to([P, 2, T]), ALU.mult) \
                        .then_inc(read(name), 1)

                for u in range(FF // W):
                    over_rms(tf[:, u % 2, :], f"fa{u}")
                    halves.make_low(dve, nc, L, 1, 24 + 2 * u + SPLIT)
                    if u >= 2:
                        dve.wait_ge(ffl_ready, L * (FF // W) + u - 1)
                    over_rms(ft[:, u % 2, :], f"fb{u}")
                    dve.wait_ge(silu_done, L * (FF // W) + u + 1)
                    taken(dve, L, f"fb{u}")
                    v.tensor_tensor(ft[:, u % 2, :], ft[:, u % 2, :], tf[:, u % 2, :], ALU.mult).then_inc(ff_made, 1)
                    halves.make_low(dve, nc, L, 1, 25 + 2 * u + SPLIT)
                for u in range(4):
                    for i in range(3):
                        halves.make_low(dve, nc, L, 1, 24 + 2 * (FF // W) + 3 * u + i + SPLIT)
                    done(dve, L, f"fo{u}")
                    v.tensor_tensor(x[:, 2 * u:2 * u + 2, :], unit(f"fo{u}")[:], x[:, 2 * u:2 * u + 2, :], ALU.add) \
                        .then_inc(read(f"fo{u}"), 1)
            dve.wait_ge(final_root, 1)
            linked(v.reciprocal(rstd[:, 0, :], rstd[:, 0, :]))
            for k in range(KD):
                last = v.scalar_tensor_tensor(out=x[:, k, :], in0=x[:, k, :], scalar=con[:, C_GF + k:C_GF + k + 1],
                                              in1=rstd[:, 0, :], op0=ALU.mult, op1=ALU.mult)
            last.then_inc(x_final, 1)
            dve.wait_ge(x_final, 1)

        @block.gpsimd
        def _(pool):
            g_ = nc.gpsimd
            links = [0]

            def linked(ins):
                links[0] += 1
                ins.then_inc(link["pool"], 1)
                pool.wait_ge(link["pool"], links[0])

            g_.memset(tab[32:33, :], NEG).then_inc(tab_set, 1)
            pool.wait_ge(tab_set, 1)
            for L in range(LAYERS):
                pool.wait_ge(misc_in, 16 * (L + 1))
                for s, name in enumerate(("rawk", "rawv")):
                    taken(pool, L, name)
                    for g in range(NG):
                        r = raw[:, s, g, :]
                        win = bass.AP(tensor=r.tensor, offset=r.offset, ap=[list(r.ap[0]), [16, NC], [2, 16]])
                        pos = misc[:, M_POSK + 16 * s:M_POSK + 16 * s + 16].unsqueeze(1).broadcast_to([P, NC, 16])
                        last = g_.tensor_tensor(wins[:, s, g], win, pos, ALU.add)
                    last.then_inc(wins_ready, 1)
                for n in range(8):
                    taken(pool, L, f"{'qk'[n // 4]}r{n % 4}")
                    dst = (qr if n < 4 else kr)[:, 2 * (n % 4):2 * (n % 4) + 2, :]
                    g_.tensor_tensor(dst, rot[:, n % 2, 0].rearrange("p (a t) -> p a t", a=2),
                                     rot[:, n % 2, 1].rearrange("p (a t) -> p a t", a=2), ALU.add) \
                        .then_inc(rot_added, 1)
                for u in range(RH):
                    pool.wait_ge(rstd_ready, L * RH + u + 1)
                    g_.tensor_tensor(dev[:, 4 * u:4 * u + 4, :], dev[:, 4 * u:4 * u + 4, :],
                                     rstd[:, u % 2, :].unsqueeze(1).broadcast_to([P, 4, T]), ALU.mult) \
                        .then_inc(normed, 1)
                pool.wait_ge(normed, (L + 1) * RH)
                for n in range(NH):
                    b = n % 2
                    pool.wait_ge(coef_ready, L * NH + n + 1)
                    for at, w, j in ((0, T, 3), (512, P, 2)):
                        p = prob[:, b, at:at + 2 * w].rearrange("p (s k) -> p s k", s=2)
                        g_.tensor_tensor(p, p, stat[:, b, 2, j:j + 3:2].unsqueeze(2).broadcast_to([P, 2, w]), ALU.mult)
                    p = prob[:, b, 768:800].rearrange("p (s k) -> p s k", s=2)[:, :, 0:NC]
                    g_.tensor_tensor(p, p, stat[:, b, 2, 0:2].unsqueeze(2).broadcast_to([P, 2, NC]), ALU.mult) \
                        .then_inc(prob_ready, 1)
                    if n < 8:
                        taken(pool, L, f"side{n}")
                        c = slice(2 * n, 2 * n + 2)
                        g_.tensor_tensor(dev[:, c, :], dev[:, c, :], gt[:, b, :].rearrange("p (a t) -> p a t", a=2),
                                         ALU.mult).then_inc(y_ready, 1)
                for u in range(4):
                    taken(pool, L, f"wn{u}")
                    g_.tensor_tensor(mix[:, 2 * u:2 * u + 2, :], mix[:, 2 * u:2 * u + 2, :],
                                     part[:, u % 2, :].rearrange("p (a t) -> p a t", a=2), ALU.add) \
                        .then_inc(mix_ready, 1)
                for u in range(FF // W):
                    pool.wait_ge(ffh_ready, L * (FF // W) + u + 1)
                    c = slice(2 * u, 2 * u + 2)
                    g_.tensor_tensor(ffl[:, c, :], ft[:, u % 2, :].rearrange("p (a t) -> p a t", a=2),
                                     ffh[:, c, :].bitcast(F32), ALU.subtract).then_inc(ffl_ready, 1)


def chunked(w):
    k, n = w.shape
    return w.reshape(k // P, P, n).transpose(1, 0, 2)


def weight_tiles(w):
    k, n = w.shape
    out = []
    for u in range(n // W):
        for r in range(0, k, D):
            t = np.zeros((P, KD, W), np.float32)
            c = chunked(w[r:r + D, u * W:(u + 1) * W])
            t[:, :c.shape[1]] = c
            out.append(t.reshape(P, TILE))
    return out


def first_weights(i, w_in, w1k, w1v, w_o_ret, w_o_nsa, w_out, w_ffn_in, w_ffn_out):
    w = w_in[i]
    q_n, kv = 6144, 7168
    heads = [np.arange(hd * HD, (hd + 1) * HD) for hd in range(NH)]
    order = np.concatenate([np.concatenate([heads[c], heads[8 + c]]) for c in range(8)])
    kvc = lambda s, g=None: kv + s * P + (np.arange(P) if g is None else g * HD + np.arange(HD))
    out = []
    for s in (0, 1):
        out += weight_tiles(w[:, np.concatenate([kvc(s, 0), kvc(s, 0), kvc(s, 1), kvc(s, 1)])])
    out += weight_tiles(w[:, 0:2048])
    out += weight_tiles(w1k[i]) + weight_tiles(w1v[i])
    out += weight_tiles(w[:, 2048:4096])
    out += weight_tiles(w[:, np.concatenate([kvc(2), kvc(4)])])
    out += weight_tiles(w[:, np.concatenate([kvc(3), kvc(5)])])
    out += weight_tiles(w[:, q_n + order])
    out += weight_tiles(w[:, 4096:6144]) + weight_tiles(w[:, 7984:7984 + 2048])
    out += weight_tiles(w_o_ret[i]) + weight_tiles(w_o_nsa[i][order]) + weight_tiles(w_out[i])
    a, b = weight_tiles(w_ffn_in[i][:, :FF]), weight_tiles(w_ffn_in[i][:, FF:])
    for u in range(FF // W):
        out += [a[u], b[u]]
    out += weight_tiles(w_ffn_out[i])
    return np.stack(out)


def first_misc(i, w_in, pos_k, pos_v, w2k, w2v, g1, g2):
    m = np.zeros((P, M1), np.float32)
    m[:, M_GATE:M_GATE + 384] = chunked(w_in[i][:, 7936:7984]).reshape(P, 384)
    m[:, M_W2K:M_W2K + 128] = chunked(w2k[i]).reshape(P, 128)
    m[:, M_W2V:M_W2V + 128] = chunked(w2v[i]).reshape(P, 128)
    for at, pos in ((M_POSK, pos_k), (M_POSV, pos_v)):
        m[:, at:at + 16] = pos[i].reshape(16, P).T
    m[:, M_G1:M_G1 + KD] = g1[i].reshape(KD, P).T
    m[:, M_G2:M_G2 + KD] = g2[i].reshape(KD, P).T
    return m


def first_constants(norm_final_g):
    c = np.zeros((P, C1), np.float32)
    c[:, C_ID:C_ID + P] = np.eye(P)
    c[:, C_ONE:C_ONE + P] = 1 / D
    c[:, C_MEAN:C_MEAN + P] = 1 / RV
    c[:, C_VAR:C_VAR + P] = 4 / RV
    f = np.float32(10000.0) ** (-np.arange(P, dtype=np.float32) / P)
    ang = (np.arange(T, dtype=np.float32)[None] * f[:, None]).astype(np.float64)
    c[:, C_COS:C_COS + 512] = np.concatenate([np.cos(ang)] * 2, 1)
    c[:, C_SIN:C_SIN + 512] = np.concatenate([-np.sin(ang), np.sin(ang)], 1)
    for hd in range(RH):
        lg = math.log(1 - 2.0 ** (-5 - hd))
        m, n = np.arange(P)[:, None], np.arange(T)[None]
        full = np.where(n >= m, np.exp(lg * np.maximum(n - m, 0)), 0) / 16
        c[:, C_DT + hd * 384:C_DT + hd * 384 + T] = full
        c[:, C_DT + hd * 384 + T:C_DT + (hd + 1) * 384] = full[:, 0:P]
    c[:, C_ROW] = np.arange(P) >= 31
    c[:, C_EPS], c[:, C_EPS4] = 1e-6, 4e-5
    c[:, C_GF:C_GF + KD] = norm_final_g.reshape(KD, P).T
    return c


def distance_rows(dist):
    d = np.maximum(dist, 1).astype(np.float32)
    large = 16 + (np.log(d / 16) / np.float32(math.log(8)) * 16).astype(np.int32)
    b = np.where(dist < 16, np.maximum(dist, 0), np.minimum(large, 31))
    b = np.where(dist < 0, 32, b)
    return (np.arange(33)[:, None] == b[None]).astype(np.float32)


AH, BH, CH = 4, 8, 8
HID = 4 * D
KH = HID // P
TOP = 64
ACCS2 = 4
GONE = -3e38
QK_ITEMS = ("ik", "iq", "ck0", "ck1", "cq0", "cq1", "ak0", "ak1", "aq0", "aq1")


def second_plan():
    p = Plan(ACCS2, RING)

    def norm_rot(i):
        if QK_ITEMS[i] != "iq":
            p.add(f"ms_{QK_ITEMS[i]}")
        p.add(f"rot_{QK_ITEMS[i]}")

    p.add("norm1")
    p.add("iw")
    p.add("ik", 1)
    p.add("iq", 1)
    p.add("iw_t")
    norm_rot(0)
    for i in range(2, len(QK_ITEMS)):
        p.add(QK_ITEMS[i], 1)
        norm_rot(i - 1)
    p.add("bq0", 1)
    norm_rot(len(QK_ITEMS) - 1)
    for name in ("bq1", "bk0", "bk1", "cv0", "cv1", "av0", "av1", "bv0", "bv1"):
        p.add(name, 1)
    for u in range(12):
        p.add(f"gl{u}", 1)

    def branch(name, u):
        p.add(f"{name}{u}", 1 - u % 2)
        if u % 2:
            p.tiles[f"{name}{u}"] = p.tiles[f"{name}{u - 1}"]

    for u in range(4):
        branch("bb", u)
    for u in range(AH):
        branch("bc", u)
        if u >= 2:
            p.add(f"msa{u - 2}")
    p.add("msa2")
    p.add("msa3")
    for u in range(4):
        branch("ba", u)
    for u in range(4):
        p.add(f"wo{u}", 1)
    for u in range(HID // W):
        p.add(f"up{u}", 1)
        if u == 0:
            p.add("norm2")
    for u in range(4):
        p.add(f"dn{u}", 4)
    for u in range(4):
        p.add(f"pg{u}", 1)
        if u == 0:
            p.add("norm3")
    for u in range(4):
        p.add(f"pp{u}", 1 if u == 0 else 0)
        p.tiles[f"pp{u}"] = p.tiles["pp0"]
    return p.close((("ik", "bv1"), ("gl0", "gl11"), ("wo0", "pg3")))


N_IW, N_GAIN, N_SUB, N_LAM, N_G1, N_G2, N_G3, N_LINIT, N_LREST = 0, 32, 37, 38, 294, 302, 310, 318, 319
M2 = 320
GAIN_OF = {"ik": 0, "ck": 1, "cq": 2, "ak": 3, "aq": 4}
E_ONE, E_EPS, E_EPS64, E_FREQ, E_ID, E_G1, E_G64, E_HEAD, E_ROT, E_TRI, E_NEG, E_CH, E_S01, E_SNEG = \
    0, 128, 129, 130, 131, 259, 387, 515, 643, 771, 899, 1027, 1411, 1795
E_FIRST = E_ID
C2 = 2179
TWO_PI_1 = 6.28125
TWO_PI_2 = float((np.float32(2 * math.pi - TWO_PI_1).view(np.uint32) & np.uint32(0xfffff000)).view(np.float32))
TWO_PI_3 = 2 * math.pi - TWO_PI_1 - TWO_PI_2
MAGIC = 12582912.0


def second_block(nc, outer, ring, x, w2, m2, c2, pos, pt, out):
    plan = second_plan()
    UNITS = len(plan.names)
    with ExitStack() as ctx:
        def sb(name, shape, dt=F32):
            return ctx.enter_context(nc.sbuf_tensor("b_" + name, shape, dt))

        def sem(name):
            return outer.enter_context(nc.semaphore("b_" + name))

        def pairs(ap):
            return ap.rearrange("p (a t) -> p a t", a=2)

        _, high_p, low_p = overlay(nc, ("b_before_p", [P, 42 * T], F32), ("b_high_p", [P, SPLIT, KD, W], F32R),
                                   ("b_low_p", [P, SPLIT, KD, W], F32R))
        _, high_g, low_g = overlay(nc, ("b_before_g", [P, 64 * T], F32), ("b_high_g", [P, SPLIT, KD, W], F32R),
                                   ("b_low_g", [P, SPLIT, KD, W], F32R))
        high_f, low_f, hidh, hidl = overlay(
            nc, ("b_high_f", [P, SPLIT, KD, W], F32R), ("b_low_f", [P, SPLIT, KD, W], F32R),
            ("b_hidh", [P, KH, T], F32R), ("b_hidl", [P, KH, T], F32R))
        qkv = sb("qkv", [P, 36, T])
        cq, ck, aq, ak, bq, bk = (qkv[:, 4 * i:4 * i + 4, :] for i in range(6))
        av, bv, cv = (qkv[:, 24 + 4 * i:28 + 4 * i, :].rearrange("p a b -> p (a b)")
                      .rearrange("p (j n) -> p j n", j=2) for i in range(3))
        gates = sb("gates", [P, 24, T])
        rel = gates[:, 0:6, :].rearrange("p a b -> p (a b)")
        sg = gates[:, 0:8, :]
        yb, yc, ya = (sb(f"y{c}", [P, 4, T]) for c in "bca")
        mrg = sb("mrg", [P, KD, T])
        qkw = sb("qkw", [P, 3, 2, 512])
        iq = sb("iq", [P, 2, T])
        ik = sb("ik", [P, T])
        posi = sb("posi", [P, T], I32)
        att = sb("att", [P, 4608])
        ah, al = (ctx.enter_context(nc.sbuf_tensor("b_" + n, [P, KD, T], F32R)) for n in ("ah", "al"))
        lnb = att[:, 0:768].rearrange("p (b n) -> p b n", b=2)
        spb = att[:, 768:1536].rearrange("p (b n) -> p b n", b=2)
        eb = att[:, 1536:2304].rearrange("p (b n) -> p b n", b=2)
        prob = att[:, 2304:3840].rearrange("p (b n) -> p b n", b=2)
        probT = att[:, 3840:4608].rearrange("p (b n) -> p b n", b=2)
        sq = htmp = att[:, 0:2048].rearrange("p (c t) -> p c t", c=KD)
        sqa = att[:, 0:512].rearrange("p (b n) -> p b n", b=2)
        rsa = att[:, 512:1024].rearrange("p (b n) -> p b n", b=2)
        ft = att[:, 1024:2048].rearrange("p (b n) -> p b n", b=2)
        part = sb("part", [P, 2, 512])
        iw = sb("iw", [P, 2, 4])
        iwf = sb("iwf", [4, T])
        score = sb("score", [P, 384])
        mx8 = sb("mx8", [P, 2, 8])
        chosen = sb("chosen", [P, 384])
        rstd = sb("rstd", [P, T])
        early = sb("early", [P, 1])
        stat = sb("stat", [P, 2, 3, 4])
        cosb = sb("cosb", [P, T])
        sinb = sb("sinb", [P, T])
        ang = qkv[:, 0, :]
        turn = qkv[:, 1:3, :]
        angs = qkv[:, 3:5, :]
        misc = sb("misc", [P, M2])
        lam = sb("lam", [P, 8])
        lamp = sb("lamp", [P, 2, 64])
        pin = sb("pin", [P, 2, T])
        con = sb("con", [P, C2])

        acc = [ctx.enter_context(nc.psum_tensor(f"b_acc{b}", [P, 2, T], F32)) for b in range(ACCS2)]
        lg = [ctx.enter_context(nc.psum_tensor(f"b_lg{b}", [P, 512], F32)) for b in range(2)]
        tr = ctx.enter_context(nc.psum_tensor("b_tr", [P, 512], F32))
        avo = ctx.enter_context(nc.psum_tensor("b_avo", [P, 512], F32))

        def aprob(c, b):
            return prob[:, b, 384 * c:384 * c + 384]

        def cmat(at):
            return con[:, at:at + P]

        loaded = [sem(f"tile_loaded{s}") for s in range(RING)]
        pos_in, tables_in = sem("positions_loaded"), sem("tables_loaded")
        misc_in, con_in, p_in, out_stored = sem("misc_loaded"), sem("con_loaded"), sem("p_loaded"), sem("out_stored")
        unit_done = sem("unit_done")
        bank_read = [sem(f"bank_read{b}") for b in range(ACCS2)]
        angles, rope_set = sem("angles"), sem("rope_set")
        squares, h_ready, x_ple = sem("squares"), sem("h_ready"), sem("x_ple")
        qk_rstd, qk_out = sem("qk_rstd"), sem("qk_out")
        idx_done, rel_ready, chosen_ready, lam_exp = sem("idx_done"), sem("rel_ready"), sem("chosen"), sem("lam_exp")
        lam_in, lam_set = sem("lam_in"), sem("lam_set")
        z_done, ln_ready, z_read, sp_ready, zs_done, e_ready, a_ready, bo_done, yb_ready = (sem(n) for n in (
            "z_done", "ln_ready", "z_read", "sp_ready", "zs_done", "e_ready", "a_ready", "bo_done", "yb_ready"))
        c_lg, c_read, c_max, c_exp, c_coef, c_prob, c_tr, c_pt, c_av, yc_ready = (sem("c_" + n) for n in (
            "logits", "read", "max", "exp", "coef", "prob", "transposed", "probT", "values", "y"))
        a_lg, a_read, a_max, a_exp, a_coef, a_prob, a_tr, a_pt, a_av, a_raw, a_rstd, ya_ready = (
            sem("a_" + n) for n in ("logits", "read", "max", "exp", "coef", "prob", "transposed", "probT", "values",
                                    "raw", "rstd", "y"))
        mrg_ready, relu_ready, sg_ready = sem("mrg_ready"), sem("relu_ready"), sem("ple_gate_ready")
        halves = Halves(plan, ring, loaded, unit_done, sem)
        halves.place([high_p, high_g, high_f], [low_p, low_g, low_f])
        high_a, low_a, hidh_ready, hidl_ready = (sem(n) for n in (
            "operand_high", "operand_low", "hidden_high", "hidden_low"))
        link = {e: sem(f"{e}_link") for e in ("dve", "act", "pool")}

        def unit(name):
            return acc[plan.bank(name)]

        def done(eng, L, name):
            eng.wait_ge(unit_done, L * UNITS + plan.n(name) + 1)

        def raw_read(eng, L, t):
            if t in plan.split:
                halves.raw_read(eng, L, t)
            else:
                done(eng, L, plan.last_user(t))

        def read(name):
            return bank_read[plan.bank(name)]

        def taken(eng, L, name):
            b = plan.bank(name)
            eng.wait_ge(bank_read[b], L * plan.units_of_bank(b) + plan.n(name) // ACCS2 + 1)

        block = ctx.enter_context(nc.Block())

        @block.sync
        def _(sp):
            sp.dma_start(con[:, 0:E_FIRST], c2[:, 0:E_FIRST]).then_inc(con_in, 16)
            for L in range(LAYERS):
                if L:
                    sp.wait_ge(low_a, L * 16)
                sp.dma_start(misc[:], m2[L]).then_inc(misc_in, 16)
                if L == 0:
                    sp.dma_start(posi[:], pos).then_inc(pos_in, 16)
                for t in range(plan.count):
                    if L == 0 and t == 1:
                        sp.dma_start(con[:, E_FIRST:], c2[:, E_FIRST:]).then_inc(tables_in, 16)
                    s = t % RING
                    if t >= RING:
                        raw_read(sp, L, t - RING)
                    elif L:
                        raw_read(sp, L - 1, max(v for v in range(plan.count) if v % RING == s))
                    sp.dma_start(ring[:, s, :, :].rearrange("p k n -> p (k n)"), w2[L, t]).then_inc(loaded[s], 16)
                    if t == RING - 1:
                        if L:
                            sp.wait_ge(x_ple, L * 4)
                        sp.dma_start(pin[:], pt[L]).then_inc(p_in, 16)
            sp.wait_ge(x_ple, LAYERS * 4)
            sp.dma_start(out, x[:]).then_inc(out_stored, 16)
            sp.wait_ge(out_stored, 16)

        @block.tensor
        def _(pe):
            mm = nc.tensor.matmul

            def begin(L, name):
                b, n = plan.bank(name), plan.n(name)
                before = L * plan.units_of_bank(b) + n // ACCS2
                if before:
                    pe.wait_ge(bank_read[b], before)
                return acc[b]

            def tile(L, t):
                s = t % RING
                pe.wait_ge(loaded[s], 16 * (L * plan.tiles_of_slot(s) + t // RING + 1))
                return ring[:, s]

            def split_features(L, name, operand, chunks=KD, ready=None):
                ps = begin(L, name)
                tiles = plan.tiles[name]
                for i, t in enumerate(tiles):
                    last = halves.features(pe, nc, L, t, ps, operand, i * KD, chunks, ready)
                    last.then_inc(unit_done if t == tiles[-1] else halves.part_done, 1)

            def narrow(L, name, src, chunks, at):
                ps = begin(L, name)
                w = tile(L, plan.tiles[name][0]).rearrange("p k n -> p (k n)").rearrange("p (k n) -> p k n", k=chunks)
                for j in range(2):
                    for k in range(chunks):
                        last = mm(ps[:, j, :], w[:, k, at + j * P:at + (j + 1) * P], src[:, k, :],
                                  start=(k == 0), stop=(k == chunks - 1))
                last.then_inc(unit_done, 1)

            def split_tokens(L, name):
                ps = begin(L, name)
                halves.tokens(pe, nc, L, plan.tiles[name][0], ps, (ah, al)).then_inc(unit_done, 1)

            def few_features(L, name, w, n, before):
                ps = begin(L, name)
                for k in range(KD):
                    pe.wait_ge(h_ready, before + k + 1)
                    last = mm(ps[0:n, 0, :], w[:, n * k:n * (k + 1)], htmp[:, k, :], start=(k == 0), stop=(k == KD - 1))
                last.then_inc(unit_done, 1)

            def turned(L, name, src, of, n):
                ps = begin(L, name)
                taken(pe, L, of)
                for j in range(2):
                    last = nc.tensor.transpose(ps[:, j, 0:n], src[0:n, j * P:(j + 1) * P], con[0:n, E_ID:E_ID + n])
                last.then_inc(unit_done, 1)

            def norm(L, name, base):
                ps = begin(L, name)
                for k in range(KD):
                    if k % 2 == 0:
                        pe.wait_ge(squares, base + k // 2 + 1)
                    last = mm(ps[:, 0, :], cmat(E_ONE), sq[:, k, :], start=(k == 0), stop=(k == KD - 1))
                last.then_inc(unit_done, 1)

            def norm_rot(L, i):
                name = QK_ITEMS[i]
                w = T if name == "ik" else 2 * T
                if name != "iq":
                    ps = begin(L, f"ms_{name}").rearrange("p a b -> p (a b)")
                    taken(pe, L, name)
                    mm(ps[:, 0:w], cmat(E_G64 if name[1] == "q" else E_G1), qkw[:, 0, i % 2, 0:w],
                       start=True, stop=True).then_inc(unit_done, 1)
                ps = begin(L, f"rot_{name}").rearrange("p a b -> p (a b)")
                taken(pe, L, name)
                mm(ps[:, 0:w], cmat(E_ROT), qkw[:, 1, i % 2, 0:w], start=True, stop=True).then_inc(unit_done, 1)

            def logits(ps, q, k):
                mm(ps[:, 0:P], q[:, 0:P], k[:, 0:P], start=True, stop=True)
                return mm(ps[:, P:P + T], q[:, P:T], k, start=True, stop=True)

            def transposes(b):
                t = nc.tensor.transpose
                t(tr[:, 0:P], prob[:, b, 0:P], cmat(E_ID))
                t(tr[:, P:2 * P], prob[:, b, P:2 * P], cmat(E_ID))
                return t(tr[:, 2 * P:3 * P], prob[:, b, 2 * P:3 * P], cmat(E_ID))

            pe.wait_ge(con_in, 16)
            for L in range(LAYERS):
                norm(L, "norm1", L * 12)
                pe.wait_ge(misc_in, 16 * (L + 1))
                few_features(L, "iw", misc[:, N_IW:N_IW + 32], 4, L * 8)
                split_features(L, "ik", (ah, al), ready=(low_a, L * 16))
                split_features(L, "iq", (ah, al))
                pe.wait_ge(tables_in, 16)
                turned(L, "iw_t", iwf, "iw", 4)
                norm_rot(L, 0)
                for i in range(2, len(QK_ITEMS)):
                    split_features(L, QK_ITEMS[i], (ah, al))
                    norm_rot(L, i - 1)
                    if i == 3:
                        pe.wait_ge(qk_out, L * 10 + 2)
                        for hd in range(4):
                            r = slice((hd % 2) * 64, (hd % 2) * 64 + 64)
                            q = iq[r, hd // 2, :]
                            mm(lg[hd % 2][:, (hd // 2) * T:(hd // 2) * T + T], q[:, P:T], ik[r, :],
                               start=True, stop=True)
                        for hd in range(4):
                            r = slice((hd % 2) * 64, (hd % 2) * 64 + 64)
                            last = mm((tr, avo)[hd % 2][:, (hd // 2) * P:(hd // 2 + 1) * P], iq[r, hd // 2, 0:P], ik[r, 0:P],
                                      start=True, stop=True)
                        last.then_inc(idx_done, 1)
                split_features(L, "bq0", (ah, al))
                norm_rot(L, len(QK_ITEMS) - 1)
                for name in ("bq1", "bk0", "bk1"):
                    split_features(L, name, (ah, al))
                for name in ("cv0", "cv1", "av0", "av1", "bv0", "bv1"):
                    split_tokens(L, name)
                taken(pe, L, "bv1")
                pe.wait_ge(rel_ready, L + 1)
                for n in range(BH + 1):
                    if n < BH:
                        r = slice((n % 2) * 64, (n % 2) * 64 + 64)
                        if L * BH + n:
                            pe.wait_ge(z_read, L * BH + n)
                        mm(lg[0][:, 0:T], bk[r, n // 2, 0:P], bq[r, n // 2, :], start=True, stop=True)
                        mm(lg[0][:, T:T + P], bk[r, n // 2, P:T], bq[r, n // 2, P:T], start=True, stop=True) \
                            .then_inc(z_done, 1)
                    if n >= 1:
                        m, b = n - 1, (n - 1) % 2
                        r = slice((m % 2) * 64, (m % 2) * 64 + 64)
                        pe.wait_ge(sp_ready, L * BH + m + 1)
                        if L * BH + m:
                            pe.wait_ge(e_ready, L * BH + m)
                        e = lg[1]
                        mm(e[:, 0:T], bk[r, m // 2, 0:P], bq[r, m // 2, :], start=True, stop=False)
                        mm(e[:, 0:T], cmat(E_TRI), spb[:, b, 0:T], start=False, stop=False)
                        mm(e[:, P:T], cmat(E_NEG), spb[:, b, T:T + P], start=False, stop=True)
                        mm(e[:, T:T + P], bk[r, m // 2, P:T], bq[r, m // 2, P:T], start=True, stop=False)
                        mm(e[:, T:T + P], cmat(E_TRI), spb[:, b, T:T + P], start=False, stop=True) \
                            .then_inc(zs_done, 1)
                    if n == BH:
                        pe.wait_ge(z_read, (L + 1) * BH)
                        logits(lg[0], cq[0:64, 0, :], ck[0:64, 0, :]).then_inc(c_lg, 1)
                    split_features(L, f"gl{n}", (ah, al))
                    if n >= 1:
                        m, b = n - 1, (n - 1) % 2
                        pe.wait_ge(a_ready, L * BH + m + 1)
                        if m % 2 == 0:
                            if m:
                                pe.wait_ge(yb_ready, L * 4 + m // 2)
                            elif L:
                                pe.wait_ge(a_raw, L * AH)
                        o = avo[(m % 2) * 64:(m % 2) * 64 + 64, 0:T]
                        mm(o, bv[:, 0, m * 64:(m + 1) * 64], eb[:, b, 0:T], start=True, stop=False)
                        mm(o[:, P:T], bv[:, 1, m * 64:(m + 1) * 64], eb[:, b, T:T + P], start=False, stop=True) \
                            .then_inc(bo_done, 1)
                pe.wait_ge(e_ready, (L + 1) * BH)
                for n in range(CH + 2):
                    if n < CH:
                        r = slice((n % 2) * 64, (n % 2) * 64 + 64)
                        if n >= 2:
                            pe.wait_ge(c_read, L * CH + n - 1)
                        if n:
                            logits(lg[n % 2], cq[r, n // 2, :], ck[r, n // 2, :]).then_inc(c_lg, 1)
                        if n < 3:
                            split_features(L, f"gl{9 + n}", (ah, al))
                        elif n >= 4:
                            if n == 4:
                                pe.wait_ge(yb_ready, (L + 1) * 4)
                            narrow(L, f"bb{n - 4}", yb, 4, (n % 2) * W)
                    if 1 <= n <= CH:
                        pe.wait_ge(c_prob, L * CH + n)
                        if n >= 2:
                            pe.wait_ge(c_pt, L * CH + n - 1)
                        transposes((n - 1) % 2).then_inc(c_tr, 1)
                    if n == CH + 1:
                        pe.wait_ge(c_read, (L + 1) * CH)
                        logits(lg[0], aq[0:64, 0, :], ak[0:64, 0, :])
                        logits(lg[1], aq[64:P, 0, :], ak[64:P, 0, :]).then_inc(a_lg, 1)
                    if n >= 2:
                        m, b = n - 2, n % 2
                        pe.wait_ge(c_pt, L * CH + m + 1)
                        if m % 2 == 0:
                            if m:
                                pe.wait_ge(yc_ready, L * 4 + m // 2)
                            else:
                                pe.wait_ge(yb_ready, (L + 1) * 4)
                        o = avo[(m % 2) * 64:(m % 2) * 64 + 64, 0:T]
                        mm(o, cv[:, 0, m * 64:(m + 1) * 64], probT[:, b, 0:T], start=True, stop=False)
                        mm(o[:, P:T], cv[:, 1, m * 64:(m + 1) * 64], probT[:, b, T:T + P], start=False, stop=True) \
                            .then_inc(c_av, 1)
                pe.wait_ge(yc_ready, (L + 1) * 4)
                for n in range(AH + 2):
                    if n < AH:
                        if n:
                            pe.wait_ge(a_read, L * AH + n)
                            logits(lg[0], aq[0:64, n, :], ak[0:64, n, :])
                            logits(lg[1], aq[64:P, n, :], ak[64:P, n, :]).then_inc(a_lg, 1)
                        narrow(L, f"bc{n}", yc, 4, (n % 2) * W)
                    if 1 <= n <= AH:
                        pe.wait_ge(a_prob, L * AH + n)
                        if n >= 2:
                            pe.wait_ge(a_pt, L * AH + n - 1)
                        transposes((n - 1) % 2).then_inc(a_tr, 1)
                        m, b = n - 1, (n - 1) % 2
                        pe.wait_ge(a_pt, L * AH + m + 1)
                        if m:
                            pe.wait_ge(a_raw, L * AH + m)
                        mm(avo[:, 0:T], av[:, 0, m * P:(m + 1) * P], probT[:, b, 0:T], start=True, stop=False)
                        mm(avo[:, P:T], av[:, 1, m * P:(m + 1) * P], probT[:, b, T:T + P], start=False, stop=True) \
                            .then_inc(a_av, 1)
                    if n >= 2:
                        m = n - 2
                        ps = begin(L, f"msa{m}")
                        pe.wait_ge(a_raw, L * AH + m + 1)
                        mm(ps[:, 0, :], cmat(E_HEAD), sqa[:, m % 2, :], start=True, stop=True).then_inc(unit_done, 1)
                pe.wait_ge(ya_ready, (L + 1) * AH)
                for u in range(4):
                    narrow(L, f"ba{u}", ya, 4, (u % 2) * W)
                for u in range(4):
                    split_features(L, f"wo{u}", (ah, al), ready=None if u else (low_a, L * 16 + 4))
                for u in range(HID // W):
                    split_features(L, f"up{u}", (ah, al), ready=None if u else (low_a, L * 16 + 8))
                    if u == 0:
                        norm(L, "norm2", L * 12 + 4)
                for u in range(4):
                    split_features(L, f"dn{u}", (hidh, hidl), KH, ready=None if u else (hidl_ready, L * (HID // W)))
                for u in range(4):
                    split_features(L, f"pg{u}", (ah, al), ready=None if u else (low_a, L * 16 + 12))
                    if u == 0:
                        norm(L, "norm3", L * 12 + 8)
                pe.wait_ge(p_in, 16 * (L + 1))
                for u in range(4):
                    narrow(L, f"pp{u}", pin, 2, u * W)

        @block.scalar
        def _(act):
            op = nc.scalar.activation
            links = [0]

            def linked(ins):
                links[0] += 1
                ins.then_inc(link["act"], 1)
                act.wait_ge(link["act"], links[0])

            def squares_of():
                for p in range(4):
                    yield p
                    op(sq[:, 2 * p:2 * p + 2, :], x[:, 2 * p:2 * p + 2, :], ACT.Square).then_inc(squares, 1)

            def root(L, name):
                op(early[:, :], con[:, E_EPS:E_EPS + 1], ACT.Sqrt)
                done(act, L, name)
                op(rstd[:, :], unit(name)[:, 0, :], ACT.Sqrt, bias=con[:, E_EPS:E_EPS + 1]).then_inc(read(name), 1)

            def raw_item(L, i):
                name = QK_ITEMS[i]
                w = T if name == "ik" else 2 * T
                done(act, L, name)
                if i >= 2:
                    act.wait_ge(qk_out, L * 10 + i - 1)
                ps = unit(name)[:].rearrange("p a b -> p (a b)")[:, 0:w]
                if name == "iq":
                    op(qkw[:, 1, i % 2, 0:w], ps, ACT.Copy).then_inc(read(name), 1)
                else:
                    g = N_GAIN + GAIN_OF[name[:2]]
                    op(qkw[:, 0, i % 2, 0:w], ps, ACT.Square)
                    op(qkw[:, 1, i % 2, 0:w], ps, ACT.Copy, scale=misc[:, g:g + 1]).then_inc(read(name), 1)

            def root_item(L, i):
                name = QK_ITEMS[i]
                if name != "iq":
                    w = T if name == "ik" else 2 * T
                    done(act, L, f"ms_{name}")
                    e = E_EPS64 if name[1] == "q" else E_EPS
                    op(qkw[:, 0, i % 2, 0:w], unit(f"ms_{name}")[:].rearrange("p a b -> p (a b)")[:, 0:w], ACT.Sqrt,
                       bias=con[:, e:e + 1]).then_inc(read(f"ms_{name}"), 1)

            act.wait_ge(con_in, 16)
            for L in range(LAYERS):
                def scaled_high(gain, p):
                    for c in (2 * p, 2 * p + 1):
                        last = op(ah[:, c, :], x[:, c, :], ACT.Copy, scale=misc[:, gain + c:gain + c + 1])
                    last.then_inc(high_a, 1)

                def high_halves(src, p):
                    op(ah[:, 2 * p:2 * p + 2, :], src[:, 2 * p:2 * p + 2, :], ACT.Copy).then_inc(high_a, 1)

                for p in squares_of():
                    if L:
                        act.wait_ge(x_ple, (L - 1) * 4 + p + 1)
                root(L, "norm1")
                halves.make_high(act, nc, L, 0, 0)
                for p in range(4):
                    act.wait_ge(h_ready, L * 8 + 2 * p + 2)
                    high_halves(htmp, p)
                halves.make_high(act, nc, L, 0, 1)
                done(act, L, "iw")
                op(iwf[:, :], unit("iw")[0:4, 0, :], ACT.Copy, scale=0.5).then_inc(read("iw"), 1)
                act.wait_ge(misc_in, 16 * (L + 1))
                raw_item(L, 0)
                halves.make_high(act, nc, L, 0, 2)
                raw_item(L, 1)
                halves.make_high(act, nc, L, 0, 3)
                done(act, L, "iw_t")
                op(iw[:], unit("iw_t")[:, :, 0:4], ACT.Copy).then_inc(read("iw_t"), 1)
                if L == 0:
                    act.wait_ge(angles, 1)
                    op(sinb[:, :], angs[:, 0, :], ACT.Sin)
                    op(cosb[:, :], angs[:, 1, :], ACT.Sin).then_inc(rope_set, 1)
                root_item(L, 0)
                for i in range(2, len(QK_ITEMS)):
                    raw_item(L, i)
                    halves.make_high(act, nc, L, 0, i + SPLIT)
                    root_item(L, i - 1)
                    if i == 3:
                        act.wait_ge(idx_done, L + 1)
                        op(rel[:, 0:512], lg[0][:, :], ACT.Relu, scale=HD ** -0.5)
                        op(rel[:, 512:1024], lg[1][:, :], ACT.Relu, scale=HD ** -0.5)
                        op(rel[:, 1024:1280], tr[:, 0:T], ACT.Relu, scale=HD ** -0.5)
                        op(rel[:, 1280:1536], avo[:, 0:T], ACT.Relu, scale=HD ** -0.5).then_inc(rel_ready, 1)
                done(act, L, "bq0")
                op(bq[:, 0:2, :], unit("bq0")[:], ACT.Copy, scale=HD ** -0.5).then_inc(read("bq0"), 1)
                halves.make_high(act, nc, L, 0, 10 + SPLIT)
                root_item(L, len(QK_ITEMS) - 1)
                for n, (name, dst, s) in enumerate((("bq1", bq[:, 2:4, :], HD ** -0.5), ("bk0", bk[:, 0:2, :], 1.0),
                                     ("bk1", bk[:, 2:4, :], 1.0),
                                     ("cv0", cv[:, :, 0:W], 1.0), ("cv1", cv[:, :, W:2 * W], 1.0),
                                     ("av0", av[:, :, 0:W], 1.0), ("av1", av[:, :, W:2 * W], 1.0),
                                     ("bv0", bv[:, :, 0:W], 1.0), ("bv1", bv[:, :, W:2 * W], 1.0))):
                    done(act, L, name)
                    op(dst, unit(name)[:], ACT.Copy, scale=s).then_inc(read(name), 1)
                    halves.make_high(act, nc, L, 0, 11 + n + SPLIT)
                act.wait_ge(lam_in, L + 1)
                op(lam[:, 2:4], lam[:, 0:2], ACT.Exp).then_inc(lam_exp, 1)
                act.wait_ge(chosen_ready, L + 1)
                act.wait_ge(qk_out, (L + 1) * 10)
                for i in range(SPLIT):
                    halves.make_high(act, nc, L, 1, i)
                for n in range(BH + 1):
                    if n < BH:
                        b = n % 2
                        act.wait_ge(z_done, L * BH + n + 1)
                        if L * BH + n >= 2:
                            act.wait_ge(z_read, L * BH + n - 1)
                        linked(op(lnb[:, b, :], lg[0][:, 0:384], ACT.Abs))
                        linked(op(lnb[:, b, :], lnb[:, b, :], ACT.Exp, scale=-1.0))
                        op(lnb[:, b, :], lnb[:, b, :], ACT.Ln, bias=1.0).then_inc(ln_ready, 1)
                    if n >= 1:
                        act.wait_ge(e_ready, L * BH + n)
                        b = (n - 1) % 2
                        op(eb[:, b, :], eb[:, b, :], ACT.Exp).then_inc(a_ready, 1)
                    if n < BH:
                        done(act, L, f"gl{n}")
                        op(gates[:, 2 * n:2 * n + 2, :], unit(f"gl{n}")[:], ACT.Tanh, scale=0.5) \
                            .then_inc(read(f"gl{n}"), 1)
                        halves.make_high(act, nc, L, 1, n + SPLIT)
                    if n >= 2 and n % 2 == 0:
                        act.wait_ge(bo_done, L * BH + n)
                        op(yb[:, n // 2 - 1, :], avo[:, 0:T], ACT.Copy).then_inc(yb_ready, 1)
                for n in range(CH + 2):
                    if n < CH:
                        b = n % 2
                        act.wait_ge(c_max, L * CH + n + 1)
                        op(prob[:, b, 0:P], prob[:, b, 0:P], ACT.Exp, bias=stat[:, b, 0, 0:1],
                           accum_out=stat[:, b, 1, 0:1])
                        op(prob[:, b, P:384], prob[:, b, P:384], ACT.Exp, bias=stat[:, b, 0, 1:2],
                           accum_out=stat[:, b, 1, 1:2]).then_inc(c_exp, 1)
                        if n < 4:
                            done(act, L, f"gl{8 + n}")
                            op(gates[:, 16 + 2 * n:18 + 2 * n, :], unit(f"gl{8 + n}")[:], ACT.Tanh, scale=0.5) \
                                .then_inc(read(f"gl{8 + n}"), 1)
                            halves.make_high(act, nc, L, 1, 8 + n + SPLIT)
                    if 1 <= n <= CH:
                        m, b = n - 1, (n - 1) % 2
                        act.wait_ge(c_tr, L * CH + n)
                        if m >= 2:
                            act.wait_ge(c_av, L * CH + m - 1)
                        op(probT[:, b, :], tr[:, 0:384], ACT.Copy).then_inc(c_pt, 1)
                    if n >= 3 and n % 2 == 1:
                        act.wait_ge(c_av, L * CH + n - 1)
                        op(yc[:, (n - 3) // 2, :], avo[:, 0:T], ACT.Copy).then_inc(yc_ready, 1)
                act.wait_ge(c_av, (L + 1) * CH)
                for n in range(AH + 2):
                    if n < AH:
                        b = n % 2
                        act.wait_ge(a_max, L * AH + n + 1)
                        for c in range(2):
                            for t, (lo, hi) in enumerate(((0, P), (P, 384))):
                                p = aprob(c, b)[:, lo:hi]
                                last = op(p, p, ACT.Exp, bias=stat[:, b, 0, 2 * c + t:2 * c + t + 1],
                                          accum_out=stat[:, b, 1, 2 * c + t:2 * c + t + 1])
                        last.then_inc(a_exp, 1)
                    if 1 <= n <= AH:
                        m, b = n - 1, (n - 1) % 2
                        act.wait_ge(a_tr, L * AH + n)
                        op(probT[:, b, :], tr[:, 0:384], ACT.Copy).then_inc(a_pt, 1)
                        act.wait_ge(a_av, L * AH + n)
                        if m >= 2:
                            done(act, L, f"msa{m - 2}")
                        op(sqa[:, b, :], avo[:, 0:T], ACT.Square)
                        op(ya[:, m, :], avo[:, 0:T], ACT.Copy).then_inc(a_raw, 1)
                    if n >= 2:
                        m = n - 2
                        done(act, L, f"msa{m}")
                        if m >= 2:
                            act.wait_ge(ya_ready, L * AH + m - 1)
                        op(rsa[:, m % 2, :], unit(f"msa{m}")[:, 0, :], ACT.Sqrt, bias=con[:, E_EPS:E_EPS + 1]) \
                            .then_inc(read(f"msa{m}"), 1)
                act.wait_ge(ya_ready, (L + 1) * AH)
                for i in range(SPLIT):
                    halves.make_high(act, nc, L, 2, i)

                for p in range(4):
                    act.wait_ge(mrg_ready, L * 8 + 4 + p + 1)
                    high_halves(mrg, p)
                for p in squares_of():
                    if p:
                        halves.make_high(act, nc, L, 2, p - 1 + SPLIT)
                    if p == 3:
                        done(act, L, "wo3")
                        for q in range(3):
                            scaled_high(N_G2, q)
                    taken(act, L, f"wo{p}")
                scaled_high(N_G2, 3)
                halves.make_high(act, nc, L, 2, 3 + SPLIT)
                root(L, "norm2")

                def hidden_high(u):
                    act.wait_ge(relu_ready, L * (HID // W) + u + 1)
                    op(hidh[:, 2 * u:2 * u + 2, :], pairs(ft[:, u % 2, :]), ACT.Copy).then_inc(hidh_ready, 1)

                for u in range(HID // W):
                    halves.make_high(act, nc, L, 2, 4 + u + SPLIT)
                    if u:
                        hidden_high(u - 1)
                hidden_high(HID // W - 1)
                for p in squares_of():
                    if p:
                        scaled_high(N_G3, p - 1)
                    for i in range(4 if p < 3 else 3):
                        halves.make_high(act, nc, L, 2, 4 + HID // W + 4 * p + i + SPLIT)
                    taken(act, L, f"dn{p}")
                scaled_high(N_G3, 3)
                halves.make_high(act, nc, L, 2, 19 + HID // W + SPLIT)
                root(L, "norm3")
                for u in range(4):
                    halves.make_high(act, nc, L, 2, 20 + HID // W + u + SPLIT)
                    taken(act, L, f"pg{u}")
                    op(sg[:, 2 * u:2 * u + 2, :], pairs(part[:, u % 2, :]), ACT.Tanh, scale=0.5).then_inc(sg_ready, 1)

        @block.vector
        def _(dve):
            v = nc.vector
            links = [0]

            def linked(ins):
                links[0] += 1
                ins.then_inc(link["dve"], 1)
                dve.wait_ge(link["dve"], links[0])

            def norm(L, name, gain, h):
                taken(dve, L, name)
                linked(v.reciprocal(rstd[:, :], rstd[:, :]))
                for k in range(KD):
                    v.scalar_tensor_tensor(out=h[:, k, :], in0=x[:, k, :], scalar=misc[:, gain + k:gain + k + 1],
                                           in1=rstd[:, :], op0=ALU.mult, op1=ALU.mult).then_inc(h_ready, 1)

            def item(L, i):
                name = QK_ITEMS[i]
                w = T if name == "ik" else 2 * T
                a = w // T
                done(dve, L, f"rot_{name}")
                if i >= 2:
                    dve.wait_ge(qk_out, L * 10 + i - 1)
                v.tensor_tensor(qkw[:, 2, i % 2, 0:w].rearrange("p (a t) -> p a t", a=a),
                                unit(f"rot_{name}")[:, 0:a, :], sinb[:].unsqueeze(1).broadcast_to([P, a, T]),
                                ALU.mult).then_inc(read(f"rot_{name}"), 1)
                if name != "iq":
                    taken(dve, L, f"ms_{name}")
                    v.reciprocal(qkw[:, 0, i % 2, 0:w], qkw[:, 0, i % 2, 0:w]).then_inc(qk_rstd, 1)

            def index_score(L, j):
                lo, hi, base, w = ((0, P, 1024, P), (P, 384, 0, T))[j]
                s = score[:, lo:hi]
                for hd in range(4):
                    at = base + ((hd % 2) * 2 + hd // 2) * w
                    r = rel[:, at:at + w]
                    if hd == 0:
                        linked(v.tensor_scalar(s, r, iw[:, j, 0:1], 0.0, ALU.mult, ALU.add))
                    else:
                        linked(v.scalar_tensor_tensor(out=s, in0=r, scalar=iw[:, j, hd:hd + 1], in1=s,
                                                      op0=ALU.mult, op1=ALU.add))
                linked(v.tensor_tensor(s, s, con[:, E_CH + lo:E_CH + hi], ALU.add))

            def top_eight():
                for j, (lo, hi) in enumerate(((0, P), (P, 384))):
                    linked(v.max(mx8[:, j, :], score[:, lo:hi]))
                    linked(v.match_replace(score[:, lo:hi], mx8[:, j, :], score[:, lo:hi], GONE))

            def rotary_angles():
                dve.wait_ge(pos_in, 16)
                linked(v.tensor_copy(ang, posi[:, :]))
                linked(v.tensor_scalar(ang, ang, con[:, E_FREQ:E_FREQ + 1], None, ALU.mult))
                for j, quarter in ((0, 0.0), (1, 0.25)):
                    linked(v.tensor_scalar(turn[:, j, :], ang, 1 / (2 * math.pi), quarter, ALU.mult, ALU.add))
                    linked(v.tensor_scalar(turn[:, j, :], turn[:, j, :], MAGIC, None, ALU.add))
                    linked(v.tensor_scalar(turn[:, j, :], turn[:, j, :], -MAGIC, None, ALU.add))
                    linked(v.scalar_tensor_tensor(out=angs[:, j, :], in0=turn[:, j, :], scalar=-TWO_PI_1, in1=ang,
                                                  op0=ALU.mult, op1=ALU.add))
                    for c in (TWO_PI_2, TWO_PI_3):
                        linked(v.scalar_tensor_tensor(out=angs[:, j, :], in0=turn[:, j, :], scalar=-c,
                                                      in1=angs[:, j, :], op0=ALU.mult, op1=ALU.add))
                    if j:
                        linked(v.tensor_scalar(angs[:, j, :], angs[:, j, :], math.pi / 2, None, ALU.add))
                    ins = v.tensor_scalar(angs[:, j, :], angs[:, j, :], -3.1415925, 3.1415925, ALU.max, ALU.min)
                    if j:
                        ins.then_inc(angles, 1)

            dve.wait_ge(con_in, 16)
            for L in range(LAYERS):
                def scaled_low(gain, base):
                    for c in range(KD):
                        if c % 2 == 0:
                            dve.wait_ge(high_a, L * 16 + base + c // 2 + 1)
                        last = v.scalar_tensor_tensor(
                            out=al[:, c, :], in0=x[:, c, :], scalar=misc[:, gain + c:gain + c + 1],
                            in1=ah[:, c, :].bitcast(F32), op0=ALU.mult, op1=ALU.subtract)
                        if c % 2:
                            last.then_inc(low_a, 1)

                def over_rms(u, name):
                    done(dve, L, name)
                    v.tensor_tensor(pairs(part[:, u % 2, :]), unit(name)[:],
                                    rstd[:, :].unsqueeze(1).broadcast_to([P, 2, T]), ALU.mult) \
                        .then_inc(read(name), 1)

                def low_halves(src, base):
                    for p in range(4):
                        dve.wait_ge(high_a, L * 16 + base + p + 1)
                        c = slice(2 * p, 2 * p + 2)
                        v.tensor_tensor(al[:, c, :], src[:, c, :], ah[:, c, :].bitcast(F32), ALU.subtract) \
                            .then_inc(low_a, 1)

                dve.wait_ge(misc_in, 16 * (L + 1))
                norm(L, "norm1", N_G1, htmp)
                halves.make_low(dve, nc, L, 0, 0)
                low_halves(htmp, 0)
                halves.make_low(dve, nc, L, 0, 1)
                l4 = misc[:, N_LAM:N_LAM + 256].rearrange("p (a b d) -> p a b d", a=2, b=2)
                linked(v.tensor_tensor(lamp[:], l4[:, :, 0, :], l4[:, :, 1, :], ALU.mult))
                v.tensor_reduce(lam[:, 0:2], lamp[:], AX, ALU.add).then_inc(lam_in, 1)
                if L == 0:
                    rotary_angles()
                halves.make_low(dve, nc, L, 0, 2)
                halves.make_low(dve, nc, L, 0, 3)
                if L == 0:
                    dve.wait_ge(rope_set, 1)
                for i in range(4):
                    item(L, i)
                    halves.make_low(dve, nc, L, 0, 4 + i)
                dve.wait_ge(tables_in, 16)
                dve.wait_ge(rel_ready, L + 1)
                taken(dve, L, "iw_t")
                for i in range(4, len(QK_ITEMS)):
                    if i < 6:
                        index_score(L, i - 4)
                    item(L, i)
                    halves.make_low(dve, nc, L, 0, 4 + i)
                for i in range(14, 20):
                    top_eight()
                    halves.make_low(dve, nc, L, 0, i)
                for _ in range(TOP // 8 - 6):
                    top_eight()
                v.tensor_scalar(chosen[:, :], score[:, :], GONE / 2, NEG, ALU.is_gt, ALU.mult) \
                    .then_inc(chosen_ready, 1)
                dve.wait_ge(chosen_ready, L + 1)
                dve.wait_ge(lam_exp, L + 1)
                linked(v.tensor_tensor(lam[:, 4:5], lam[:, 3:4], lam[:, 2:3], ALU.subtract))
                linked(v.tensor_tensor(lam[:, 5:6], lam[:, 4:5], misc[:, N_LINIT:N_LINIT + 1], ALU.subtract))
                v.tensor_tensor(lam[:, 6:7], misc[:, N_SUB:N_SUB + 1], misc[:, N_LREST:N_LREST + 1], ALU.mult) \
                    .then_inc(lam_set, 1)
                dve.wait_ge(lam_set, L + 1)
                for i in range(SPLIT):
                    halves.make_low(dve, nc, L, 1, i)
                for n in range(BH + 1):
                    if n < BH:
                        b = n % 2
                        dve.wait_ge(ln_ready, L * BH + n + 1)
                        if n >= 2:
                            dve.wait_ge(zs_done, L * BH + n - 1)
                        v.scalar_tensor_tensor(out=spb[:, b, :], in0=lg[0][:, 0:384], scalar=0.0, in1=lnb[:, b, :],
                                               op0=ALU.max, op1=ALU.add).then_inc(z_read, 1)
                    if n >= 1:
                        m, b = n - 1, (n - 1) % 2
                        dve.wait_ge(zs_done, L * BH + n)
                        if m >= 2:
                            dve.wait_ge(bo_done, L * BH + m - 1)
                        v.tensor_tensor(eb[:, b, :], lg[1][:, 0:384], con[:, E_SNEG:E_SNEG + 384], ALU.add) \
                            .then_inc(e_ready, 1)
                    if n < BH:
                        halves.make_low(dve, nc, L, 1, n + SPLIT)
                for n in range(CH + 1):
                    if n < CH:
                        b = n % 2
                        dve.wait_ge(c_lg, L * CH + n + 1)
                        if n >= 2:
                            dve.wait_ge(c_tr, L * CH + n - 1)
                        v.tensor_tensor(prob[:, b, 0:384], lg[b][:, 0:384], chosen[:, :], ALU.add).then_inc(c_read, 1)
                        dve.wait_ge(c_read, L * CH + n + 1)
                        v.tensor_reduce(stat[:, b, 0, 0:1], prob[:, b, 0:P], AX, ALU.max, negate=True)
                        v.tensor_reduce(stat[:, b, 0, 1:2], prob[:, b, P:384], AX, ALU.max, negate=True) \
                            .then_inc(c_max, 1)
                    if n >= 1:
                        b = (n - 1) % 2
                        dve.wait_ge(c_exp, L * CH + n)
                        v.reciprocal(stat[:, b, 2, 0:2], stat[:, b, 1, 0:2]).then_inc(c_coef, 1)
                    if n < 4:
                        halves.make_low(dve, nc, L, 1, 8 + n + SPLIT)
                    if 4 <= n < CH:
                        u = n - 4
                        done(dve, L, f"bb{u}")
                        v.scalar_tensor_tensor(out=mrg[:, 2 * u:2 * u + 2, :], in0=gates[:, 8 + 2 * u:10 + 2 * u, :],
                                               scalar=1.0, in1=unit(f"bb{u}")[:], op0=ALU.add, op1=ALU.mult) \
                            .then_inc(read(f"bb{u}"), 1)

                def gated(L, name, gate, n):
                    done(dve, L, name)
                    if n >= 2:
                        dve.wait_ge(mrg_ready, L * 8 + n - 1)
                    v.scalar_tensor_tensor(out=pairs(part[:, n % 2, :]), in0=gates[:, gate:gate + 2, :], scalar=1.0,
                                           in1=unit(name)[:], op0=ALU.add, op1=ALU.mult).then_inc(read(name), 1)

                def head_norm(L, m):
                    taken(dve, L, f"msa{m}")
                    linked(v.reciprocal(rsa[:, m % 2, :], rsa[:, m % 2, :]))
                    v.scalar_tensor_tensor(out=ya[:, m, :], in0=ya[:, m, :], scalar=lam[:, 6:7], in1=rsa[:, m % 2, :],
                                           op0=ALU.mult, op1=ALU.mult).then_inc(ya_ready, 1)

                dve.wait_ge(c_tr, (L + 1) * CH)
                for n in range(AH + 2):
                    if n < AH:
                        b = n % 2
                        dve.wait_ge(a_lg, L * AH + n + 1)
                        if n >= 2:
                            dve.wait_ge(a_tr, L * AH + n - 1)
                        for c in range(2):
                            last = v.tensor_tensor(aprob(c, b), lg[c][:, 0:384], con[:, E_CH:E_CH + 384], ALU.add)
                        last.then_inc(a_read, 1)
                        dve.wait_ge(a_read, L * AH + n + 1)
                        for c in range(2):
                            for t, (lo, hi) in enumerate(((0, P), (P, 384))):
                                last = v.tensor_reduce(stat[:, b, 0, 2 * c + t:2 * c + t + 1], aprob(c, b)[:, lo:hi],
                                                       AX, ALU.max, negate=True)
                        last.then_inc(a_max, 1)
                        dve.wait_ge(a_exp, L * AH + n + 1)
                        linked(v.reciprocal(stat[:, b, 2, :], stat[:, b, 1, :]))
                        v.tensor_scalar(stat[:, b, 2, 2:4], stat[:, b, 2, 2:4], lam[:, 5:6], None, ALU.mult) \
                            .then_inc(a_coef, 1)
                        gated(L, f"bc{n}", 16 + 2 * n, n)
                    if n >= 2:
                        head_norm(L, n - 2)
                for u in range(4):
                    gated(L, f"ba{u}", 2 * u, 4 + u)
                    if u < SPLIT:
                        halves.make_low(dve, nc, L, 2, u)

                low_halves(mrg, 4)
                for u in range(4):
                    done(dve, L, f"wo{u}")
                    v.scalar_tensor_tensor(out=x[:, 2 * u:2 * u + 2, :], in0=unit(f"wo{u}")[:], scalar=0.5,
                                           in1=x[:, 2 * u:2 * u + 2, :], op0=ALU.mult, op1=ALU.add) \
                        .then_inc(read(f"wo{u}"), 1)
                    if u < 3:
                        halves.make_low(dve, nc, L, 2, u + SPLIT)
                scaled_low(N_G2, 8)
                halves.make_low(dve, nc, L, 2, 3 + SPLIT)
                taken(dve, L, "norm2")
                linked(v.reciprocal(rstd[:, :], rstd[:, :]))
                for u in range(HID // W):
                    over_rms(u, f"up{u}")
                    taken(dve, L, f"up{u}")
                    if u >= 2:
                        dve.wait_ge(hidl_ready, L * (HID // W) + u - 1)
                    v.scalar_tensor_tensor(out=ft[:, u % 2, :], in0=part[:, u % 2, :], scalar=0.0,
                                           in1=part[:, u % 2, :], op0=ALU.max, op1=ALU.mult).then_inc(relu_ready, 1)
                    halves.make_low(dve, nc, L, 2, 4 + u + SPLIT)
                for u in range(4):
                    for i in range(4 if u < 3 else 3):
                        halves.make_low(dve, nc, L, 2, 4 + HID // W + 4 * u + i + SPLIT)
                    done(dve, L, f"dn{u}")
                    v.tensor_tensor(x[:, 2 * u:2 * u + 2, :], unit(f"dn{u}")[:], x[:, 2 * u:2 * u + 2, :], ALU.add) \
                        .then_inc(read(f"dn{u}"), 1)
                scaled_low(N_G3, 12)
                halves.make_low(dve, nc, L, 2, 19 + HID // W + SPLIT)
                taken(dve, L, "norm3")
                linked(v.reciprocal(rstd[:, :], rstd[:, :]))
                for u in range(4):
                    if u >= 2:
                        dve.wait_ge(sg_ready, L * 4 + u - 1)
                    over_rms(u, f"pg{u}")
                    halves.make_low(dve, nc, L, 2, 20 + HID // W + u + SPLIT)
                dve.wait_ge(sg_ready, L * 4 + 4)
                for u in range(4):
                    done(dve, L, f"pp{u}")
                    v.scalar_tensor_tensor(out=pairs(part[:, u % 2, :]), in0=sg[:, 2 * u:2 * u + 2, :], scalar=1.0,
                                           in1=unit(f"pp{u}")[:], op0=ALU.add, op1=ALU.mult) \
                        .then_inc(read(f"pp{u}"), 1)
                    taken(dve, L, f"pp{u}")
                    v.scalar_tensor_tensor(out=x[:, 2 * u:2 * u + 2, :], in0=pairs(part[:, u % 2, :]), scalar=0.5,
                                           in1=x[:, 2 * u:2 * u + 2, :], op0=ALU.mult, op1=ALU.add).then_inc(x_ple, 1)

        @block.gpsimd
        def _(pool):
            g_ = nc.gpsimd
            links = [0]

            def linked(ins):
                links[0] += 1
                ins.then_inc(link["pool"], 1)
                pool.wait_ge(link["pool"], links[0])

            pool.wait_ge(tables_in, 16)
            pool.wait_ge(rope_set, 1)
            dest = {"ik": ik[:].unsqueeze(1), "iq": iq[:], "ck0": ck[:, 0:2, :], "ck1": ck[:, 2:4, :],
                    "cq0": cq[:, 0:2, :], "cq1": cq[:, 2:4, :], "ak0": ak[:, 0:2, :], "ak1": ak[:, 2:4, :],
                    "aq0": aq[:, 0:2, :], "aq1": aq[:, 2:4, :]}
            for L in range(LAYERS):
                for i, name in enumerate(QK_ITEMS):
                    a = 1 if name == "ik" else 2
                    view = [qkw[:, c, i % 2, 0:a * T].rearrange("p (a t) -> p a t", a=a) for c in range(3)]
                    taken(pool, L, f"rot_{name}")
                    linked(g_.tensor_tensor(view[1], view[1], cosb[:].unsqueeze(1).broadcast_to([P, a, T]), ALU.mult))
                    if name == "iq":
                        g_.tensor_tensor(dest[name], view[1], view[2], ALU.add).then_inc(qk_out, 1)
                    else:
                        linked(g_.tensor_tensor(view[1], view[1], view[2], ALU.add))
                        pool.wait_ge(qk_rstd, L * 9 + (1 if i == 0 else i))
                        g_.tensor_tensor(dest[name], view[1], view[0], ALU.mult).then_inc(qk_out, 1)
                for n in range(BH):
                    pool.wait_ge(z_read, L * BH + n + 1)
                    g_.tensor_tensor(spb[:, n % 2, :], spb[:, n % 2, :], con[:, E_S01:E_S01 + 384], ALU.mult) \
                        .then_inc(sp_ready, 1)
                for n in range(CH):
                    b = n % 2
                    pool.wait_ge(c_coef, L * CH + n + 1)
                    for j, (lo, hi) in enumerate(((0, P), (P, 384))):
                        last = g_.tensor_scalar(prob[:, b, lo:hi], prob[:, b, lo:hi], stat[:, b, 2, j:j + 1], None,
                                                ALU.mult)
                    last.then_inc(c_prob, 1)
                for n in range(AH):
                    b = n % 2
                    pool.wait_ge(a_coef, L * AH + n + 1)
                    for c in range(2):
                        for j, (lo, hi) in enumerate(((0, P), (P, 384))):
                            p = aprob(c, b)[:, lo:hi]
                            last = g_.tensor_scalar(p, p, stat[:, b, 2, 2 * c + j:2 * c + j + 1], None, ALU.mult)
                    linked(last)
                    g_.tensor_tensor(aprob(0, b), aprob(0, b), aprob(1, b), ALU.add).then_inc(a_prob, 1)
                    u = n
                    taken(pool, L, f"bc{u}")
                    g_.tensor_tensor(mrg[:, 2 * u:2 * u + 2, :], mrg[:, 2 * u:2 * u + 2, :],
                                     pairs(part[:, u % 2, :]), ALU.add).then_inc(mrg_ready, 1)
                for u in range(4):
                    taken(pool, L, f"ba{u}")
                    g_.tensor_tensor(mrg[:, 2 * u:2 * u + 2, :], mrg[:, 2 * u:2 * u + 2, :],
                                     pairs(part[:, u % 2, :]), ALU.add).then_inc(mrg_ready, 1)
                for u in range(HID // W):
                    pool.wait_ge(hidh_ready, L * (HID // W) + u + 1)
                    c = slice(2 * u, 2 * u + 2)
                    g_.tensor_tensor(hidl[:, c, :], pairs(ft[:, u % 2, :]), hidh[:, c, :].bitcast(F32), ALU.subtract) \
                        .then_inc(hidl_ready, 1)


def second_weights(i, w_in, w_br_a, w_br_b, w_br_c, w_out, w_up, w_down, w_gate, w_proj):
    w = w_in[i]
    ik = np.zeros((D, W), np.float32)
    ik[:, 0:64] = ik[:, 64:128] = w[:, 4864:4928]
    out = weight_tiles(ik) + weight_tiles(w[:, 4608:4864])
    for at in (3584, 3072, 512, 0, 1536, 2048):
        out += weight_tiles(w[:, at:at + 512])
    for at in (4096, 1024, 2560):
        out += weight_tiles(w[:, at:at + 512])
    out += weight_tiles(w[:, 4932:8004])
    for b in (w_br_b, w_br_c, w_br_a):
        for c in range(2):
            out.append(chunked(b[i][:, c * 512:(c + 1) * 512]).reshape(P, TILE))
    out += weight_tiles(w_out[i]) + weight_tiles(w_up[i])
    out += weight_tiles(w_down[i]) + weight_tiles(w_gate[i])
    out.append(chunked(w_proj[i]).reshape(P, TILE))
    return np.stack(out)


def second_misc(i, w_in, gains, subln, a_lambda, g1, g2, g3):
    m = np.zeros((P, M2), np.float32)
    m[:, N_IW:N_IW + 32] = chunked(w_in[i][:, 4928:4932]).reshape(P, 32)
    for j, g in enumerate(gains):
        m[:, N_GAIN + j] = np.concatenate([g[i], g[i]])
    m[:, N_SUB] = subln[i]
    m[:, N_LAM:N_LAM + 256] = a_lambda[i].reshape(1, 256)
    for at, g in ((N_G1, g1), (N_G2, g2), (N_G3, g3)):
        m[:, at:at + KD] = g[i].reshape(KD, P).T
    init = 0.8 - 0.6 * math.exp(-0.3 * i)
    m[:, N_LINIT], m[:, N_LREST] = init, 1 - init
    return m


def second_constants():
    c = np.zeros((P, C2), np.float32)
    i = np.arange(P)
    c[:, E_ID:E_ID + P] = np.eye(P)
    c[:, E_ONE:E_ONE + P] = 1 / D
    same = (i[:, None] // 64 == i[None] // 64)
    c[:, E_G1:E_G1 + P], c[:, E_G64:E_G64 + P] = same / 64, same
    c[:, E_HEAD:E_HEAD + P] = 1 / P
    for m in range(P):
        if m % 64 < 32:
            c[m + 32, E_ROT + m] = -1
        else:
            c[m - 32, E_ROT + m] = 1
    c[:, E_TRI:E_TRI + P] = -(i[:, None] >= i[None]).astype(np.float32)
    c[:, E_NEG:E_NEG + P] = -1
    q, k = i[:, None], np.arange(T)[None]
    c[:, E_CH:E_CH + P] = np.where(k[:, :P] // 64 <= q // 64, 0, NEG)
    c[:, E_CH + P:E_CH + 384] = np.where(k // 64 <= (q + P) // 64, 0, NEG)
    kk, qq = i[:, None], np.arange(T)[None]
    strict = np.concatenate([kk < qq, (kk + P < qq)[:, P:]], 1)
    c[:, E_S01:E_S01 + 384] = strict
    c[:, E_SNEG:E_SNEG + 384] = np.where(strict, 0, NEG)
    inv = np.float32(10000.0) ** (-np.arange(0, 64, 2, dtype=np.float32) / 64)
    c[:, E_FREQ] = inv[i % 32]
    c[:, E_EPS], c[:, E_EPS64] = 1e-6, 64e-6
    return c


def program(nc, x, w1, m1, c1, onehot, onehot_rev, flip, rel, w2, m2, c2, pos, pt, out):
    with ExitStack() as outer:
        ring = outer.enter_context(nc.sbuf_tensor("ring", [P, RING, KD, W], F32))
        x_sb = outer.enter_context(nc.sbuf_tensor("x", [P, KD, T], F32))
        first_block(nc, outer, ring, x_sb, x, w1, m1, c1, onehot, onehot_rev, flip, rel)
        second_block(nc, outer, ring, x_sb, w2, m2, c2, pos, pt, out)


def kernel(**inputs):
    import concourse.bacc as bacc
    from concourse.bass_utils import run_bass_kernel_spmd

    a = {name: np.asarray(value) for name, value in inputs.items()}
    layers = range(LAYERS)
    first = [a[n] for n in ("w_in", "cmp_w1_k", "cmp_w1_v", "w_o_ret", "w_o_nsa", "w_out", "w_ffn_in", "w_ffn_out")]
    second = [a[n + "_2"] for n in ("w_in", "w_br_a", "w_br_b", "w_br_c", "w_out", "w_up", "w_down", "w_ple_gate",
                                    "w_ple_proj")]
    gains = [a[n + "_2"] for n in ("idx_k_norm", "c_k_norm", "c_q_norm", "a_k_norm", "a_q_norm")]
    arrays = {
        "x_t": chunked(np.ascontiguousarray(a["x"][0].T)),
        "w1": np.stack([first_weights(i, *first) for i in layers]),
        "m1": np.stack([first_misc(i, a["w_in"], a["cmp_pos_k"], a["cmp_pos_v"], a["cmp_w2_k"], a["cmp_w2_v"],
                                   a["norm_mix_g"], a["norm_ffn_g"]) for i in layers]),
        "c1": first_constants(a["norm_final_g"]),
        "onehot": distance_rows(np.arange(-255, 256)),
        "onehot_rev": distance_rows(255 - np.arange(384)),
        "flip": np.eye(P, dtype=np.float32)[::-1],
        "rel": a["rel_bias"],
        "w2": np.stack([second_weights(i, *second) for i in layers]),
        "m2": np.stack([second_misc(i, a["w_in_2"], gains, a["a_subln_2"], a["a_lambda_2"], a["attn_norm_2"],
                                    a["mlp_norm_2"], a["ple_norm_2"]) for i in layers]),
        "c2": second_constants(),
        "pos": np.broadcast_to(a["positions_2"].astype(np.int32), (P, T)),
        "p_t": np.stack([chunked(np.ascontiguousarray(a["p_2"][i, 0].T)) for i in layers]),
    }
    arrays = {f"in_{n}": np.ascontiguousarray(v) for n, v in arrays.items()}
    nc = bacc.Bacc("TRN2", target_bir_lowering=False, num_devices=1)
    args = [nc.dram_tensor(n, v.shape, I32 if v.dtype.kind == "i" else F32, kind="ExternalInput").ap()
            for n, v in arrays.items()]
    out = nc.dram_tensor("out_t", (P, KD, T), F32, kind="ExternalOutput").ap()
    program(nc, *args, out)
    r = run_bass_kernel_spmd(nc, [arrays], core_ids=[0])
    got = np.asarray(r.results[0]["out_t"])
    return np.ascontiguousarray(got.transpose(2, 1, 0)).reshape(1, T, D)
```
